# Optimizing a Trainium2 kernel written in Bass

```python
import math
import jax
import jax.numpy as jnp
from jax import lax
import numpy as np
import jax, jax.numpy as jnp

D_MODEL = 1024
BATCH = 1
SEQ = 256
DEPTH = 1

N_MIXERS = 4
NORM_EPS = 1e-6
NEG_INF = -1e30
F32 = jnp.float32

MOBA_HEADS = 16
MOBA_HEAD_DIM = D_MODEL // MOBA_HEADS
MOBA_BLOCK = 256
MOBA_TOPK = 3
MOBA_Q_CHUNK = 16

RWKV_HEAD_DIM = 64
RWKV_HEADS = D_MODEL // RWKV_HEAD_DIM
RWKV_DECAY_LORA = 64
RWKV_AAA_LORA = 64
RWKV_GATE_LORA = 160
RWKV_GN_EPS = 64e-5
RWKV_N_MIX = 6

SSD_D_INNER = 2 * D_MODEL
SSD_HEAD_DIM = 64
SSD_HEADS = SSD_D_INNER // SSD_HEAD_DIM
SSD_GROUPS = 4
SSD_STATE = 128
SSD_CONV = 4
SSD_CHUNK = 128
SSD_CONV_DIM = SSD_D_INNER + 2 * SSD_GROUPS * SSD_STATE
SSD_IN_DIM = SSD_D_INNER + SSD_CONV_DIM + SSD_HEADS
SSD_NORM_EPS = 1e-5

CONF_KERNEL = 31
CONF_LN_EPS = 1e-5

D_FF = 2816
FFN_CONV = 3


def _rmsnorm(x, g):
    x32 = x.astype(F32)
    y = x32 * lax.rsqrt(jnp.mean(x32 * x32, axis=-1, keepdims=True) + NORM_EPS)
    return (y * g.astype(F32)).astype(x.dtype)

def _layernorm(x, w, b, eps):
    x32 = x.astype(F32)
    mu = jnp.mean(x32, axis=-1, keepdims=True)
    var = jnp.mean(jnp.square(x32 - mu), axis=-1, keepdims=True)
    return ((x32 - mu) * lax.rsqrt(var + eps) * w.astype(F32) + b.astype(F32)).astype(x.dtype)

def _causal_dwconv(x, w, b):
    k, c = w.shape
    y = lax.conv_general_dilated(x, w[:, None, :], window_strides=(1,), padding=[(k - 1, 0)],
                                 dimension_numbers=('NWC', 'WIO', 'NWC'), feature_group_count=c)
    return y + b

def _moba(x, w_qkv, w_o):
    b, s, d = x.shape
    h, dh, bs, qc = MOBA_HEADS, MOBA_HEAD_DIM, MOBA_BLOCK, MOBA_Q_CHUNK
    qkv = jnp.einsum('bsd,de->bse', x, w_qkv).reshape(b, s, 3, h, dh)
    q = jnp.transpose(qkv[:, :, 0], (0, 2, 1, 3)) * dh ** -0.5
    k = jnp.transpose(qkv[:, :, 1], (0, 2, 1, 3))
    v = jnp.transpose(qkv[:, :, 2], (0, 2, 1, 3))
    n_blk = -(-s // bs)
    pad = n_blk * bs - s
    kb = jnp.pad(k, ((0, 0), (0, 0), (0, pad), (0, 0))).reshape(b, h, n_blk, bs, dh)
    vb = jnp.pad(v, ((0, 0), (0, 0), (0, pad), (0, 0))).reshape(b, h, n_blk, bs, dh)
    k_mean = jnp.mean(kb, axis=3)
    q_blk = jnp.arange(s) // bs
    gate = jnp.einsum('bhsd,bhnd->bhsn', q, k_mean).astype(F32)
    fully_past = jnp.arange(n_blk)[None, :] < q_blk[:, None]
    gate = jnp.where(fully_past, gate, NEG_INF)
    n_sel = min(MOBA_TOPK, n_blk)
    _, sel = lax.top_k(gate, n_sel)
    sel_valid = sel < q_blk[:, None]
    bi = jnp.arange(b)[:, None, None, None]
    hi = jnp.arange(h)[None, :, None, None]

    def chunk(c):
        start = c * qc
        q_c = lax.dynamic_slice_in_dim(q, start, qc, axis=2)
        sel_c = lax.dynamic_slice_in_dim(sel, start, qc, axis=2)
        val_c = lax.dynamic_slice_in_dim(sel_valid, start, qc, axis=2)
        k_sel = kb[bi, hi, sel_c]
        v_sel = vb[bi, hi, sel_c]
        own = start // bs
        k_own = lax.dynamic_index_in_dim(kb, own, axis=2, keepdims=False)
        v_own = lax.dynamic_index_in_dim(vb, own, axis=2, keepdims=False)
        s_sel = jnp.einsum('bhqd,bhqnkd->bhqnk', q_c, k_sel).astype(F32)
        s_sel = jnp.where(val_c[..., None], s_sel, NEG_INF).reshape(b, h, qc, n_sel * bs)
        s_own = jnp.einsum('bhqd,bhkd->bhqk', q_c, k_own).astype(F32)
        q_pos = start + jnp.arange(qc)
        k_pos = own * bs + jnp.arange(bs)
        s_own = jnp.where(k_pos[None, :] <= q_pos[:, None], s_own, NEG_INF)
        p = jax.nn.softmax(jnp.concatenate([s_sel, s_own], axis=-1), axis=-1).astype(v.dtype)
        p_sel = p[..., :n_sel * bs].reshape(b, h, qc, n_sel, bs)
        p_own = p[..., n_sel * bs:]
        return (jnp.einsum('bhqnk,bhqnkd->bhqd', p_sel, v_sel)
                + jnp.einsum('bhqk,bhkd->bhqd', p_own, v_own))

    o = lax.map(chunk, jnp.arange(s // qc))
    o = jnp.transpose(o, (1, 0, 3, 2, 4)).reshape(b, s, d)
    return o @ w_o

def _rwkv7(x, mu, w_rkv, w0, w1, w2, a0, a1, a2, g1, g2, k_k, k_a, r_k, gn_w, gn_b, w_o):
    b, s, d = x.shape
    h, n = RWKV_HEADS, RWKV_HEAD_DIM
    xx = jnp.pad(x, ((0, 0), (1, 0), (0, 0)))[:, :-1] - x
    xm = x[:, :, None, :] + xx[:, :, None, :] * mu
    rkv = jnp.einsum('bsid,ide->bsie', xm[:, :, :3], w_rkv)
    r, k, v = rkv[:, :, 0], rkv[:, :, 1], rkv[:, :, 2]
    xw, xa, xg = xm[:, :, 3], xm[:, :, 4], xm[:, :, 5]
    w = -jax.nn.softplus(-(w0 + jnp.tanh(xw @ w1) @ w2).astype(F32)) - 0.5
    decay = jnp.exp(-jnp.exp(w))
    a = jax.nn.sigmoid(a0 + (xa @ a1) @ a2)
    g = jax.nn.sigmoid(xg @ g1) @ g2
    kk = (k * k_k).reshape(b, s, h, n).astype(F32)
    kk = kk / jnp.maximum(jnp.sqrt(jnp.sum(kk * kk, axis=-1, keepdims=True)), 1e-12)
    k = k * (1.0 + (a - 1.0) * k_a)
    r, k, v, a = (t.reshape(b, s, h, n) for t in (r, k, v, a))

    def to_time(t):
        return jnp.swapaxes(t.astype(F32), 0, 1)

    xs = (to_time(r), to_time(decay.reshape(b, s, h, n)), to_time(k), to_time(v),
          to_time(-kk), to_time(kk * a))

    def step(state, inp):
        r_t, w_t, k_t, v_t, a_t, b_t = inp
        sa = jnp.einsum('bhij,bhj->bhi', state, a_t)
        state = (state * w_t[:, :, None, :] + sa[..., None] * b_t[:, :, None, :]
                 + v_t[..., None] * k_t[:, :, None, :])
        return state, jnp.einsum('bhij,bhj->bhi', state, r_t)

    _, y = lax.scan(step, jnp.zeros((b, h, n, n), F32), xs)
    y = jnp.swapaxes(y, 0, 1)
    mu_y = jnp.mean(y, axis=-1, keepdims=True)
    var_y = jnp.mean(jnp.square(y - mu_y), axis=-1, keepdims=True)
    yn = ((y - mu_y) * lax.rsqrt(var_y + RWKV_GN_EPS)).reshape(b, s, d)
    yn = yn * gn_w.astype(F32) + gn_b.astype(F32)
    bonus = (jnp.sum(r * k * r_k, axis=-1, keepdims=True) * v).reshape(b, s, d).astype(F32)
    return ((yn + bonus).astype(x.dtype) * g) @ w_o

def _segsum(a):
    t = a.shape[-1]
    rep = jnp.broadcast_to(a[..., :, None], a.shape + (t,))
    rep = jnp.where(jnp.tril(jnp.ones((t, t), bool), -1), rep, 0.0)
    cs = jnp.cumsum(rep, axis=-2)
    return jnp.where(jnp.tril(jnp.ones((t, t), bool)), cs, -jnp.inf)

def _ssd_chunked(xd, adt, bm, cm):
    b, s, h, p = xd.shape
    g, n = bm.shape[2], bm.shape[3]
    e = h // g
    lc = SSD_CHUNK
    c = s // lc
    xc = xd.reshape(b, c, lc, g, e, p)
    bc = bm.reshape(b, c, lc, g, n)
    cc = cm.reshape(b, c, lc, g, n)
    ac = jnp.transpose(adt.reshape(b, c, lc, g, e), (0, 3, 4, 1, 2))
    a_cs = jnp.cumsum(ac, axis=-1)
    lmat = jnp.exp(_segsum(ac))
    cb = jnp.einsum('bclgn,bcsgn->bgcls', cc, bc)
    y_diag = jnp.einsum('bgecls,bcsgep->bclgep', cb[:, :, None] * lmat, xc)
    decay_states = jnp.exp(a_cs[..., -1:] - a_cs)
    states = jnp.einsum('bclgn,bgecl,bclgep->bcgepn', bc, decay_states, xc)
    states = jnp.concatenate([jnp.zeros_like(states[:, :1]), states], axis=1)
    chunk_a = jnp.pad(a_cs[..., -1], ((0, 0), (0, 0), (0, 0), (1, 0)))
    decay_chunk = jnp.exp(_segsum(chunk_a))
    states = jnp.einsum('bgezc,bcgepn->bzgepn', decay_chunk, states)[:, :-1]
    y_off = jnp.einsum('bclgn,bcgepn,bgecl->bclgep', cc, states, jnp.exp(a_cs))
    return (y_diag + y_off).reshape(b, s, h, p)

def _mamba2(x, w_in, conv_w, conv_b, dt_bias, a_log, d_skip, norm_w, w_out):
    b, s, _ = x.shape
    di, h, p, g, n = SSD_D_INNER, SSD_HEADS, SSD_HEAD_DIM, SSD_GROUPS, SSD_STATE
    zxbcdt = x @ w_in
    z, xbc, dt = jnp.split(zxbcdt, [di, di + SSD_CONV_DIM], axis=-1)
    xbc = jax.nn.silu(_causal_dwconv(xbc, conv_w, conv_b))
    xs, bm, cm = jnp.split(xbc, [di, di + g * n], axis=-1)
    dt = jax.nn.softplus((dt + dt_bias).astype(F32))
    a = -jnp.exp(a_log.astype(F32))
    xh = xs.reshape(b, s, h, p).astype(F32)
    y = _ssd_chunked(xh * dt[..., None], dt * a,
                     bm.reshape(b, s, g, n).astype(F32), cm.reshape(b, s, g, n).astype(F32))
    y = (y + xh * d_skip.astype(F32)[:, None]).reshape(b, s, di)
    yz = (y * jax.nn.silu(z.astype(F32))).reshape(b, s, g, di // g)
    yz = yz * lax.rsqrt(jnp.mean(yz * yz, axis=-1, keepdims=True) + SSD_NORM_EPS)
    yz = yz.reshape(b, s, di) * norm_w.astype(F32)
    return yz.astype(x.dtype) @ w_out

def _conformer_conv(x, w_pw1, b_pw1, dw_w, dw_b, ln_w, ln_b, w_pw2, b_pw2):
    u = jax.nn.glu(x @ w_pw1 + b_pw1, axis=-1)
    u = _causal_dwconv(u, dw_w, dw_b)
    u = jax.nn.silu(_layernorm(u, ln_w, ln_b, CONF_LN_EPS))
    return u @ w_pw2 + b_pw2

def _conv_ffn(x, w_up, conv_w, conv_b, w_down):
    u = _causal_dwconv(x @ w_up, conv_w, conv_b)
    gate, up = jnp.split(u, 2, axis=-1)
    return (jax.nn.silu(gate) * up) @ w_down

def _count(kind):
    return len(range(kind, DEPTH, N_MIXERS))

def first_inputs(seed: int = 0) -> dict:
    key = jax.random.key(seed)
    ks = iter(jax.random.split(key, 64))

    def nrm(shape, scale):
        return jax.random.normal(next(ks), shape, F32) * scale

    def uni(shape, lo, hi):
        return jax.random.uniform(next(ks), shape, F32, lo, hi)

    d = D_MODEL
    n_a, n_b, n_c, n_d = (_count(m) for m in range(N_MIXERS))
    dt0 = jnp.exp(uni((n_c, SSD_HEADS), math.log(1e-3), math.log(1e-1)))
    return {
        'x': nrm((BATCH, SEQ, d), 1.0),
        'norm_mix': 1.0 + nrm((DEPTH, d), 0.02),
        'norm_ffn': 1.0 + nrm((DEPTH, d), 0.02),
        'norm_final': 1.0 + nrm((d,), 0.02),
        'ffn_w_up': nrm((DEPTH, d, 2 * D_FF), d ** -0.5),
        'ffn_conv_w': nrm((DEPTH, FFN_CONV, 2 * D_FF), FFN_CONV ** -0.5),
        'ffn_conv_b': nrm((DEPTH, 2 * D_FF), 0.01),
        'ffn_w_down': nrm((DEPTH, D_FF, d), D_FF ** -0.5),
        'moba_w_qkv': nrm((n_a, d, 3 * d), d ** -0.5),
        'moba_w_o': nrm((n_a, d, d), d ** -0.5),
        'rwkv_mu': uni((n_b, RWKV_N_MIX, d), 0.0, 1.0),
        'rwkv_w_rkv': nrm((n_b, 3, d, d), d ** -0.5),
        'rwkv_w0': uni((n_b, d), -6.0, 1.0),
        'rwkv_w1': nrm((n_b, d, RWKV_DECAY_LORA), d ** -0.5),
        'rwkv_w2': nrm((n_b, RWKV_DECAY_LORA, d), 0.1 * RWKV_DECAY_LORA ** -0.5),
        'rwkv_a0': nrm((n_b, d), 0.1),
        'rwkv_a1': nrm((n_b, d, RWKV_AAA_LORA), d ** -0.5),
        'rwkv_a2': nrm((n_b, RWKV_AAA_LORA, d), 0.1 * RWKV_AAA_LORA ** -0.5),
        'rwkv_g1': nrm((n_b, d, RWKV_GATE_LORA), d ** -0.5),
        'rwkv_g2': nrm((n_b, RWKV_GATE_LORA, d), RWKV_GATE_LORA ** -0.5),
        'rwkv_k_k': 0.85 + nrm((n_b, d), 0.02),
        'rwkv_k_a': 1.0 + nrm((n_b, d), 0.02),
        'rwkv_r_k': nrm((n_b, RWKV_HEADS, RWKV_HEAD_DIM), 0.1),
        'rwkv_gn_w': 1.0 + nrm((n_b, d), 0.02),
        'rwkv_gn_b': nrm((n_b, d), 0.01),
        'rwkv_w_o': nrm((n_b, d, d), d ** -0.5),
        'ssd_w_in': nrm((n_c, d, SSD_IN_DIM), d ** -0.5),
        'ssd_conv_w': nrm((n_c, SSD_CONV, SSD_CONV_DIM), SSD_CONV ** -0.5),
        'ssd_conv_b': nrm((n_c, SSD_CONV_DIM), 0.01),
        'ssd_dt_bias': dt0 + jnp.log(-jnp.expm1(-dt0)),
        'ssd_a_log': jnp.log(uni((n_c, SSD_HEADS), 1.0, 16.0)),
        'ssd_d': 1.0 + nrm((n_c, SSD_HEADS), 0.1),
        'ssd_norm_w': 1.0 + nrm((n_c, SSD_D_INNER), 0.02),
        'ssd_w_out': nrm((n_c, SSD_D_INNER, d), SSD_D_INNER ** -0.5),
        'conf_w_pw1': nrm((n_d, d, 2 * d), d ** -0.5),
        'conf_b_pw1': nrm((n_d, 2 * d), 0.01),
        'conf_dw_w': nrm((n_d, CONF_KERNEL, d), CONF_KERNEL ** -0.5),
        'conf_dw_b': nrm((n_d, d), 0.01),
        'conf_ln_w': 1.0 + nrm((n_d, d), 0.02),
        'conf_ln_b': nrm((n_d, d), 0.01),
        'conf_w_pw2': nrm((n_d, d, d), d ** -0.5),
        'conf_b_pw2': nrm((n_d, d), 0.01),
    }

def first_block(x, norm_mix, norm_ffn, norm_final, ffn_w_up, ffn_conv_w, ffn_conv_b, ffn_w_down,
              moba_w_qkv, moba_w_o,
              rwkv_mu, rwkv_w_rkv, rwkv_w0, rwkv_w1, rwkv_w2, rwkv_a0, rwkv_a1, rwkv_a2,
              rwkv_g1, rwkv_g2, rwkv_k_k, rwkv_k_a, rwkv_r_k, rwkv_gn_w, rwkv_gn_b, rwkv_w_o,
              ssd_w_in, ssd_conv_w, ssd_conv_b, ssd_dt_bias, ssd_a_log, ssd_d, ssd_norm_w, ssd_w_out,
              conf_w_pw1, conf_b_pw1, conf_dw_w, conf_dw_b, conf_ln_w, conf_ln_b, conf_w_pw2, conf_b_pw2):
    for i in range(DEPTH):
        kind, j = i % N_MIXERS, i // N_MIXERS
        hn = _rmsnorm(x, norm_mix[i])
        if kind == 0:
            mix = _moba(hn, moba_w_qkv[j], moba_w_o[j])
        elif kind == 1:
            mix = _rwkv7(hn, rwkv_mu[j], rwkv_w_rkv[j], rwkv_w0[j], rwkv_w1[j], rwkv_w2[j],
                         rwkv_a0[j], rwkv_a1[j], rwkv_a2[j], rwkv_g1[j], rwkv_g2[j],
                         rwkv_k_k[j], rwkv_k_a[j], rwkv_r_k[j], rwkv_gn_w[j], rwkv_gn_b[j], rwkv_w_o[j])
        elif kind == 2:
            mix = _mamba2(hn, ssd_w_in[j], ssd_conv_w[j], ssd_conv_b[j], ssd_dt_bias[j],
                          ssd_a_log[j], ssd_d[j], ssd_norm_w[j], ssd_w_out[j])
        else:
            mix = _conformer_conv(hn, conf_w_pw1[j], conf_b_pw1[j], conf_dw_w[j], conf_dw_b[j],
                                  conf_ln_w[j], conf_ln_b[j], conf_w_pw2[j], conf_b_pw2[j])
        x = x + mix
        x = x + _conv_ffn(_rmsnorm(x, norm_ffn[i]), ffn_w_up[i], ffn_conv_w[i], ffn_conv_b[i], ffn_w_down[i])
    return _rmsnorm(x, norm_final)


N_META = 16
DN_HEADS = 4
DN_HEAD_DIM = 128
DN_WIDTH = DN_HEADS * DN_HEAD_DIM
DN_CONV = 4
DN_CHUNK = 64
SB_HEADS = 8
SB_HEAD_DIM = 64
SB_WIDTH = SB_HEADS * SB_HEAD_DIM
SB_BLOCK = 128
N_BRANCH = 2
IN_COLS = 4 * DN_WIDTH + 2 * DN_HEADS + 3 * SB_WIDTH + N_BRANCH * D_MODEL
SPLIT_POINTS = [3 * DN_WIDTH, 4 * DN_WIDTH, 4 * DN_WIDTH + DN_HEADS, 4 * DN_WIDTH + 2 * DN_HEADS,
                4 * DN_WIDTH + 2 * DN_HEADS + 3 * SB_WIDTH]
COL_DN_V0 = 2 * DN_WIDTH
COL_SB_V0 = 4 * DN_WIDTH + 2 * DN_HEADS + 2 * SB_WIDTH
N_GROUPS = 4
EXPERTS_PER_GROUP = 8
TOP_K_IN_GROUP = 2
EXPERT_FF = 256
DEEPNORM_ALPHA = (2.0 * DEPTH) ** 0.25
DEEPNORM_BETA = (8.0 * DEPTH) ** -0.25
LN_EPS = 1e-5
RMS_EPS = 1e-6


def layer_norm(x, g, b):
    xf = x.astype(jnp.float32)
    mu = jnp.mean(xf, -1, keepdims=True)
    var = jnp.mean(jnp.square(xf - mu), -1, keepdims=True)
    return ((xf - mu) * lax.rsqrt(var + LN_EPS) * g.astype(jnp.float32) + b.astype(jnp.float32)).astype(x.dtype)

def rms_norm(x, g):
    xf = x.astype(jnp.float32)
    return xf * lax.rsqrt(jnp.mean(xf * xf, -1, keepdims=True) + RMS_EPS) * g.astype(jnp.float32)

def l2_normalize(x):
    xf = x.astype(jnp.float32)
    return xf * lax.rsqrt(jnp.sum(xf * xf, -1, keepdims=True) + RMS_EPS)

def split_heads(t, n):
    b, l, _ = t.shape
    return t.reshape(b, l, n, -1).transpose(0, 2, 1, 3)

def merge_heads(t):
    b, h, l, d = t.shape
    return t.transpose(0, 2, 1, 3).reshape(b, l, h * d)

def causal_depthwise_conv(x, w):
    c = x.shape[-1]
    return lax.conv_general_dilated(x, w[:, None, :], window_strides=(1,), padding=[(w.shape[0] - 1, 0)],
                                    dimension_numbers=("NWC", "WIO", "NWC"), feature_group_count=c)

def gated_delta_rule_chunked(q, k, v, beta, g):
    b, h, l, dk = q.shape
    dv = v.shape[-1]
    c = DN_CHUNK
    n = l // c
    q = q.reshape(b, h, n, c, dk)
    k = k.reshape(b, h, n, c, dk)
    v = v.reshape(b, h, n, c, dv)
    beta = beta.reshape(b, h, n, c)
    decay = jnp.cumsum(g.reshape(b, h, n, c), axis=-1)
    idx = jnp.arange(c)
    causal = idx[:, None] >= idx[None, :]
    strict = idx[:, None] > idx[None, :]
    diff = decay[..., :, None] - decay[..., None, :]
    lmask = jnp.where(causal, jnp.exp(jnp.where(causal, diff, 0.0)), 0.0)
    k_beta = k * beta[..., None]
    v_beta = v * beta[..., None]
    a = jnp.where(strict, jnp.einsum("bhnid,bhnjd->bhnij", k_beta, k) * lmask, 0.0)
    m = a + jnp.eye(c, dtype=a.dtype)
    u = lax.linalg.triangular_solve(m, v_beta, left_side=True, lower=True, unit_diagonal=True)
    w = lax.linalg.triangular_solve(m, k_beta * jnp.exp(decay)[..., None], left_side=True, lower=True,
                                    unit_diagonal=True)
    qk = jnp.where(causal, jnp.einsum("bhnid,bhnjd->bhnij", q, k) * lmask, 0.0)
    q_dec = q * jnp.exp(decay)[..., None]
    k_dec = k * jnp.exp(decay[..., -1:] - decay)[..., None]
    chunk_decay = jnp.exp(decay[..., -1])
    xs = tuple(jnp.moveaxis(t, 2, 0) for t in (q_dec, k_dec, u, w, qk, chunk_decay))

    def step(state, inp):
        qd, kd, uc, wc, qkc, cd = inp
        v_new = uc - jnp.einsum("bhcd,bhde->bhce", wc, state)
        o = jnp.einsum("bhcd,bhde->bhce", qd, state) + jnp.einsum("bhij,bhje->bhie", qkc, v_new)
        state = state * cd[..., None, None] + jnp.einsum("bhcd,bhce->bhde", kd, v_new)
        return state, o

    s0 = jnp.zeros((b, h, dk, dv), jnp.float32)
    _, o = lax.scan(step, s0, xs)
    return jnp.moveaxis(o, 0, 2).reshape(b, h, l, dv)

def stick_breaking_attention(q, k, v):
    l = q.shape[2]
    scale = q.shape[-1] ** -0.5
    bounds = [0] + list(range(N_META, l, SB_BLOCK)) + [l]
    outs = []
    for s0, s1 in zip(bounds[:-1], bounds[1:]):
        z = jnp.einsum("bhqd,bhkd->bhqk", q[:, :, s0:s1], k[:, :, :s1]).astype(jnp.float32) * scale
        mask = jnp.arange(s1)[None, :] < jnp.arange(s0, s1)[:, None]
        log_keep = jnp.where(mask, jax.nn.log_sigmoid(-z), 0.0)
        later = lax.cumsum(log_keep, axis=3, reverse=True) - log_keep
        weights = jnp.where(mask, jnp.exp(jax.nn.log_sigmoid(z) + later), 0.0)
        outs.append(jnp.einsum("bhqk,bhkd->bhqd", weights.astype(v.dtype), v[:, :, :s1]))
    return jnp.concatenate(outs, axis=2)

def hybrid_mixer(x, w_in, b_gate, dn_conv_w, dn_a_log, dn_dt_bias, dn_norm_g, w_branch_dn, w_branch_sb, w_out):
    b, l, d = x.shape
    proj = x @ w_in
    dn_qkv, dn_z, dn_b, dn_a, sb_qkv, gates = jnp.split(proj, SPLIT_POINTS, axis=-1)
    dn_qkv = jax.nn.silu(causal_depthwise_conv(dn_qkv, dn_conv_w))
    q, k, v = jnp.split(dn_qkv, 3, axis=-1)
    q = l2_normalize(split_heads(q, DN_HEADS)) * (DN_HEAD_DIM ** -0.5)
    k = l2_normalize(split_heads(k, DN_HEADS))
    v = split_heads(v, DN_HEADS).astype(jnp.float32)
    beta = jax.nn.sigmoid(dn_b.astype(jnp.float32)).transpose(0, 2, 1)
    g = (-jnp.exp(dn_a_log.astype(jnp.float32))
         * jax.nn.softplus(dn_a.astype(jnp.float32) + dn_dt_bias.astype(jnp.float32))).transpose(0, 2, 1)
    pad = (DN_CHUNK - N_META % DN_CHUNK) % DN_CHUNK
    front = lambda t: jnp.pad(t, [(0, 0), (0, 0), (pad, 0)] + [(0, 0)] * (t.ndim - 3))
    o_dn = gated_delta_rule_chunked(front(q), front(k), front(v), front(beta), front(g))[:, :, pad:]
    o_dn = merge_heads(rms_norm(o_dn, dn_norm_g)) * jax.nn.silu(dn_z.astype(jnp.float32))
    sq, sk, sv = (split_heads(t, SB_HEADS) for t in jnp.split(sb_qkv, 3, axis=-1))
    o_sb = merge_heads(stick_breaking_attention(sq, sk, sv))
    gate = jax.nn.sigmoid(gates.reshape(b, l, N_BRANCH, d) + b_gate)
    merged = (gate[:, :, 0] * (o_dn.astype(x.dtype) @ w_branch_dn)
              + gate[:, :, 1] * (o_sb.astype(x.dtype) @ w_branch_sb))
    return merged @ w_out

def hierarchical_moe(h, router_group_w, router_group_b, router_expert_w, router_expert_b,
                     expert_w_gate, expert_w_up, expert_w_down):
    b, l, d = h.shape
    t = h.reshape(b * l, d)
    group_probs = jax.nn.softmax((t @ router_group_w).astype(jnp.float32) + router_group_b, axis=-1)
    g_idx = jnp.argmax(group_probs, axis=-1)
    g_prob = jnp.max(group_probs, axis=-1)
    exp_logits = jnp.einsum("td,gde->tge", t, router_expert_w).astype(jnp.float32) + router_expert_b
    sel_logits = jnp.take_along_axis(exp_logits, g_idx[:, None, None], axis=1)[:, 0]
    top_logit, top_idx = lax.top_k(sel_logits, TOP_K_IN_GROUP)
    top_w = jax.nn.softmax(top_logit, axis=-1) * g_prob[:, None]
    combine_e = jnp.sum(jax.nn.one_hot(top_idx, EXPERTS_PER_GROUP) * top_w[..., None], axis=1)
    combine = jax.nn.one_hot(g_idx, N_GROUPS)[:, :, None] * combine_e[:, None, :]
    y = jnp.zeros_like(t)
    for gi in range(N_GROUPS):
        hid = (jax.nn.silu(jnp.einsum("td,edf->tef", t, expert_w_gate[gi]))
               * jnp.einsum("td,edf->tef", t, expert_w_up[gi]))
        hid = hid * combine[:, gi, :, None].astype(hid.dtype)
        y = y + jnp.einsum("tef,efd->td", hid, expert_w_down[gi])
    return y.reshape(b, l, d)

def second_inputs(seed: int = 0) -> dict:
    key = jax.random.key(seed)
    ks = jax.random.split(key, 24)
    f32 = jnp.float32
    nrm = lambda k, shape, scale: jax.random.normal(k, shape, f32) * scale
    col_scale = np.ones((IN_COLS,), np.float32)
    col_scale[COL_DN_V0:COL_DN_V0 + DN_WIDTH] = DEEPNORM_BETA
    col_scale[COL_SB_V0:COL_SB_V0 + SB_WIDTH] = DEEPNORM_BETA
    dt = jnp.exp(jax.random.uniform(ks[6], (DEPTH, DN_HEADS), f32, math.log(1e-3), math.log(1e-1)))
    return {
        "x": nrm(ks[0], (BATCH, SEQ, D_MODEL), 1.0),
        "meta_tokens": nrm(ks[1], (N_META, D_MODEL), 1.0),
        "ln_emb_g": 1.0 + nrm(ks[2], (D_MODEL,), 0.05),
        "ln_emb_b": nrm(ks[3], (D_MODEL,), 0.02),
        "w_in": nrm(ks[4], (DEPTH, D_MODEL, IN_COLS), D_MODEL ** -0.5) * jnp.asarray(col_scale),
        "b_gate": nrm(ks[5], (DEPTH, N_BRANCH, D_MODEL), 0.02),
        "dn_conv_w": nrm(ks[7], (DEPTH, DN_CONV, 3 * DN_WIDTH), DN_CONV ** -0.5),
        "dn_a_log": jnp.log(jax.random.uniform(ks[8], (DEPTH, DN_HEADS), f32, 1.0, 16.0)),
        "dn_dt_bias": jnp.log(jnp.expm1(dt)),
        "dn_norm_g": 1.0 + nrm(ks[9], (DEPTH, DN_HEAD_DIM), 0.05),
        "w_branch_dn": nrm(ks[10], (DEPTH, DN_WIDTH, D_MODEL), DEEPNORM_BETA * DN_WIDTH ** -0.5),
        "w_branch_sb": nrm(ks[11], (DEPTH, SB_WIDTH, D_MODEL), DEEPNORM_BETA * SB_WIDTH ** -0.5),
        "w_out": nrm(ks[12], (DEPTH, D_MODEL, D_MODEL), DEEPNORM_BETA * D_MODEL ** -0.5),
        "ln1_g": 1.0 + nrm(ks[13], (DEPTH, D_MODEL), 0.05),
        "ln1_b": nrm(ks[14], (DEPTH, D_MODEL), 0.02),
        "router_group_w": nrm(ks[15], (DEPTH, D_MODEL, N_GROUPS), D_MODEL ** -0.5),
        "router_group_b": nrm(ks[16], (DEPTH, N_GROUPS), 0.01),
        "router_expert_w": nrm(ks[17], (DEPTH, N_GROUPS, D_MODEL, EXPERTS_PER_GROUP), D_MODEL ** -0.5),
        "router_expert_b": nrm(ks[18], (DEPTH, N_GROUPS, EXPERTS_PER_GROUP), 0.01),
        "expert_w_gate": nrm(ks[19], (DEPTH, N_GROUPS, EXPERTS_PER_GROUP, D_MODEL, EXPERT_FF), D_MODEL ** -0.5),
        "expert_w_up": nrm(ks[20], (DEPTH, N_GROUPS, EXPERTS_PER_GROUP, D_MODEL, EXPERT_FF),
                           DEEPNORM_BETA * D_MODEL ** -0.5),
        "expert_w_down": nrm(ks[21], (DEPTH, N_GROUPS, EXPERTS_PER_GROUP, EXPERT_FF, D_MODEL),
                             DEEPNORM_BETA * EXPERT_FF ** -0.5),
        "ln2_g": 1.0 + nrm(ks[22], (DEPTH, D_MODEL), 0.05),
        "ln2_b": nrm(ks[23], (DEPTH, D_MODEL), 0.02),
    }

def second_block(x, meta_tokens, ln_emb_g, ln_emb_b, w_in, b_gate, dn_conv_w, dn_a_log, dn_dt_bias, dn_norm_g,
              w_branch_dn, w_branch_sb, w_out, ln1_g, ln1_b, router_group_w, router_group_b, router_expert_w,
              router_expert_b, expert_w_gate, expert_w_up, expert_w_down, ln2_g, ln2_b):
    b = x.shape[0]
    meta = jnp.broadcast_to(meta_tokens[None].astype(x.dtype), (b, N_META, x.shape[-1]))
    h = layer_norm(jnp.concatenate([meta, x], axis=1), ln_emb_g, ln_emb_b)
    for i in range(DEPTH):
        mix = hybrid_mixer(h, w_in[i], b_gate[i], dn_conv_w[i], dn_a_log[i], dn_dt_bias[i], dn_norm_g[i],
                           w_branch_dn[i], w_branch_sb[i], w_out[i])
        h = layer_norm(DEEPNORM_ALPHA * h + mix, ln1_g[i], ln1_b[i])
        ffn = hierarchical_moe(h, router_group_w[i], router_group_b[i], router_expert_w[i], router_expert_b[i],
                               expert_w_gate[i], expert_w_up[i], expert_w_down[i])
        h = layer_norm(DEEPNORM_ALPHA * h + ffn, ln2_g[i], ln2_b[i])
    return h[:, N_META:]


def setup_inputs(seed=0):
    out = dict(first_inputs(seed))
    for name, value in second_inputs(seed + 1).items():
        if name != "x":
            out[name + "_2"] = value
    return out


def reference(
    x, norm_mix, norm_ffn, norm_final, ffn_w_up, ffn_conv_w, ffn_conv_b, ffn_w_down, moba_w_qkv,
    moba_w_o, rwkv_mu, rwkv_w_rkv, rwkv_w0, rwkv_w1, rwkv_w2, rwkv_a0, rwkv_a1, rwkv_a2,
    rwkv_g1, rwkv_g2, rwkv_k_k, rwkv_k_a, rwkv_r_k, rwkv_gn_w, rwkv_gn_b, rwkv_w_o, ssd_w_in,
    ssd_conv_w, ssd_conv_b, ssd_dt_bias, ssd_a_log, ssd_d, ssd_norm_w, ssd_w_out, conf_w_pw1,
    conf_b_pw1, conf_dw_w, conf_dw_b, conf_ln_w, conf_ln_b, conf_w_pw2, conf_b_pw2,
    meta_tokens_2, ln_emb_g_2, ln_emb_b_2, w_in_2, b_gate_2, dn_conv_w_2, dn_a_log_2,
    dn_dt_bias_2, dn_norm_g_2, w_branch_dn_2, w_branch_sb_2, w_out_2, ln1_g_2, ln1_b_2,
    router_group_w_2, router_group_b_2, router_expert_w_2, router_expert_b_2, expert_w_gate_2,
    expert_w_up_2, expert_w_down_2, ln2_g_2, ln2_b_2,
):
    x = first_block(
        x, norm_mix, norm_ffn, norm_final, ffn_w_up, ffn_conv_w, ffn_conv_b, ffn_w_down,
        moba_w_qkv, moba_w_o, rwkv_mu, rwkv_w_rkv, rwkv_w0, rwkv_w1, rwkv_w2, rwkv_a0, rwkv_a1,
        rwkv_a2, rwkv_g1, rwkv_g2, rwkv_k_k, rwkv_k_a, rwkv_r_k, rwkv_gn_w, rwkv_gn_b, rwkv_w_o,
        ssd_w_in, ssd_conv_w, ssd_conv_b, ssd_dt_bias, ssd_a_log, ssd_d, ssd_norm_w, ssd_w_out,
        conf_w_pw1, conf_b_pw1, conf_dw_w, conf_dw_b, conf_ln_w, conf_ln_b, conf_w_pw2,
        conf_b_pw2,
    )
    return second_block(
        x, meta_tokens_2, ln_emb_g_2, ln_emb_b_2, w_in_2, b_gate_2, dn_conv_w_2, dn_a_log_2,
        dn_dt_bias_2, dn_norm_g_2, w_branch_dn_2, w_branch_sb_2, w_out_2, ln1_g_2, ln1_b_2,
        router_group_w_2, router_group_b_2, router_expert_w_2, router_expert_b_2,
        expert_w_gate_2, expert_w_up_2, expert_w_down_2, ln2_g_2, ln2_b_2,
    )


_drawn_inputs = setup_inputs


def setup_inputs(seed=0):
    import zlib

    import numpy as np

    out = dict(_drawn_inputs(seed))
    spreads = {}
    factors = {'norm_mix': 5.375,
     'norm_ffn': 3.639,
     'ffn_conv_b': 6.487,
     'meta_tokens_2': 4.18,
     'b_gate_2': 8.0,
     'dn_a_log_2': 18.141,
     'dn_norm_g_2': 8.0,
     'ln1_b_2': 2.752,
     'router_group_b_2': 25.629,
     'router_expert_b_2': 29.955,
     'ln2_b_2': 2.852,
     'dn_dt_bias_2': 2.864}
    for name, (base, spread) in spreads.items():
        noise = np.random.default_rng([zlib.crc32(name.encode()), seed]).standard_normal(out[name].shape)
        drawn = base * np.exp(spread * noise) if base else spread * noise
        out[name] = jnp.asarray(drawn.astype(out[name].dtype))
    for name, factor in factors.items():
        out[name] = (out[name] * factor).astype(out[name].dtype)
    return out
```

```python
from contextlib import ExitStack

import numpy as np

import concourse.bass as bass
from concourse import mybir

F32 = mybir.dt.float32
F32R = mybir.dt.float32r
BF16 = mybir.dt.bfloat16
I32 = mybir.dt.int32
U32 = mybir.dt.uint32
ACT = mybir.ActivationFunctionType
ALU = mybir.AluOpType
AX = mybir.AxisListType

P = 128
D = 1024
KD = D // P
SEQ = 256
TT = SEQ // P
META = 16
NT = SEQ + META

A_HEADS, A_DH = 16, 64
FF = 2816
FT = FF // P
FJ = FF // 256

DN_H, DN_D = 4, 128
DN_W = DN_H * DN_D
DN_TAPS = 4
SB_H, SB_DH = 8, 64
SB_W = SB_H * SB_DH
LEVELS = 7
GROUPS, EPG = 4, 8
NE = GROUPS * EPG
EFF = 256
PAIRS = 2 * SEQ
ALPHA = 2.0 ** 0.25
GR = 2048

CONSTS = [("ident", P), ("ones", P), ("le", P), ("gt", P), ("nge", P), ("nones", P), ("lt", P), ("keep", 416), ("drop", 416),
          ("causal", 3 * P), ("level", LEVELS * P), ("slots", PAIRS), ("falling", 8), ("eps6", 1), ("eps5", 1)]
CAT = {}
_o = 0
for _n, _w in CONSTS:
    CAT[_n] = (_o, _w)
    _o += _w
CONST_COLS = _o


def constants():
    p = np.arange(P)[:, None]

    def f(n):
        return np.arange(n)[None, :]

    c = {"ident": p == f(P), "ones": np.ones((P, P)), "le": p <= f(P), "gt": p > f(P), "nge": -1.0 * (p >= f(P)),
         "nones": -np.ones((P, P)), "lt": p < f(P)}
    diag = np.where(f(P) <= p, 0.0, -1e30)
    c["causal"] = np.concatenate([diag, np.zeros((P, P)), diag], 1)
    c["keep"] = np.concatenate([p < f(SEQ) + META, p < f(NT - P), p < f(META)], 1)
    c["drop"] = np.where(c["keep"], 0.0, -1e30)
    j, i = p, f(P)
    c["level"] = np.concatenate([(j // (2 << s) == i // (2 << s)) & ((j >> s) % 2 == 0) & ((i >> s) % 2 == 1)
                                 for s in range(LEVELS)], 1)
    c["slots"] = np.broadcast_to(f(PAIRS), (P, PAIRS))
    c["falling"] = np.broadcast_to(8 - f(8), (P, 8))
    c["eps6"] = np.full((P, 1), 1e-6)
    c["eps5"] = np.full((P, 1), 1e-5)
    return np.concatenate([c[n].astype(np.float32) for n, _ in CONSTS], 1)


def build(nc, a, out):
    with ExitStack() as ctx:
        def sem(name):
            return ctx.enter_context(nc.semaphore(name))

        ARENA = 212800
        SBUF0 = -(-nc.sbuf_base // 32) * 32

        def place(name, shape, at, dt=F32):
            nbytes = 4 * int(np.prod(shape[1:]))
            assert at % 32 == 0 and at + nbytes <= ARENA, (name, at, nbytes)
            return nc.alloc_sbuf_tensor_at(name, shape, dt, offset=SBUF0 + at)

        cst = place("cst", [P, CONST_COLS], 0)

        def con(name, n=None, rows=P):
            o, w = CAT[name]
            return cst[0:rows, o:o + (n or w)]

        small = place("small", [P, 1024], 14144)
        cols = place("cols", [P, 256], 19200)
        vrow = place("vrow", [P, 2, P], 20224)
        X = place("X", [P, TT, D], 21248)
        hT_hi = place("hT_hi", [P, KD, NT], 29440, F32R)
        hT_lo = place("hT_lo", [P, KD, NT], 38144, F32R)
        R, H = 3, 2
        raw = place("raw", [P, R, GR], 46848)
        whi = place("whi", [P, H, GR], 71424, F32R)
        wlo = place("wlo", [P, H, GR], 87808, F32R)
        PH = 104192
        rows = place("rows", [P, 4, D], PH)
        XN = place("XN", [P, TT, D], PH + 16384)
        qT = place("qT", [P, KD, SEQ], PH + 24576)
        kT = place("kT", [P, KD, SEQ], PH + 32768)
        vv = place("vv", [P, TT, D], PH + 40960)
        oT_hi = place("oT_hi", [P, KD, SEQ], PH + 49152, F32R)
        oT_lo = place("oT_lo", [P, KD, SEQ], PH + 57344, F32R)
        prob = place("prob", [P, 2, 3 * P], PH + 65536)
        probT = place("probT", [P, 2, 3 * P], PH + 68608)
        cgate = place("cgate", [P, 2, 2, SEQ], PH + 71680)
        cup = place("cup", [P, 2, 2, SEQ], PH + 75776)
        hid = place("hid", [P, 2, 2, SEQ], PH + 79872)
        hid_hi = place("hid_hi", [P, 2, 2, SEQ], PH + 83968, F32R)
        hid_lo = place("hid_lo", [P, 2, 2, SEQ], PH + 88064, F32R)
        MT = place("MT", [META, D], PH + 92160)
        zero = place("zero", [1, D], PH + 96256, BF16)

        PG = ctx.enter_context(nc.psum_tensor("PG", [P, 4, 512], F32))
        PM = ctx.enter_context(nc.psum_tensor("PM", [P, 4, 512], F32))

        _used = [0]

        def tiny(n):
            o = _used[0]
            _used[0] += n
            assert _used[0] <= 1024
            return small[:, o:o + n]

        ss, rt, rs = tiny(6), tiny(6), tiny(6)
        mx, nmx, psum_, rinv = tiny(4), tiny(4), tiny(4), tiny(4)
        lnst, lnmv, lnrt, lnrs = tiny(48), tiny(8), tiny(4), tiny(4)

        s_x = [sem(f"s_x{t}") for t in range(TT)]
        s_cst, s_row, s_vrow, s_meta = sem("s_cst"), [sem(f"s_row{i}") for i in range(4)], sem("s_vrow"), sem("s_meta")
        landed = [sem(f"landed{i}") for i in range(R)]
        s_hi, s_lo, s_gran, s_ev = sem("s_hi"), sem("s_lo"), sem("s_gran"), sem("s_ev")
        s_ss, s_rt, s_rs, s_xn, s_xT, s_xhi, s_xlo = (sem(n) for n in ("s_ss", "s_rt", "s_rs", "s_xn", "s_xT", "s_xhi", "s_xlo"))
        s_S, s_mx, s_nmx, s_exp, s_rinv, s_prob, s_PT, s_probT, s_PV, s_oThi, s_oTlo = (
            sem(n) for n in ("s_S", "s_mx", "s_nmx", "s_exp", "s_rinv", "s_prob", "s_PT", "s_probT", "s_PV", "s_oThi", "s_oTlo"))
        s_colsT, s_cols = sem("s_colsT"), sem("s_cols")
        s_gaff, s_gtap, s_gconv, s_gsilu, s_uaff, s_utap, s_uconv, s_hid, s_hidhi, s_hidlo = (
            sem(n) for n in ("s_gaff", "s_gtap", "s_gconv", "s_gsilu", "s_uaff", "s_utap", "s_uconv", "s_hid", "s_hidhi", "s_hidlo"))
        s_mst, s_mmv, s_mrt, s_metaln = sem("s_mst"), sem("s_mmv"), sem("s_mrt"), sem("s_metaln")
        s_zero, s_x2 = sem("s_zero"), sem("s_x2")
        s_ln, s_lnv, s_lnrt, s_h, s_out = sem("s_ln"), sem("s_lnv"), sem("s_lnrt"), sem("s_h"), sem("s_out")

        def colview(w):
            return w.rearrange("(k p) n -> p k n", p=P)

        wqkv, wo = colview(a["moba_w_qkv"][0]), colview(a["moba_w_o"][0])
        wup, wdn = colview(a["ffn_w_up"][0]), a["ffn_w_down"][0].rearrange("(g p) n -> p g n", p=P)
        G_QKV, G_WO, G_FFN = 0, 12, 16
        G_IN = G_FFN + 3 * FJ
        G_DN, G_Z, G_SB, G_GATE, G_BSB, G_BDN, G_OUT = G_IN, G_IN + 6, G_IN + 8, G_IN + 14, G_IN + 22, G_IN + 24, G_IN + 26
        G_END = G_OUT + 4
        win = colview(a["w_in_2"][0])
        IN_Z, IN_BA, IN_SB, IN_GATE = 3 * DN_W, 4 * DN_W, 4 * DN_W + 2 * DN_H, 4 * DN_W + 2 * DN_H + 3 * SB_W
        CH = [(0, P), (P, P), (2 * P, META)]
        LEV = [LEVELS, LEVELS, 4]

        plan = []

        def plan_add(kind, *args):
            plan.append((kind, *args))

        for n in range(G_DN, G_Z):
            plan_add("gran", n)
            if n > G_DN:
                plan_add("silu", n - 1)
            if n == G_DN + 4:
                plan_add("square")
        plan_add("silu", G_Z - 1)
        plan_add("gran", G_Z)
        plan_add("ba")
        plan_add("gran", G_Z + 1)
        plan_add("gran", G_SB)
        for m in range(4):
            plan_add("norm", m)
        plan_add("gran", G_SB + 1)
        for m in range(4, 8):
            plan_add("norm", m)
        plan_add("decays")
        plan_add("gran", G_SB + 2)
        for c in range(3):
            plan_add("D", c)
        plan_add("gran", G_SB + 3)
        for c in range(3):
            plan_add("drow", c)
        for c in (1, 2):
            plan_add("dcol", c)
        plan_add("gran", G_SB + 4)
        for c in range(3):
            plan_add("G", c)
        for c in range(2):
            plan_add("ktr", c)
        plan_add("gran", G_SB + 5)
        for c in range(3):
            plan_add("QK", c)
        for c in range(3):
            plan_add("L0", c)
        for c in range(3):
            plan_add("vtr", c)
        for c in range(3):
            plan_add("sbv", c)
        for s in range(1, LEVELS):
            h = s - 1
            cs = [c for c in range(3) if s < LEV[c]]
            for c in cs:
                plan_add("X", s, c)
            plan_add("Z", h)
            plan_add("gran", G_GATE + h)
            for c in cs:
                plan_add("Y", s, c)
            plan_add("C", h)
            for c in cs:
                if s < LEV[c] - 1:
                    plan_add("T", s, c)
            if h > 0:
                plan_add("V", h - 1)
        plan_add("UV", 0)
        plan_add("gran", G_GATE + 6)
        plan_add("V", 5)
        plan_add("SU", 0)
        plan_add("Z", 6)
        plan_add("O", 0)
        plan_add("KS", 1)
        plan_add("gran", G_GATE + 7)
        plan_add("C", 6)
        plan_add("UV", 1)
        plan_add("Z", 7)
        plan_add("V", 6)
        plan_add("SU", 1)
        plan_add("C", 7)
        plan_add("O", 1)
        plan_add("KS", 2)
        plan_add("V", 7)
        plan_add("UV", 2)
        plan_add("O", 2)
        plan_add("sigmoid")
        plan_add("gran", G_BSB)
        plan_add("osq")
        plan_add("gran", G_BSB + 1)
        plan_add("orms", 0)
        plan_add("orms", 1)
        for n in range(G_BDN, G_END):
            plan_add("gran", n)

        BANKED = ("ba", "norm", "D", "drow", "dcol", "G", "ktr", "QK", "L0", "vtr", "sbv", "X", "Y", "T", "KS", "UV", "O", "SU", "orms")
        TURN = {}
        for st in plan:
            if st[0] in BANKED:
                TURN[st] = (len(TURN) % 2, len(TURN) // 2)
        pm_full, pm_free = [sem(f"pm_full{b}") for b in range(2)], [sem(f"pm_free{b}") for b in range(2)]

        def vacant(eng, *st):
            b, k = TURN[st]
            if k:
                eng.wait_ge(pm_free[b], k)
            return PM[:, b, :]

        def produced(eng, *st):
            b, k = TURN[st]
            eng.wait_ge(pm_full[b], k + 1)
            return PM[:, b, :]

        def consumed(eng, *st):
            b, k = TURN[st]
            eng.wait_ge(pm_free[b], k + 1)

        def full(*st):
            return pm_full[TURN[st][0]]

        def free(*st):
            return pm_free[TURN[st][0]]

        def heads(bank, n=P, w=P):
            return bank.rearrange("p (h n) -> p h n", h=DN_H)[0:n, :, 0:w]

        gT = place("gT", [P, 16, SEQ], PH)
        sbvT = place("sbvT", [P, 4, NT], PH)
        sqb = place("sqb", [P, 8, NT], PH + 4352)
        stick = place("stick", [P, 2, 416], PH + 16384)
        S = place("S", [P, DN_H, DN_D], PH + 22528)
        dnT = place("dnT", [P, 12, NT], PH + 24576)
        osq = place("osq", [P, DN_H, SEQ], PH + 32768)
        zT = place("zT", [P, DN_H, SEQ], PH + 37632)
        sbq = place("sbq", [P, 4, SEQ], PH + 41728)
        sbk = place("sbk", [P, 4, 3 * P], PH + 45824)
        sbv = place("sbv", [P, 3, SB_W], PH + 51968)
        osb_hi = place("osb_hi", [P, 4, SEQ], PH + 58112, F32R)
        osb_lo = place("osb_lo", [P, 4, SEQ], PH + 62208, F32R)
        dE, dA, dN, dX, dT, dU = (place(n, [P, 2, DN_H, P], PH + 66304 + 4096 * i) for i, n in enumerate(("dE", "dA", "dN", "dX", "dT", "dU")))
        odn = place("odn", [P, DN_H, SEQ], PH + 66304 + 4 * 4096)
        odn_hi = place("odn_hi", [P, DN_H, SEQ], PH + 66304 + 4096, F32R)
        odn_lo = place("odn_lo", [P, DN_H, SEQ], PH + 66304 + 2 * 4096, F32R)
        kd = place("kd", [P, 2, DN_H, DN_D], PH + 90880)
        vtok = place("vtok", [P, 3, DN_H, DN_D], PH + 94976)
        cE, cA, cN, cX, cT, cU = (place(n, [P, DN_H, META], PH + 101120 + 256 * i) for i, n in enumerate(("cE", "cA", "cN", "cX", "cT", "cU")))
        cR = place("cR", [P, DN_H, DN_D], PH + 102656)
        cV = place("cV", [P, DN_H, DN_D], PH + 104704)
        mT = place("mT", [P, KD, SEQ], PH + 24576)
        lnrow = place("lnrow", [P, 2, D], PH + 41728)

        def mat(ab, cc, c):
            return ab[:, c, :, :] if c < 2 else cc[0:META, :, :]

        wba = tiny(KD * 8).rearrange("p (k n) -> p k n", k=KD)
        dtb, alog, ea = tiny(4), tiny(4), tiny(4)
        ba = tiny(24).rearrange("p (c n) -> p c n", c=3)
        gx, gn, gy, gu, gp, beta, gdec, edcol = (tiny(12).rearrange("p (c n) -> p c n", c=3) for _ in range(8))
        cdc = tiny(4)

        s_dnaff, s_dntap, s_dnsilu, s_sq, s_l2, s_wba, s_init = (sem(n) for n in ("s_dnaff", "s_dntap", "s_dnsilu", "s_sq", "s_l2", "s_wba", "s_init"))
        s_bx, s_ey, s_dec, s_gm, s_gb, s_eD, s_E, s_cd = (sem(n) for n in ("s_bx", "s_ey", "s_dec", "s_gm", "s_gb", "s_eD", "s_E", "s_cd"))
        s_A, s_N, s_qd, s_U0, s_R, s_z, s_e, s_sp, s_cs, s_arg, s_w, s_pv, s_osbhi, s_osblo = (
            sem(n) for n in ("s_A", "s_N", "s_qd", "s_U0", "s_R", "s_z", "s_e", "s_sp", "s_cs", "s_arg", "s_w", "s_pv", "s_osbhi", "s_osblo"))
        s_sig, s_osq, s_on, s_odnhi, s_odnlo, s_m, s_mhi, s_mlo, s_lnrow = (
            sem(n) for n in ("s_sig", "s_osq", "s_on", "s_odnhi", "s_odnlo", "s_m", "s_mhi", "s_mlo", "s_lnrow"))

        def evacs(n):
            return 2 * (n + 1) if n < G_FFN else 2 * G_FFN + 2 * (n - G_IN + 1)

        def masks():
            return [(0, st[1]) if st[0] == "L0" else (st[1], st[2]) for st in plan if st[0] in ("L0", "X")]
        E_OF_HEAD = [1 + 3 + 3 * (h + 1) for h in range(SB_H)]
        MASKED = {m: i + 1 for i, m in enumerate(masks())}

        WIN = 64
        NL = GROUPS + NE
        RING = 12
        slot_at = [PH + 50176, PH + 58368, PH + 91136, PH + 66560, PH + 74752, PH + 82944, PH, PH + 8192, PH + 16384,
                   46848, 55040, 63232]
        ring = [place(f"expert_w{i}", [P, GR], at) for i, at in enumerate(slot_at)]
        X_hi = place("X_hi", [P, TT, D], 29440, F32R)
        X_lo = place("X_lo", [P, TT, D], 37632, F32R)
        xw = place("xw", [P, 2, KD, SEQ], 29440)
        pair = place("pair", [P, KD, PAIRS + 2 * SEQ], 71424)
        pick1 = place("pick1", [P, TT, PAIRS], PH + 24576)
        pick2 = place("pick2", [P, TT, PAIRS], PH + 28672)
        pick = place("pick", [P, TT, PAIRS], PH + 32768, F32R)
        pickT = place("pickT", [P, PAIRS // P, SEQ], PH + 36864, F32R)
        h1T = place("h1T", [P, KD, SEQ], PH + 99328)
        sg = place("sg", [P, 2, 2, SEQ], PH + 99328)
        hm = place("hm", [P, 2, 2, SEQ], PH + 103424)
        yg_hi = place("yg_hi", [P, PAIRS // P, D], PH, F32R)
        yg_lo = place("yg_lo", [P, PAIRS // P, D], PH + 50176, F32R)
        offi = place("offi", [P, 40], 18240, I32)
        wide = place("wide", [P, 4, TT, NE], 45824)
        M1, M2, M12, slotpos = (wide[:, i, :, :] for i in range(4))

        def grouped(m):
            return m.rearrange("p t (g e) -> p t g e", g=GROUPS)

        def tiny2(n):
            return tiny(TT * n).rearrange("p (t n) -> p t n", t=TT)

        wr = tiny(KD * NL).rearrange("p (k n) -> p k n", k=KD)
        rb = tiny(NL)
        logit, d5, e5, goh, gkey = tiny2(NL), tiny2(5), tiny2(5), tiny2(GROUPS), tiny2(GROUPS)
        sel, esel, ekey, oh1, oh2 = (tiny2(EPG) for _ in range(5))
        gmax, kmax, top1, top2, gsum, w1, w2, pos1, pos2 = (tiny2(1) for _ in range(9))
        prod = tiny(TT * NE).rearrange("p (t g e) -> p t g e", t=TT, g=GROUPS)
        incl, off, cmax, wslot = tiny(NE), tiny(NE), tiny(1), tiny(PAIRS // P)

        s_wr, s_h1T, s_xhi3, s_xlo3, s_logit, s_d5, s_e5, s_M, s_rank, s_off, s_P, s_w12 = (
            sem(n) for n in ("s_wr", "s_h1T", "s_xhi3", "s_xlo3", "s_logit", "s_d5", "s_e5", "s_M", "s_rank", "s_off", "s_P", "s_w12"))
        s_pad, s_xg, s_xga, s_xgv, s_pT, s_pickT = (sem(n) for n in ("s_pad", "s_xg", "s_xga", "s_xgv", "s_pT", "s_pickT"))
        in_ring = [sem(f"in_ring{i}") for i in range(RING)]
        s_win, s_mg, s_mu, s_md, s_sg, s_hm, s_yg, s_ygT, s_yghi, s_yglo, s_sum, s_res = (
            sem(n) for n in ("s_win", "s_mg", "s_mu", "s_md", "s_sg", "s_hm", "s_yg", "s_ygT", "s_yghi", "s_yglo", "s_sum", "s_res"))

        def by_count(eng, moe):
            eng.wait_ge(s_off, 1)
            fullest = eng.value_load(offi[0:1, NE:NE + 1], min_val=0, max_val=SEQ)
            with eng.If(fullest > WIN):
                moe(SEQ)
            with eng.Else():
                moe(WIN)

        def sums(W, par, what):
            if what < 2:
                return PG[:, 2 * par + what, 0:2 * W].rearrange("p (f n) -> p f n", f=2)
            y = PM[:, par, :] if W == WIN else PM[:, :, :].rearrange("p b n -> p (b n)")
            return y.rearrange("p (k n) -> p k n", k=KD)
        block = ctx.enter_context(nc.Block())

        @block.sync
        def _(sp):
            def load(n, src, it=0):
                if n >= R:
                    sp.wait_ge(s_lo, n - R + 1 + 6 * it)
                sp.dma_start(raw[:, n % R, :].rearrange("p (k n) -> p k n", k=src.shape[1]), src).then_inc(landed[n % R], 16)

            for i in range(12):
                load(G_QKV + i, wqkv[:, :, 256 * i:256 * i + 256])
            for i in range(4):
                load(G_WO + i, wo[:, :, 256 * i:256 * i + 256])
            load(G_FFN, wup[:, :, 0:256])
            load(G_FFN + 1, wup[:, :, FF:FF + 256])
            with sp.Fori(0, (FJ - 1) // 2) as it:
                for u in range(2):
                    n = G_FFN + 2 + 3 * u
                    j = 2 * it + 1 + u
                    load(n, wup[:, :, bass.ds(256 * j, 256)], it)
                    load(n + 1, wup[:, :, bass.ds(FF + 256 * j, 256)], it)
                    load(n + 2, wdn[:, bass.ds(2 * j - 2, 2), :], it)
            load(G_IN - 1, wdn[:, 2 * FJ - 2:2 * FJ, :])
            for i in range(6):
                load(G_DN + i, win[:, :, 256 * i:256 * i + 256])
            for i in range(2):
                load(G_Z + i, win[:, :, IN_Z + 256 * i:IN_Z + 256 * i + 256])
            for i in range(6):
                load(G_SB + i, win[:, :, IN_SB + 256 * i:IN_SB + 256 * i + 256])
            for i in range(8):
                load(G_GATE + i, win[:, :, IN_GATE + 256 * i:IN_GATE + 256 * i + 256])
            for g, name in ((G_BSB, "w_branch_sb_2"), (G_BDN, "w_branch_dn_2")):
                for i in range(2):
                    load(g + i, colview(a[name][0])[:, :, 512 * i:512 * i + 512])
            for i in range(4):
                load(G_OUT + i, colview(a["w_out_2"][0])[:, :, 256 * i:256 * i + 256])
            wexp = [a[f"expert_w_{n}_2"][0].rearrange("g e r c -> (g e) r c") for n in ("gate", "up", "down")]

            def expert_load(e, i, kind):
                src = wexp[kind][bass.ds(e, 1), :, :].rearrange("o (k p) n -> p (o k) n", p=P)
                dst = ring[3 * i + kind][:, :].rearrange("p (k n) -> p k n", k=src.shape[1])
                sp.dma_start(dst, src).then_inc(in_ring[3 * i + kind], 16)

            for i in range(4):
                for kind in range(3):
                    s = 3 * i + kind
                    if s < 3:
                        sp.wait_ge(s_gran, G_BDN)
                    elif s < 6:
                        sp.wait_ge(s_gran, G_OUT)
                    elif s < 9:
                        sp.wait_ge(s_m, 2)
                    else:
                        sp.wait_ge(s_lo, G_END)
                    expert_load(i, i, kind)
            with sp.Fori(1, NE // 4) as r:
                for i in range(4):
                    for kind, done in enumerate((s_mg, s_mu, s_md)):
                        sp.wait_ge(done, 4 * r + i - 3)
                        expert_load(4 * r + i, i, kind)
            for t in range(TT):
                sp.wait_ge(s_h, 2 * TT + t + 1)
                sp.dma_start(out[P * t:P * t + P, :], X[:, t, :]).then_inc(s_out, 16)
            sp.wait_ge(s_out, 16 * TT)

        @block.gpsimd
        def _(pool):
            def row(slot, vec):
                pool.dma_start(rows[:, slot, :], vec.partition_broadcast(P)).then_inc(s_row[slot], 16)

            row(0, a["norm_mix"][0])
            flat = a["ffn_conv_w"][0].rearrange("k (t p) -> (k t) p", p=P)
            n3 = 3 * 2 * FT
            pool.dma_start(vrow[:, 0, :], flat[0:P, :]).then_inc(s_vrow, 16)
            pool.dma_start(vrow[0:4, 1, :], flat[P:n3, :]).then_inc(s_vrow, 16)
            pool.dma_start(vrow[4:48, 1, :], a["ffn_conv_b"][0].rearrange("(t p) -> t p", p=P)).then_inc(s_vrow, 16)
            pool.dma_start(vrow[48:64, 1, :], a["b_gate_2"][0].rearrange("b (t p) -> (b t) p", p=P)).then_inc(s_vrow, 16)
            pool.dma_start(vrow[64:112, 1, :], a["dn_conv_w_2"][0].rearrange("k (t p) -> (k t) p", p=P)).then_inc(s_vrow, 16)
            pool.dma_start(vrow[112:113, 1, :], a["dn_norm_g_2"]).then_inc(s_vrow, 16)
            row(1, a["norm_ffn"][0])
            row(2, a["norm_final"])
            row(3, a["ln_emb_g_2"])
            pool.dma_start(MT[:, :], a["meta_tokens_2"]).then_inc(s_meta, 16)
            pool.wait_ge(s_xn, TT)
            row(0, a["ln_emb_b_2"])
            pool.dma_start(wba, win[:, :, IN_BA:IN_BA + 8]).then_inc(s_wba, 16)
            pool.dma_start(dtb, a["dn_dt_bias_2"][0].partition_broadcast(P)).then_inc(s_wba, 16)
            pool.dma_start(alog, a["dn_a_log_2"][0].partition_broadcast(P)).then_inc(s_wba, 16)
            pool.dma_start(wr[:, :, 0:GROUPS], colview(a["router_group_w_2"][0])).then_inc(s_wr, 16)
            for g in range(GROUPS):
                c = slice(GROUPS + EPG * g, GROUPS + EPG * g + EPG)
                pool.dma_start(wr[:, :, c], colview(a["router_expert_w_2"][0, g])).then_inc(s_wr, 16)
            pool.dma_start(rb[:, 0:GROUPS], a["router_group_b_2"][0].partition_broadcast(P)).then_inc(s_wr, 16)
            pool.dma_start(rb[:, GROUPS:NL], a["router_expert_b_2"][0].rearrange("g e -> (g e)").partition_broadcast(P)).then_inc(s_wr, 16)
            pool.wait_ge(s_xlo, 13)
            pool.memset(sbk[:, :, NT:3 * P], 0.0).then_inc(s_init, 1)
            pool.memset(sbv[:, 2, :], 0.0).then_inc(s_init, 1)
            pool.memset(ba, 0.0).then_inc(s_init, 1)

            def bc(ap, n, w):
                return ap.unsqueeze(1).to_broadcast([n, DN_H, w])

            for st in plan:
                if st[0] == "D":
                    c = st[1]
                    n = CH[c][1]
                    pool.wait_ge(s_eD, c + 1)
                    e = mat(dE, cE, c)
                    pool.tensor_tensor(e, e, bc(con("le")[0:n, 0:n], n, n), ALU.mult).then_inc(s_E, 1)
                elif st[0] in ("L0", "X"):
                    s, c = (0, st[1]) if st[0] == "L0" else (st[1], st[2])
                    n = CH[c][1]
                    pool.wait_ge(s_A, c + 1)
                    if s >= 2:
                        produced(pool, "X", s - 1, c)
                    elif s == 1:
                        pool.wait_ge(s_U0, c + 1)
                    m = con("level")[0:n, P * s:P * s + n]
                    pool.tensor_tensor(mat(dN, cN, c), mat(dA, cA, c), bc(m, n, n), ALU.mult).then_inc(s_N, 1)
            pool.wait_ge(s_w, SB_H)
            pool.wait_ge(s_pv, SB_H)
            for i, name in enumerate(("ln1_g_2", "ln1_b_2")):
                pool.dma_start(lnrow[:, i, :], a[name][0].partition_broadcast(P)).then_inc(s_lnrow, 16)
            for i, n in enumerate(("ln2_g_2", "ln2_b_2")):
                if i == 0:
                    pool.wait_ge(s_h, 2 * TT)
                pool.dma_start(lnrow[:, i, :], a[n][0].partition_broadcast(P)).then_inc(s_lnrow, 16)
            pool.wait_ge(s_gran, G_END)
            pool.memset(pair[:, :, PAIRS + SEQ:PAIRS + 2 * SEQ], 0.0).then_inc(s_pad, 1)
            pool.wait_ge(s_xga, KD // 2)
            pool.wait_ge(s_xgv, KD // 2)
            pool.wait_ge(s_pad, 1)

            def moe(W):
                def window(e, i, first=False):
                    at = pool.value_load(offi[0:1, bass.ds(e, 1)], min_val=0, max_val=PAIRS)
                    if not (first and i < 2):
                        pool.wait_ge(s_mu, e - 1)
                    pool.tensor_copy(xw[:, i % 2, :, 0:W], pair[:, :, bass.ds(at + SEQ, W)]).then_inc(s_win, 1)

                for i in range(4):
                    window(i, i, first=True)
                with pool.Fori(1, NE // 4) as r:
                    for i in range(4):
                        window(4 * r + i, i)

            by_count(pool, moe)

        @block.scalar
        def _(act):
            for t in range(TT):
                act.dma_start(X[:, t, :], a["x"][0, P * t:P * t + P, :]).then_inc(s_x[t], 16)
            act.dma_start(cst[:, :], a["consts"]).then_inc(s_cst, 16)

            def hi_part(n, it=0):
                act.wait_ge(landed[n % R], 16 * (n // R + 1) + 32 * it)
                if n >= H:
                    act.wait_ge(s_gran, n - H + 1 + 6 * it)
                act.activation(whi[:, n % H, :], raw[:, n % R, :], ACT.Copy).then_inc(s_hi, 1)

            def norm_sq(q):
                for t in range(TT):
                    if q == 0:
                        act.wait_ge(s_x[t], 16)
                    act.activation(XN[:, t, :], X[:, t, :], ACT.Square, accum_out=ss[:, 2 * q + t:2 * q + t + 1]).then_inc(s_ss, 1)
                if q == 0:
                    act.wait_ge(s_cst, 16)
                for t in range(TT):
                    i = 2 * q + t
                    act.wait_ge(s_ss, i + 1)
                    act.activation(rt[:, i:i + 1], ss[:, i:i + 1], ACT.Sqrt, scale=1.0 / D, bias=con("eps6")).then_inc(s_rt, 1)

            def norm_hi(q):
                for t in range(TT):
                    for f in range(2):
                        act.wait_ge(s_xT, 4 * q + 2 * t + f + 1)
                        act.activation(hT_hi[:, 4 * f:4 * f + 4, P * t:P * t + P],
                                       PM[:, 2 * t + f, :].rearrange("p (k n) -> p k n", k=4), ACT.Copy).then_inc(s_xhi, 1)

            norm_sq(0)
            hi_part(0)
            norm_hi(0)
            for n in range(12):
                hi_part(n + 1)
                act.wait_ge(s_gran, n + 1)
                src = PG[:, 2 * (n % 2), 0:256]
                if n < 4:
                    act.activation(qT[:, 2 * n, :], src, ACT.Copy, scale=A_DH ** -0.5).then_inc(s_ev, 1)
                elif n < 8:
                    act.activation(kT[:, 2 * n - 8, :], src, ACT.Copy).then_inc(s_ev, 1)
                else:
                    act.activation(vv[:, 0, 256 * (n - 8):256 * (n - 8) + 256], src, ACT.Copy).then_inc(s_ev, 1)
            for i in range(A_HEADS + 2):
                if i < A_HEADS:
                    h = i
                    act.wait_ge(s_nmx, h + 1)
                    for t in range(2):
                        c = (0, P) if t == 0 else (P, 3 * P)
                        act.activation(prob[:, h % 2, c[0]:c[1]], prob[:, h % 2, c[0]:c[1]], ACT.Exp,
                                       bias=nmx[:, 2 * (h % 2) + t:2 * (h % 2) + t + 1],
                                       accum_out=psum_[:, 2 * (h % 2) + t:2 * (h % 2) + t + 1]).then_inc(s_exp, 1)
                if 1 <= i <= A_HEADS:
                    h = i - 1
                    act.wait_ge(s_PT, h + 1)
                    if h >= 2:
                        act.wait_ge(s_PV, h - 1)
                    act.activation(probT[:, h % 2, :], PM[:, 2 + h % 2, 0:3 * P], ACT.Copy).then_inc(s_probT, 1)
                if i >= 2 and i % 2 == 1:
                    hp = (i - 2) // 2
                    act.wait_ge(s_PV, 2 * hp + 2)
                    act.activation(oT_hi[:, hp, :], PG[:, hp % 2, 0:SEQ], ACT.Copy).then_inc(s_oThi, 1)
            for n in range(G_WO, G_FFN):
                hi_part(n + 1)
                if n == G_WO:
                    act.wait_ge(s_mmv, 1)
                    act.activation(lnrt[0:META, 2:3], lnmv[0:META, 5:6], ACT.Sqrt, bias=con("eps5", rows=META)).then_inc(s_mrt, 1)
            act.wait_ge(s_ev, 32)
            norm_sq(1)
            norm_hi(1)
            act.wait_ge(s_colsT, 1)
            act.activation(cols[:, 0:P + 113], PG[:, 2, 0:P + 113], ACT.Copy).then_inc(s_cols, 1)
            act.wait_ge(s_cols, 1)

            def col(i, n=1):
                return cols[:, bass.ds(i, n)]

            def affine(j, dst, bank, tile0, s_done, par, cnt, gran):
                act.wait_ge(s_gran, gran)
                for f in range(2):
                    act.activation(dst[:, par, f, :], PG[:, bank + f, 0:SEQ], ACT.Identity,
                                   scale=col(2 * 2 * FT + tile0 + f), bias=col(3 * 2 * FT + tile0 + f)).then_inc(s_done, 1)

            def ffn_step(n, j, par, it, first=False, last=False):
                hi_part(n + 1, it)
                affine(j, cgate, 0, 2 * j, s_gaff, par, None, n + 1 + 6 * it)
                if not first:
                    hi_part(n + 2, it)
                act.wait_ge(s_gconv, j + 1)
                act.activation(cgate[:, par, :, :], cgate[:, par, :, :], ACT.Silu).then_inc(s_gsilu, 1)
                affine(j, cup, 2, FT + 2 * j, s_uaff, par, None, n + 2 + 6 * it)
                hi_part(n + (2 if first else 3), it)
                act.wait_ge(s_hid, j + 1)
                act.activation(hid_hi[:, par, :, :], hid[:, par, :, :], ACT.Copy).then_inc(s_hidhi, 1)

            ffn_step(G_FFN, 0, 0, 0, first=True)
            with act.Fori(0, (FJ - 1) // 2) as it:
                for u in range(2):
                    ffn_step(G_FFN + 2 + 3 * u, 2 * it + 1 + u, (1 + u) % 2, it)

            for t in range(TT):
                act.wait_ge(s_x2, t + 1)
                act.activation(XN[:, t, :], X[:, t, :], ACT.Square, accum_out=ss[:, 4 + t:5 + t]).then_inc(s_ss, 1)
            for t in range(TT):
                act.wait_ge(s_ss, 4 + t + 1)
                act.activation(rt[:, 4 + t:5 + t], ss[:, 4 + t:5 + t], ACT.Sqrt, scale=1.0 / D, bias=con("eps6")).then_inc(s_rt, 1)
            for t in range(TT):
                act.wait_ge(s_lnv, t + 1)
                act.activation(lnrt[:, t:t + 1], lnmv[:, 2 * t + 1:2 * t + 2], ACT.Sqrt, bias=con("eps5")).then_inc(s_lnrt, 1)

            def ln_hi(dst, src, i):
                act.wait_ge(s_xT, i + 1)
                act.activation(dst, src, ACT.Copy).then_inc(s_xhi, 1)

            hi_part(G_DN)
            ln_hi(hT_hi[:, :, 0:META], PG[:, 0, 0:P].rearrange("p (k n) -> p k n", k=KD), 8)
            for t in range(TT):
                for f in range(2):
                    c = META + P * t
                    ln_hi(hT_hi[:, 4 * f:4 * f + 4, c:c + P], PM[:, 2 * t + f, :].rearrange("p (k n) -> p k n", k=4), 9 + 2 * t + f)

            achain = [0]

            def astep(ins):
                achain[0] += 1
                ins.then_inc(s_e, 1)
                act.wait_ge(s_e, achain[0])

            def copy_out(dst, src, *st):
                act.activation(dst, src, ACT.Copy).then_inc(free(*st), 1)

            for st in plan:
                kind = st[0]
                if kind == "gran":
                    n = st[1]
                    if n + 1 < G_END:
                        hi_part(n + 1)
                    act.wait_ge(s_gran, n + 1)
                    b = 2 * (n % 2)
                    if n < G_Z:
                        for f in range(2):
                            m = 2 * (n - G_DN) + f
                            act.activation(dnT[:, m, :], PG[:, b + f, 0:NT], ACT.Copy, scale=col(192 + 36 + m)).then_inc(s_dnaff, 1)
                    elif n < G_SB:
                        m = 2 * (n - G_Z)
                        act.activation(zT[:, m:m + 2, :], PG[:, b:b + 2, 0:SEQ], ACT.Silu).then_inc(s_ev, 2)
                    elif n < G_GATE:
                        i, m = divmod(n - G_SB, 2)
                        if i == 0:
                            act.activation(sbq[:, 2 * m, :], PG[:, b, 0:SEQ], ACT.Copy, scale=SB_DH ** -0.5).then_inc(s_ev, 1)
                        elif i == 1:
                            act.activation(sbk[:, 2 * m, 0:NT], PG[:, b, 0:NT], ACT.Copy).then_inc(s_ev, 1)
                        else:
                            act.activation(sbvT[:, 2 * m, :], PG[:, b, 0:NT], ACT.Copy).then_inc(s_ev, 1)
                    elif n < G_BSB:
                        for f in range(2):
                            m = 2 * (n - G_GATE) + f
                            act.activation(gT[:, m, :], PG[:, b + f, 0:SEQ], ACT.Identity, bias=col(176 + m)).then_inc(s_ev, 1)
                    elif G_BDN <= n < G_OUT:
                        i = n - G_BDN
                        act.wait_ge(s_m, i + 1)
                        act.activation(hT_hi[:, 4 * i:4 * i + 4, 0:SEQ], mT[:, 4 * i:4 * i + 4, :], ACT.Copy).then_inc(s_mhi, 1)
                elif kind == "silu":
                    m = 2 * (st[1] - G_DN)
                    act.wait_ge(s_ev, evacs(st[1]))
                    act.activation(dnT[:, m:m + 2, :], dnT[:, m:m + 2, :], ACT.Silu).then_inc(s_dnsilu, 1)
                elif kind == "square":
                    act.wait_ge(s_dnsilu, 4)
                    for i in range(2):
                        act.activation(sqb[:, 4 * i:4 * i + 4, :], dnT[:, 4 * i:4 * i + 4, :], ACT.Square).then_inc(s_sq, 1)
                elif kind == "ba":
                    act.wait_ge(s_init, 3)
                    bank = produced(act, *st)
                    astep(act.activation(ba[:, 0:2, :], bank[:, 0:16].rearrange("p (c n) -> p c n", c=2), ACT.Copy))
                    copy_out(ba[0:META, 2, :], bank[0:META, 16:24], *st)
                elif kind == "norm":
                    bank = produced(act, *st)
                    act.activation(sqb[:, st[1], :], bank[:, 0:NT], ACT.Sqrt, bias=con("eps6")).then_inc(free(*st), 1)
                elif kind == "decays":
                    act.preload_act_table_set("natural_log_exp_and_others")
                    consumed(act, "ba")
                    act.wait_ge(s_wba, 48)
                    act.wait_ge(s_bx, 1)
                    act.activation(gy, gn, ACT.Exp).then_inc(s_ey, 1)
                    act.activation(beta, ba[:, :, 0:4], ACT.Exp, scale=-1.0).then_inc(s_ey, 1)
                    act.activation(ea, alog, ACT.Exp).then_inc(s_ey, 1)
                elif kind == "D":
                    c = st[1]
                    n = CH[c][1]
                    bank = produced(act, *st)
                    astep(act.activation(mat(dE, cE, c), heads(bank, n, n), ACT.Exp))
                    act.sem_inc(s_eD, 1)
                    act.sem_inc(free(*st), 1)
                elif kind == "drow":
                    c = st[1]
                    n = CH[c][1]
                    bank = produced(act, *st)
                    act.activation(dT[:, c, :, :] if c < 2 else cT[:, :, :], heads(bank, P, n), ACT.Exp).then_inc(free(*st), 1)
                elif kind == "dcol":
                    c = st[1]
                    n = CH[c][1]
                    bank = produced(act, *st)
                    act.activation(edcol[0:n, c, :], bank[0:n, 0:DN_H], ACT.Exp).then_inc(free(*st), 1)
                elif kind == "vtr":
                    c = st[1]
                    n = CH[c][1]
                    copy_out(vtok[0:n, c, :, :], heads(produced(act, *st), n), *st)
                elif kind == "sbv":
                    c = st[1]
                    n = CH[c][1]
                    copy_out(sbv[0:n, c, :], produced(act, *st)[0:n, :], *st)
                elif kind == "L0":
                    c = st[1]
                    n = CH[c][1]
                    act.wait_ge(s_qd, 3)
                    copy_out(mat(dT, cT, c), heads(produced(act, *st), n, n), *st)
                elif kind in ("X", "T"):
                    c = st[2]
                    n = CH[c][1]
                    dst = mat(dX, cX, c) if kind == "X" else mat(dT, cT, c)
                    copy_out(dst, heads(produced(act, *st), n, n), *st)
                elif kind == "O":
                    c = st[1]
                    bank = heads(produced(act, *st), P, CH[c][1])
                    if c == 0:
                        copy_out(odn[:, :, 0:P - META], bank[:, :, META:P], *st)
                    elif c == 1:
                        copy_out(odn[:, :, P - META:2 * P - META], bank, *st)
                    else:
                        copy_out(odn[:, :, SEQ - META:SEQ], bank, *st)
                elif kind == "Z":
                    h = st[1]
                    act.wait_ge(s_z, h + 1)
                    e = stick[:, h % 2, :]
                    if h >= 2:
                        act.wait_ge(s_pv, h - 1)
                    astep(act.activation(e, PM[:, 2 + h % 2, 0:416], ACT.Abs))
                    astep(act.activation(e, e, ACT.Exp, scale=-1.0))
                    astep(act.activation(e, e, ACT.Ln, bias=1.0))
                elif kind == "C":
                    h = st[1]
                    act.wait_ge(s_arg, h + 1)
                    e = stick[:, h % 2, :]
                    act.activation(e, e, ACT.Exp).then_inc(s_w, 1)
                elif kind == "V":
                    h = st[1]
                    b = SB_DH * (h % 2)
                    act.wait_ge(s_pv, h + 1)
                    act.activation(osb_hi[b:b + SB_DH, h // 2, :], PM[b:b + SB_DH, 2 + h % 2, 0:SEQ], ACT.Copy).then_inc(s_osbhi, 1)
                elif kind == "sigmoid":
                    act.wait_ge(s_ev, evacs(G_BSB - 1))
                    for i in (1, 0):
                        act.activation(gT[:, 8 * i:8 * i + 8, :], gT[:, 8 * i:8 * i + 8, :], ACT.Sigmoid).then_inc(s_sig, 1)
                elif kind == "osq":
                    consumed(act, "O", 2)
                    act.activation(osq[:, :, :], odn[:, :, :], ACT.Square).then_inc(s_osq, 1)
                elif kind == "orms":
                    i = st[1]
                    bank = produced(act, *st)
                    act.activation(osq[:, 2 * i:2 * i + 2, :], bank.rearrange("p (h n) -> p h n", h=2), ACT.Sqrt, scale=1.0 / DN_D,
                                   bias=con("eps6")).then_inc(free(*st), 1)
                    if i == 1:
                        act.wait_ge(s_on, 2)
                        act.activation(odn_hi[:, :, :], odn[:, :, :], ACT.Copy).then_inc(s_odnhi, 1)
            def ln_sqrt(k):
                for t in range(TT):
                    act.wait_ge(s_lnv, TT * k + t + 1)
                    act.activation(lnrt[:, t:t + 1], lnmv[:, 2 * t + 1:2 * t + 2], ACT.Sqrt, bias=con("eps5")).then_inc(s_lnrt, 1)

            ln_sqrt(1)
            for t in range(TT):
                act.wait_ge(s_h, TT + t + 1)
                act.activation(X_hi[:, t, :], X[:, t, :], ACT.Copy).then_inc(s_xhi3, 1)
                act.wait_ge(s_xT, 13 + 2 * t + 1)
                act.activation(h1T[:, 0:4, P * t:P * t + P], PM[:, 2 * t, :].rearrange("p (k n) -> p k n", k=4), ACT.Copy).then_inc(s_h1T, 1)
            act.wait_ge(s_d5, 1)
            act.activation(e5, d5, ACT.Exp).then_inc(s_e5, 1)
            for k in range(0, KD, 2):
                act.wait_ge(s_xg, k + 1)
                act.activation(pair[:, k, SEQ:SEQ + PAIRS], PM[:, k % 4, :], ACT.Copy).then_inc(s_xga, 1)
            act.wait_ge(s_pT, 1)
            act.activation(pickT[:, :, :].rearrange("p (b j) n -> p b (j n)", b=2), PG[:, 2:4, :], ACT.Copy).then_inc(s_pickT, 1)
            act.activation(wslot, PG[:, 1, 128:128 + PAIRS // P], ACT.Copy).then_inc(s_pickT, 1)

            def moe(W):
                with act.Fori(0, NE // 4) as r:
                    for i in range(4):
                        act.wait_ge(s_mg, 4 * r + i + 1)
                        act.activation(sg[:, i % 2, :, 0:W], sums(W, i % 2, 0), ACT.Silu).then_inc(s_sg, 1)

            by_count(act, moe)
            act.wait_ge(s_pickT, 2)
            for j in range(PAIRS // P):
                act.wait_ge(s_ygT, j + 1)
                src = (PM if j < 2 else PG)[:, 2 * (j % 2):2 * (j % 2) + 2, :]
                act.activation(yg_hi[:, j, :].rearrange("p (b n) -> p b n", b=2), src, ACT.Copy, scale=wslot[:, j:j + 1]).then_inc(s_yghi, 1)
            ln_sqrt(2)
        @block.vector
        def _(dve):
            seq = [0]
            s_dve = s_rs

            def step(ins):
                seq[0] += 1
                ins.then_inc(s_dve, 1)
                dve.wait_ge(s_dve, seq[0])

            def lo_part(n, it=0):
                dve.wait_ge(s_hi, n + 1 + 6 * it)
                dve.tensor_tensor(wlo[:, n % H, :], raw[:, n % R, :], whi[:, n % H, :].bitcast(F32), ALU.subtract).then_inc(s_lo, 1)

            def norm_apply(q):
                for t in range(TT):
                    i = 2 * q + t
                    dve.wait_ge(s_rt, i + 1)
                    step(dve.reciprocal(rs[:, i:i + 1], rt[:, i:i + 1]))
                    if t == 0:
                        dve.wait_ge(s_row[q], 16)
                    dve.scalar_tensor_tensor(XN[:, t, :], X[:, t, :], rs[:, i:i + 1], rows[:, q, :], ALU.mult, ALU.mult).then_inc(s_xn, 1)

            def norm_lo(q):
                for t in range(TT):
                    for f in range(2):
                        dve.wait_ge(s_xhi, 4 * q + 2 * t + f + 1)
                        c = slice(P * t, P * t + P)
                        dve.tensor_tensor(hT_lo[:, 4 * f:4 * f + 4, c], PM[:, 2 * t + f, :].rearrange("p (k n) -> p k n", k=4),
                                          hT_hi[:, 4 * f:4 * f + 4, c].bitcast(F32), ALU.subtract).then_inc(s_xlo, 1)

            dve.memset(zero[:, :], 0.0).then_inc(s_zero, 1)
            norm_apply(0)
            lo_part(0)
            norm_lo(0)
            for n in range(12):
                lo_part(n + 1)
                dve.wait_ge(s_gran, n + 1)
                src = PG[:, 2 * (n % 2) + 1, 0:256]
                if n < 4:
                    dve.tensor_scalar(qT[:, 2 * n + 1, :], src, A_DH ** -0.5, None, ALU.mult).then_inc(s_ev, 1)
                elif n < 8:
                    dve.tensor_copy(kT[:, 2 * n - 7, :], src).then_inc(s_ev, 1)
                else:
                    dve.tensor_copy(vv[:, 1, 256 * (n - 8):256 * (n - 8) + 256], src).then_inc(s_ev, 1)
            for i in range(A_HEADS + 2):
                if i < A_HEADS:
                    h = i
                    dve.wait_ge(s_S, h + 1)
                    if h >= 2:
                        dve.wait_ge(s_PT, h - 1)
                    for t in range(2):
                        c = (0, P) if t == 0 else (P, 3 * P)
                        dve.tensor_tensor_reduce(prob[:, h % 2, c[0]:c[1]], PM[:, h % 2, c[0]:c[1]], con("causal")[:, c[0]:c[1]],
                                                 1.0, -3e38, ALU.add, ALU.max, mx[:, 2 * (h % 2) + t:2 * (h % 2) + t + 1]).then_inc(s_mx, 1)
                    dve.wait_ge(s_mx, 2 * h + 2)
                    if h >= 2:
                        dve.wait_ge(s_exp, 2 * h - 2)
                    dve.tensor_scalar(nmx[:, 2 * (h % 2):2 * (h % 2) + 2], mx[:, 2 * (h % 2):2 * (h % 2) + 2], -1.0, None, ALU.mult).then_inc(s_nmx, 1)
                if 1 <= i <= A_HEADS:
                    h = i - 1
                    dve.wait_ge(s_exp, 2 * h + 2)
                    step(dve.reciprocal(rinv[:, 2 * (h % 2):2 * (h % 2) + 2], psum_[:, 2 * (h % 2):2 * (h % 2) + 2]))
                    for t in range(2):
                        c = (0, P) if t == 0 else (P, 3 * P)
                        dve.tensor_scalar(prob[:, h % 2, c[0]:c[1]], prob[:, h % 2, c[0]:c[1]],
                                          rinv[:, 2 * (h % 2) + t:2 * (h % 2) + t + 1], None, ALU.mult).then_inc(s_prob, 1)
                if i >= 2 and i % 2 == 1:
                    hp = (i - 2) // 2
                    dve.wait_ge(s_oThi, hp + 1)
                    dve.tensor_tensor(oT_lo[:, hp, :], PG[:, hp % 2, 0:SEQ], oT_hi[:, hp, :].bitcast(F32), ALU.subtract).then_inc(s_oTlo, 1)
            dve.wait_ge(s_meta, 16)
            for f in range(2):
                dve.bn_stats(lnst[0:META, 24 + 6 * f:30 + 6 * f], MT[:, 512 * f:512 * f + 512]).then_inc(s_mst, 1)
            dve.wait_ge(s_mst, 2)
            dve.bn_aggr(lnmv[0:META, 4:6], lnst[0:META, 24:36]).then_inc(s_mmv, 1)
            for n in range(G_WO, G_FFN):
                lo_part(n + 1)
                if n == G_WO + 1:
                    dve.wait_ge(s_mrt, 1)
                    step(dve.reciprocal(lnrs[0:META, 2:3], lnrt[0:META, 2:3]))
                    step(dve.tensor_scalar(MT[:, :], MT[:, :], lnmv[0:META, 4:5], lnrs[0:META, 2:3], ALU.subtract, ALU.mult))
                    dve.wait_ge(s_row[3], 16)
                    step(dve.tensor_tensor(MT[:, :], MT[:, :], rows[0:META, 3, :], ALU.mult))
                    dve.wait_ge(s_row[0], 32)
                    dve.tensor_tensor(MT[:, :], MT[:, :], rows[0:META, 0, :], ALU.add).then_inc(s_metaln, 1)
                dve.wait_ge(s_gran, n + 1)
                c = slice(256 * (n - G_WO), 256 * (n - G_WO) + 256)
                dve.tensor_tensor(X[:, :, c], X[:, :, c], PG[:, 2 * (n % 2):2 * (n % 2) + 2, 0:256], ALU.add).then_inc(s_ev, 2)
            norm_apply(1)
            norm_lo(1)
            dve.wait_ge(s_cols, 1)

            def col(i, n=1):
                return cols[:, bass.ds(i, n)]

            def taps(dst, par, bank, tile0, s_aff, s_tap, s_conv, j):
                for back in (1, 2):
                    for f in range(2):
                        if back == 1:
                            dve.wait_ge(s_aff, 2 * j + f + 1)
                        elif f == 0:
                            dve.wait_ge(s_tap, 2 * j + 2)
                        ins = dve.scalar_tensor_tensor(dst[:, par, f, back:SEQ], PG[:, bank + f, 0:SEQ - back],
                                                       col((2 - back) * 2 * FT + tile0 + f), dst[:, par, f, back:SEQ],
                                                       ALU.mult, ALU.add)
                        if back == 1:
                            ins.then_inc(s_tap, 1)
                        elif f == 1:
                            ins.then_inc(s_conv, 1)

            def ffn_step(n, j, par, it, first=False):
                lo_part(n + 1, it)
                taps(cgate, par, 0, 2 * j, s_gaff, s_gtap, s_gconv, j)
                if not first:
                    lo_part(n + 2, it)
                taps(cup, par, 2, FT + 2 * j, s_uaff, s_utap, s_uconv, j)
                lo_part(n + (2 if first else 3), it)
                dve.wait_ge(s_gsilu, j + 1)
                dve.wait_ge(s_uconv, j + 1)
                dve.tensor_tensor(hid[:, par, :, :], cgate[:, par, :, :], cup[:, par, :, :], ALU.mult).then_inc(s_hid, 1)
                dve.wait_ge(s_hidhi, j + 1)
                dve.tensor_tensor(hid_lo[:, par, :, :], hid[:, par, :, :], hid_hi[:, par, :, :].bitcast(F32), ALU.subtract).then_inc(s_hidlo, 1)

            ffn_step(G_FFN, 0, 0, 0, first=True)
            with dve.Fori(0, (FJ - 1) // 2) as it:
                for u in range(2):
                    ffn_step(G_FFN + 2 + 3 * u, 2 * it + 1 + u, (1 + u) % 2, it)

            for t in range(TT):
                dve.wait_ge(s_gran, G_IN)
                dve.tensor_tensor(X[:, t, :].rearrange("p (h n) -> p h n", h=2), X[:, t, :].rearrange("p (h n) -> p h n", h=2),
                                  PM[:, 2 * t:2 * t + 2, :], ALU.add).then_inc(s_x2, 1)
            for t in range(TT):
                i = 4 + t
                dve.wait_ge(s_rt, i + 1)
                step(dve.reciprocal(rs[:, i:i + 1], rt[:, i:i + 1]))
                dve.wait_ge(s_row[2], 16)
                step(dve.scalar_tensor_tensor(XN[:, t, :], X[:, t, :], rs[:, i:i + 1], rows[:, 2, :], ALU.mult, ALU.mult))
                for f in range(2):
                    dve.bn_stats(lnst[:, 12 * t + 6 * f:12 * t + 6 * f + 6], XN[:, t, 512 * f:512 * f + 512]).then_inc(s_ln, 1)
                dve.wait_ge(s_ln, 2 * t + 2)
                dve.bn_aggr(lnmv[:, 2 * t:2 * t + 2], lnst[:, 12 * t:12 * t + 12]).then_inc(s_lnv, 1)
            for t in range(TT):
                dve.wait_ge(s_lnrt, t + 1)
                step(dve.reciprocal(lnrs[:, t:t + 1], lnrt[:, t:t + 1]))
                step(dve.tensor_scalar(XN[:, t, :], XN[:, t, :], lnmv[:, 2 * t:2 * t + 1], lnrs[:, t:t + 1], ALU.subtract, ALU.mult))
                dve.wait_ge(s_row[3], 16)
                step(dve.tensor_tensor(XN[:, t, :], XN[:, t, :], rows[:, 3, :], ALU.mult))
                dve.wait_ge(s_row[0], 32)
                dve.tensor_tensor(X[:, t, :], XN[:, t, :], rows[:, 0, :], ALU.add).then_inc(s_h, 1)

            lo_part(G_DN)

            def ln_lo(dst, src, i):
                dve.wait_ge(s_xhi, i + 1)
                dve.tensor_tensor(dst[0], src, dst[1].bitcast(F32), ALU.subtract).then_inc(s_xlo, 1)

            c = slice(0, META)
            ln_lo((hT_lo[:, :, c], hT_hi[:, :, c]), PG[:, 0, 0:P].rearrange("p (k n) -> p k n", k=KD), 8)
            for t in range(TT):
                for f in range(2):
                    c = slice(META + P * t, META + P * t + P)
                    ln_lo((hT_lo[:, 4 * f:4 * f + 4, c], hT_hi[:, 4 * f:4 * f + 4, c]),
                          PM[:, 2 * t + f, :].rearrange("p (k n) -> p k n", k=4), 9 + 2 * t + f)

            def hbc(ap, n, w):
                return ap.unsqueeze(2).to_broadcast([n, DN_H, w])

            def bc(ap, n, w):
                return ap.unsqueeze(1).to_broadcast([n, DN_H, w])

            for st in plan:
                kind = st[0]
                if kind == "gran":
                    n = st[1]
                    if n + 1 < G_END:
                        lo_part(n + 1)
                    b = 2 * (n % 2)
                    if n < G_Z:
                        i = n - G_DN
                        for back in range(1, DN_TAPS):
                            for f in range(2):
                                m = 2 * i + f
                                if back == 1:
                                    dve.wait_ge(s_dnaff, m + 1)
                                elif f == 0:
                                    dve.wait_ge(s_dntap, 4 * i + 2 * (back - 1))
                                dve.scalar_tensor_tensor(dnT[:, m, back:NT], PG[:, b + f, 0:NT - back],
                                                         col(192 + 12 * (DN_TAPS - 1 - back) + m), dnT[:, m, back:NT],
                                                         ALU.mult, ALU.add).then_inc(s_ev if back == DN_TAPS - 1 else s_dntap, 1)
                    elif G_SB <= n < G_GATE:
                        dve.wait_ge(s_gran, n + 1)
                        i, m = divmod(n - G_SB, 2)
                        m = 2 * m + 1
                        if i == 0:
                            dve.tensor_scalar(sbq[:, m, :], PG[:, b + 1, 0:SEQ], SB_DH ** -0.5, None, ALU.mult).then_inc(s_ev, 1)
                        else:
                            dst = sbk[:, m, 0:NT] if i == 1 else sbvT[:, m, :]
                            dve.tensor_copy(dst, PG[:, b + 1, 0:NT]).then_inc(s_ev, 1)
                    elif G_BSB <= n < G_BDN:
                        i = n - G_BSB
                        dve.wait_ge(s_sig, 1)
                        dve.wait_ge(s_gran, n + 1)
                        consumed(dve, "O", 2)
                        dve.tensor_tensor(mT[:, 4 * i:4 * i + 4, :].rearrange("p (b f) n -> p b (f n)", b=2), PG[:, b:b + 2, :],
                                          gT[:, 8 + 4 * i:12 + 4 * i, :].rearrange("p (b f) n -> p b (f n)", b=2), ALU.mult).then_inc(s_ev, 2)
                    elif G_BDN <= n < G_OUT:
                        i = n - G_BDN
                        dve.wait_ge(s_sig, 2)
                        dve.wait_ge(s_gran, n + 1)
                        g = gT[:, 4 * i:4 * i + 4, :]
                        dve.tensor_tensor(g.rearrange("p (b f) n -> p b (f n)", b=2), PG[:, b:b + 2, :],
                                          g.rearrange("p (b f) n -> p b (f n)", b=2), ALU.mult).then_inc(s_ev, 2)
                        dve.wait_ge(s_ev, evacs(n))
                        m = mT[:, 4 * i:4 * i + 4, :]
                        dve.tensor_tensor(m, m, g, ALU.add).then_inc(s_m, 1)
                        dve.wait_ge(s_mhi, i + 1)
                        mh = hT_hi[:, 4 * i:4 * i + 4, 0:SEQ].bitcast(F32)
                        dve.tensor_tensor(hT_lo[:, 4 * i:4 * i + 4, 0:SEQ], m, mh, ALU.subtract).then_inc(s_mlo, 1)
                    elif n >= G_OUT:
                        dve.wait_ge(s_gran, n + 1)
                        c = slice(256 * (n - G_OUT), 256 * (n - G_OUT) + 256)
                        dve.scalar_tensor_tensor(X[:, :, c], X[:, :, c], ALPHA, PG[:, b:b + 2, 0:256], ALU.mult, ALU.add).then_inc(s_ev, 2)
                elif kind == "norm":
                    m = st[1]
                    consumed(dve, *st)
                    step(dve.reciprocal(sqb[:, m, :], sqb[:, m, :]))
                    if m < 4:
                        dve.scalar_tensor_tensor(dnT[:, m, :], dnT[:, m, :], DN_D ** -0.5, sqb[:, m, :], ALU.mult, ALU.mult).then_inc(s_l2, 1)
                    else:
                        dve.tensor_tensor(dnT[:, m, :], dnT[:, m, :], sqb[:, m, :], ALU.mult).then_inc(s_l2, 1)
                elif kind == "decays":
                    consumed(dve, "ba")
                    dve.wait_ge(s_wba, 48)
                    bias3 = dtb.unsqueeze(1).to_broadcast([P, 3, 4])
                    step(dve.tensor_tensor(gx, ba[:, :, 4:8], bias3, ALU.add))
                    step(dve.tensor_scalar(gn, gx, -1.0, None, ALU.mult))
                    dve.tensor_tensor(gn, gn, gx, ALU.min).then_inc(s_bx, 1)
                    dve.wait_ge(s_ey, 3)
                    step(dve.tensor_scalar(gu, gy, 2.0, None, ALU.add))
                    step(dve.reciprocal(gu, gu))
                    step(dve.tensor_tensor(gy, gy, gu, ALU.mult))
                    step(dve.tensor_tensor(gu, gy, gy, ALU.mult))
                    step(dve.tensor_scalar(gp, gu, 1.0 / 17, None, ALU.mult))
                    for k in range(15, 1, -2):
                        step(dve.scalar_tensor_tensor(gp, gp, 1.0 / k, gu, ALU.add, ALU.mult))
                    step(dve.scalar_tensor_tensor(gp, gp, 1.0, gy, ALU.add, ALU.mult))
                    step(dve.tensor_scalar(gp, gp, 2.0, None, ALU.mult))
                    step(dve.scalar_tensor_tensor(gp, gx, 0.0, gp, ALU.max, ALU.add))
                    step(dve.scalar_tensor_tensor(gdec, gp, -1.0, ea.unsqueeze(1).to_broadcast([P, 3, 4]), ALU.mult, ALU.mult))
                    step(dve.tensor_scalar(beta, beta, 1.0, None, ALU.add))
                    step(dve.reciprocal(beta, beta))
                    for c in range(3):
                        n = CH[c][1]
                        gh = gdec[0:n, c, :]
                        dve.tensor_tensor(mat(dN, cN, c), bc(con("gt")[0:n, 0:n], n, n), hbc(gh, n, n), ALU.mult).then_inc(s_gm, 1)
                        dst = dX[:, c, :, :] if c < 2 else cV[0:n, :, :]
                        dve.tensor_tensor(dst, bc(con("ones")[0:n, :], n, P), hbc(gh, n, P), ALU.mult).then_inc(s_gm, 1)
                elif kind == "drow" and st[1] == 1:
                    consumed(dve, *st)
                    dve.tensor_copy(cdc, dT[:, 1, :, P - 1:P].rearrange("p h o -> p (h o)")).then_inc(s_cd, 1)
                elif kind == "G":
                    c = st[1]
                    n = CH[c][1]
                    bank = heads(produced(dve, *st), n, n)
                    A = mat(dA, cA, c)
                    step(dve.tensor_tensor(A, bank, hbc(beta[0:n, c, :], n, n), ALU.mult))
                    dve.wait_ge(s_E, c + 1)
                    dve.tensor_tensor(A, A, mat(dE, cE, c), ALU.mult).then_inc(s_A, 1)
                    dve.wait_ge(s_A, c + 1)
                    dve.sem_inc(free(*st), 1)
                elif kind == "ktr":
                    c = st[1]
                    last = dE[:, c, :, P - 1:P].to_broadcast([P, DN_H, DN_D])
                    dve.tensor_tensor(kd[:, c, :, :], heads(produced(dve, *st)), last, ALU.mult).then_inc(free(*st), 1)
                elif kind == "QK":
                    c = st[1]
                    t0, n = CH[c]
                    E = mat(dE, cE, c)
                    bank = heads(produced(dve, *st), n, n)
                    if c < 2:
                        consumed(dve, "ktr", c)
                    dve.tensor_tensor(E, bank, E, ALU.mult).then_inc(free(*st), 1)
                    consumed(dve, "drow", c)
                    q = dnT[:, 0:4, t0:t0 + n]
                    ed = dT[:, c, :, :] if c < 2 else cT[:, :, :]
                    dve.tensor_tensor(q, q, ed, ALU.mult).then_inc(s_qd, 1)
                elif kind == "L0":
                    c = st[1]
                    n = CH[c][1]
                    dve.wait_ge(s_N, MASKED[0, c])
                    dve.tensor_tensor(mat(dU, cU, c), bc(con("ident")[0:n, 0:n], n, n), mat(dN, cN, c), ALU.subtract).then_inc(s_U0, 1)
                elif kind == "Y":
                    c = st[2]
                    n = CH[c][1]
                    U = mat(dU, cU, c)
                    dve.tensor_tensor(U, U, heads(produced(dve, *st), n, n), ALU.subtract).then_inc(free(*st), 1)
                elif kind == "KS":
                    c = st[1]
                    n = CH[c][1]
                    r = dN[:, c, :, :] if c < 2 else cR[0:n, :, :]
                    step(dve.tensor_tensor(r, heads(produced(dve, *st), n), hbc(edcol[0:n, c, :], n, DN_D), ALU.mult))
                    dve.tensor_tensor(r, vtok[0:n, c, :, :], r, ALU.subtract).then_inc(free(*st), 1)
                elif kind == "UV":
                    c = st[1]
                    n = CH[c][1]
                    dst = dX[:, c, :, :] if c < 2 else cV[0:n, :, :]
                    dve.tensor_tensor(dst, heads(produced(dve, *st), n), hbc(beta[0:n, c, :], n, DN_D), ALU.mult).then_inc(free(*st), 1)
                elif kind == "SU":
                    bank = heads(produced(dve, *st))
                    if st[1] == 0:
                        dve.tensor_copy(S[:, :, :], bank).then_inc(free(*st), 1)
                    else:
                        dve.wait_ge(s_cd, 1)
                        produced(dve, "O", 1)
                        step(dve.tensor_tensor(S[:, :, :], S[:, :, :], hbc(cdc, P, DN_D), ALU.mult))
                        dve.tensor_tensor(S[:, :, :], S[:, :, :], bank, ALU.add).then_inc(free(*st), 1)
                elif kind == "Z":
                    h = st[1]
                    dve.wait_ge(s_e, E_OF_HEAD[h])
                    e = stick[:, h % 2, :]
                    step(dve.scalar_tensor_tensor(e, PM[:, 2 + h % 2, 0:416], 0.0, e, ALU.max, ALU.add))
                    dve.tensor_tensor(e, e, con("keep"), ALU.mult).then_inc(s_sp, 1)
                elif kind == "C":
                    h = st[1]
                    dve.wait_ge(s_cs, h + 1)
                    dve.tensor_tensor(stick[:, h % 2, :], PM[:, 2 + h % 2, 0:416], con("drop"), ALU.add).then_inc(s_arg, 1)
                elif kind == "V":
                    h = st[1]
                    b = SB_DH * (h % 2)
                    dve.wait_ge(s_osbhi, h + 1)
                    dve.tensor_tensor(osb_lo[b:b + SB_DH, h // 2, :], PM[b:b + SB_DH, 2 + h % 2, 0:SEQ],
                                      osb_hi[b:b + SB_DH, h // 2, :].bitcast(F32), ALU.subtract).then_inc(s_osblo, 1)
                elif kind == "orms":
                    i = st[1]
                    consumed(dve, *st)
                    r = osq[:, 2 * i:2 * i + 2, :]
                    o = odn[:, 2 * i:2 * i + 2, :]
                    step(dve.reciprocal(r, r))
                    step(dve.scalar_tensor_tensor(o, o, col(240), r, ALU.mult, ALU.mult))
                    dve.tensor_tensor(o, o, zT[:, 2 * i:2 * i + 2, :], ALU.mult).then_inc(s_on, 1)
                    if i == 1:
                        dve.wait_ge(s_odnhi, 1)
                        dve.tensor_tensor(odn_lo[:, :, :], odn[:, :, :], odn_hi[:, :, :].bitcast(F32), ALU.subtract).then_inc(s_odnlo, 1)

            def layernorm(k):
                for t in range(TT):
                    for f in range(2):
                        dve.bn_stats(lnst[:, 12 * t + 6 * f:12 * t + 6 * f + 6], X[:, t, 512 * f:512 * f + 512]).then_inc(s_ln, 1)
                    dve.wait_ge(s_ln, 4 * k + 2 * t + 2)
                    dve.bn_aggr(lnmv[:, 2 * t:2 * t + 2], lnst[:, 12 * t:12 * t + 12]).then_inc(s_lnv, 1)
                dve.wait_ge(s_lnrow, 32 * k)
                for t in range(TT):
                    dve.wait_ge(s_lnv, TT * k + t + 1)
                    step(dve.scalar_tensor_tensor(X[:, t, :], X[:, t, :], lnmv[:, 2 * t:2 * t + 1], lnrow[:, 0, :], ALU.subtract, ALU.mult))
                    dve.wait_ge(s_lnrt, TT * k + t + 1)
                    step(dve.reciprocal(lnrs[:, t:t + 1], lnrt[:, t:t + 1]))
                    dve.scalar_tensor_tensor(X[:, t, :], X[:, t, :], lnrs[:, t:t + 1], lnrow[:, 1, :], ALU.mult, ALU.add).then_inc(s_h, 1)

            dve.wait_ge(s_ev, evacs(G_END - 1))
            layernorm(1)
            for t in range(TT):
                dve.wait_ge(s_xT, 13 + 2 * t + 2)
                dve.tensor_copy(h1T[:, 4:8, P * t:P * t + P], PM[:, 2 * t + 1, :].rearrange("p (k n) -> p k n", k=4)).then_inc(s_h1T, 1)
            for t in range(TT):
                dve.wait_ge(s_xhi3, t + 1)
                dve.tensor_tensor(X_lo[:, t, :], X[:, t, :], X_hi[:, t, :].bitcast(F32), ALU.subtract).then_inc(s_xlo3, 1)

            def wide2(x, n):
                return x.to_broadcast([P, TT, n])

            def first_max(onehot, key, diff, n):
                falling = con("falling")[:, 0:n].unsqueeze(1).to_broadcast([P, TT, n])
                step(dve.scalar_tensor_tensor(key, diff, 0.0, falling, ALU.is_equal, ALU.mult))
                step(dve.tensor_reduce(kmax, key, AX.X, ALU.max))
                step(dve.tensor_tensor(onehot, key, wide2(kmax, n), ALU.is_equal))

            dve.wait_ge(s_logit, 1)
            dve.wait_ge(s_wr, 112)
            step(dve.tensor_tensor(logit, PG[:, 0, 0:2 * NL].rearrange("p (t n) -> p t n", t=TT),
                                   rb.unsqueeze(1).to_broadcast([P, TT, NL]), ALU.add))
            glog, elog = logit[:, :, 0:GROUPS], logit[:, :, GROUPS:NL]
            step(dve.tensor_reduce(gmax, glog, AX.X, ALU.max))
            step(dve.tensor_tensor(d5[:, :, 0:GROUPS], glog, wide2(gmax, GROUPS), ALU.subtract))
            first_max(goh, gkey, d5[:, :, 0:GROUPS], GROUPS)
            gwide = goh.unsqueeze(3).to_broadcast([P, TT, GROUPS, EPG])
            step(dve.tensor_tensor(prod, grouped(elog), gwide, ALU.mult))
            step(dve.tensor_reduce(sel, prod.rearrange("p t g e -> p t e g"), AX.X, ALU.add))
            step(dve.tensor_reduce(top1, sel, AX.X, ALU.max))
            step(dve.tensor_tensor(esel, sel, wide2(top1, EPG), ALU.subtract))
            first_max(oh1, ekey, esel, EPG)
            step(dve.scalar_tensor_tensor(sel, oh1, -1e30, sel, ALU.mult, ALU.add))
            step(dve.tensor_reduce(top2, sel, AX.X, ALU.max))
            dve.tensor_tensor(d5[:, :, GROUPS:5], top2, top1, ALU.subtract).then_inc(s_d5, 1)
            step(dve.tensor_tensor(esel, sel, wide2(top2, EPG), ALU.subtract))
            first_max(oh2, ekey, esel, EPG)
            for m, oh in ((M1, oh1), (M2, oh2)):
                step(dve.tensor_tensor(grouped(m), gwide, oh.unsqueeze(2).to_broadcast([P, TT, GROUPS, EPG]), ALU.mult))
            dve.tensor_tensor(M12, M1, M2, ALU.add).then_inc(s_M, 1)
            dve.wait_ge(s_e5, 1)
            step(dve.tensor_reduce(gsum, e5[:, :, 0:GROUPS], AX.X, ALU.add))
            step(dve.scalar_tensor_tensor(w1, e5[:, :, GROUPS:5], 1.0, gsum, ALU.add, ALU.mult))
            step(dve.reciprocal(w1, w1))
            dve.tensor_tensor(w2, w1, e5[:, :, GROUPS:5], ALU.mult).then_inc(s_w12, 1)
            dve.wait_ge(s_rank, 1)
            cnt = PG[:, 1, 2 * NE:3 * NE]
            step(dve.tensor_tensor_scan(incl, con("ones")[:, 0:NE], cnt, 0.0, ALU.mult, ALU.add))
            step(dve.tensor_tensor(off, incl, cnt, ALU.subtract))
            step(dve.tensor_reduce(cmax, cnt, AX.X, ALU.max))
            step(dve.tensor_copy(offi[0:1, 0:NE], off[0:1, :]))
            dve.tensor_copy(offi[0:1, NE:NE + 1], cmax[0:1, :]).then_inc(s_off, 1)
            step(dve.tensor_tensor(slotpos, PG[:, 1, 0:2 * NE].rearrange("p (t n) -> p t n", t=TT),
                                   off.unsqueeze(1).to_broadcast([P, TT, NE]), ALU.add))
            for m, pos in ((M1, pos1), (M2, pos2)):
                step(dve.tensor_tensor(m, m, slotpos, ALU.mult))
                step(dve.tensor_reduce(pos, m, AX.X, ALU.add))
            for t in range(TT):
                step(dve.tensor_scalar(pick1[:, t, :], con("slots"), pos1[:, t, :], None, ALU.is_equal))
                step(dve.tensor_scalar(pick2[:, t, :], con("slots"), pos2[:, t, :], None, ALU.is_equal))
                dve.tensor_tensor(pick[:, t, :], pick1[:, t, :], pick2[:, t, :], ALU.add).then_inc(s_P, 1)
            for k in range(1, KD, 2):
                dve.wait_ge(s_xg, k + 1)
                dve.tensor_copy(pair[:, k, SEQ:SEQ + PAIRS], PM[:, k % 4, :]).then_inc(s_xgv, 1)

            def moe(W):
                with dve.Fori(0, NE // 4) as r:
                    for i in range(4):
                        e = 4 * r + i
                        at = dve.value_load(offi[0:1, bass.ds(e, 1)], min_val=0, max_val=PAIRS)
                        dve.wait_ge(s_mu, e + 1)
                        dve.wait_ge(s_sg, e + 1)
                        dve.tensor_tensor(hm[:, i % 2, :, 0:W], sg[:, i % 2, :, 0:W], sums(W, i % 2, 1), ALU.mult).then_inc(s_hm, 1)
                        dve.wait_ge(s_md, e + 1)
                        dve.tensor_copy(pair[:, :, bass.ds(at, W)], sums(W, i % 2, 2)).then_inc(s_yg, 1)

            by_count(dve, moe)
            dve.wait_ge(s_pickT, 2)
            for j in range(PAIRS // P):
                dve.wait_ge(s_yghi, j + 1)
                src = (PM if j < 2 else PG)[:, 2 * (j % 2):2 * (j % 2) + 2, :]
                dve.scalar_tensor_tensor(yg_lo[:, j, :].rearrange("p (b n) -> p b n", b=2), src, wslot[:, j:j + 1],
                                         yg_hi[:, j, :].rearrange("p (b n) -> p b n", b=2).bitcast(F32), ALU.mult, ALU.subtract).then_inc(s_yglo, 1)
            dve.wait_ge(s_sum, 1)
            for t in range(TT):
                dve.scalar_tensor_tensor(X[:, t, :].rearrange("p (b n) -> p b n", b=2), X[:, t, :].rearrange("p (b n) -> p b n", b=2),
                                         ALPHA, PM[:, 2 * t:2 * t + 2, :], ALU.mult, ALU.add).then_inc(s_res, 1)
            dve.wait_ge(s_res, TT)
            layernorm(2)
        @block.tensor
        def _(pe):
            def norm_T(q):
                for t in range(TT):
                    pe.wait_ge(s_xn, 2 * q + t + 1)
                    for k in range(KD):
                        mm = pe.transpose(PM[:, 2 * t + k // 4, P * (k % 4):P * (k % 4) + P], XN[:, t, P * k:P * k + P], con("ident"))
                        if k % 4 == 3:
                            mm.then_inc(s_xT, 1)

            def split3(dst, lh, ll, rh, rl, start, stop, **kw):
                pe.matmul(dst, lh, rh, start=start, stop=False, **kw)
                pe.matmul(dst, lh, rl, start=False, stop=False, **kw)
                return pe.matmul(dst, ll, rh, start=False, stop=stop, **kw)

            def w_of(w, n):
                return w[:, n % H, :].rearrange("p (k n) -> p k n", k=KD)

            def features(n, bank, ah, al, c, it=0):
                pe.wait_ge(s_lo, n + 1 + 6 * it)
                hw, lw = w_of(whi, n), w_of(wlo, n)
                for f in range(2):
                    for k in range(KD):
                        mm = split3(PG[:, bank + f, 0:c.stop - c.start], hw[:, k, P * f:P * f + P], lw[:, k, P * f:P * f + P],
                                    ah[:, k, c], al[:, k, c], k == 0, k == KD - 1)
                mm.then_inc(s_gran, 1)

            def tokens(n, bank, ah, al):
                pe.wait_ge(s_lo, n + 1)
                hw, lw = w_of(whi, n), w_of(wlo, n)
                for t in range(TT):
                    for k in range(KD):
                        c = slice(P * t, P * t + P)
                        mm = split3(PG[:, bank + t, 0:256], ah[:, k, c], al[:, k, c], hw[:, k, :], lw[:, k, :], k == 0, k == KD - 1)
                mm.then_inc(s_gran, 1)

            pe.wait_ge(s_cst, 16)
            norm_T(0)
            pe.wait_ge(s_xlo, 4)
            for n in range(12):
                if n >= 2:
                    pe.wait_ge(s_ev, 2 * (n - 1))
                if n < 8:
                    features(n, 2 * (n % 2), hT_hi, hT_lo, slice(0, SEQ))
                else:
                    tokens(n, 2 * (n % 2), hT_hi, hT_lo)
            pe.wait_ge(s_ev, 24)
            for i in range(A_HEADS + 2):
                if i < A_HEADS:
                    h = i
                    b = A_DH * (h % 2)
                    if h >= 2:
                        pe.wait_ge(s_mx, 2 * h - 2)
                    pe.matmul(PM[:, h % 2, 0:P], qT[b:b + A_DH, h // 2, 0:P], kT[b:b + A_DH, h // 2, 0:P], start=True, stop=True)
                    pe.matmul(PM[:, h % 2, P:3 * P], qT[b:b + A_DH, h // 2, P:SEQ], kT[b:b + A_DH, h // 2, :], start=True, stop=True).then_inc(s_S, 1)
                if 1 <= i <= A_HEADS:
                    h = i - 1
                    pe.wait_ge(s_prob, 2 * h + 2)
                    if h >= 2:
                        pe.wait_ge(s_probT, h - 1)
                    for j in range(3):
                        mm = pe.transpose(PM[:, 2 + h % 2, P * j:P * j + P], prob[:, h % 2, P * j:P * j + P], con("ident"))
                    mm.then_inc(s_PT, 1)
                if i >= 2:
                    h = i - 2
                    hp, b = h // 2, A_DH * (h % 2)
                    pe.wait_ge(s_probT, h + 1)
                    if hp >= 2 and h % 2 == 0:
                        pe.wait_ge(s_oTlo, hp - 1)
                    o = PG[b:b + A_DH, hp % 2, 0:SEQ]
                    pe.matmul(o, vv[:, 0, A_DH * h:A_DH * h + A_DH], probT[:, h % 2, 0:SEQ], start=True, stop=False, skip_group_check=True)
                    pe.matmul(o[:, P:SEQ], vv[:, 1, A_DH * h:A_DH * h + A_DH], probT[:, h % 2, SEQ:3 * P], start=False, stop=True,
                              skip_group_check=True).then_inc(s_PV, 1)
            pe.wait_ge(s_oTlo, KD)
            for n in range(G_WO, G_FFN):
                if n >= G_WO + 2:
                    pe.wait_ge(s_ev, 2 * (n - 1))
                tokens(n, 2 * (n % 2), oT_hi, oT_lo)
            pe.wait_ge(s_vrow, 96)
            pe.wait_ge(s_ev, 32)
            pe.transpose(PG[:, 2, 0:P], vrow[:, 0, :], con("ident"))
            pe.transpose(PG[:, 2, P:P + 113], vrow[0:113, 1, :], con("ident", 113, 113)).then_inc(s_colsT, 1)
            norm_T(1)
            pe.wait_ge(s_xlo, 8)
            pe.wait_ge(s_zero, 1)
            for b in range(4):
                pe.matmul(PM[:, b, :], zero[0:1, 0:P], zero[0:1, 0:512], start=True, stop=True)

            def down(n, par, it=0, j=None):
                pe.wait_ge(s_hidlo, j + 1)
                pe.wait_ge(s_lo, n + 1 + 6 * it)
                hw = whi[:, n % H, :].rearrange("p (c n) -> p c n", c=2)
                lw = wlo[:, n % H, :].rearrange("p (c n) -> p c n", c=2)
                for t in range(TT):
                    for f in range(2):
                        for c in range(2):
                            x = slice(P * t, P * t + P)
                            w = slice(512 * f, 512 * f + 512)
                            mm = split3(PM[:, 2 * t + f, :], hid_hi[:, par, c, x], hid_lo[:, par, c, x], hw[:, c, w], lw[:, c, w],
                                        False, True, skip_group_check=True)
                mm.then_inc(s_gran, 1)
                return mm

            def ffn_step(n, j, par, it, first=False):
                if not first:
                    pe.wait_ge(s_gconv, j)
                else:
                    pe.wait_ge(s_cols, 1)
                features(n, 0, hT_hi, hT_lo, slice(0, SEQ), it)
                if not first:
                    pe.wait_ge(s_uconv, j)
                features(n + 1, 2, hT_hi, hT_lo, slice(0, SEQ), it)
                if not first:
                    down(n + 2, 1 - par, it, j - 1)

            ffn_step(G_FFN, 0, 0, 0, first=True)
            with pe.Fori(0, (FJ - 1) // 2) as it:
                for u in range(2):
                    ffn_step(G_FFN + 2 + 3 * u, 2 * it + 1 + u, (1 + u) % 2, it)
            down(G_IN - 1, (FJ - 1) % 2, 0, FJ - 1)
            pe.wait_ge(s_metaln, 1)
            for k in range(KD):
                mm = pe.transpose(PG[:, 0, META * k:META * k + META], MT[:, P * k:P * k + P], con("ident", META, META))
            mm.then_inc(s_xT, 1)
            for t in range(TT):
                pe.wait_ge(s_h, t + 1)
                for k in range(KD):
                    mm = pe.transpose(PM[:, 2 * t + k // 4, P * (k % 4):P * (k % 4) + P], X[:, t, P * k:P * k + P], con("ident"))
                    if k % 4 == 3:
                        mm.then_inc(s_xT, 1)
            pe.wait_ge(s_xlo, 13)

            def branch(n, ah, al):
                pe.wait_ge(s_lo, n + 1)
                hw, lw = (w[:, n % H, :].rearrange("p (k n) -> p k n", k=4) for w in (whi, wlo))
                for f in range(4):
                    dst = PG[:, 2 * (n % 2) + f // 2, SEQ * (f % 2):SEQ * (f % 2) + SEQ]
                    for k in range(4):
                        x = slice(P * f, P * f + P)
                        mm = split3(dst, hw[:, k, x], lw[:, k, x], ah[:, k, :], al[:, k, :], k == 0, k == 3)
                mm.then_inc(s_gran, 1)

            for st in plan:
                kind = st[0]
                if kind == "gran":
                    n = st[1]
                    if n >= G_IN + 2:
                        pe.wait_ge(s_ev, evacs(n - 2))
                    b = 2 * (n % 2)
                    if n < G_BSB:
                        own = G_Z <= n < G_SB + 2 or n >= G_GATE
                        features(n, b, hT_hi, hT_lo, slice(META if own else 0, NT))
                    elif n < G_BDN:
                        pe.wait_ge(s_osblo, SB_H)
                        branch(n, osb_hi, osb_lo)
                    elif n < G_OUT:
                        pe.wait_ge(s_odnlo, 1)
                        branch(n, odn_hi, odn_lo)
                    else:
                        pe.wait_ge(s_mlo, 2)
                        tokens(n, b, hT_hi, hT_lo)
                elif kind == "ba":
                    pe.wait_ge(s_wba, 48)
                    bank = vacant(pe, *st)
                    for c, (t0, n) in enumerate(CH):
                        for i, hT in enumerate((hT_hi, hT_lo)):
                            for k in range(KD):
                                mm = pe.matmul(bank[0:n, 8 * c:8 * c + 8], hT[:, k, t0:t0 + n].bitcast(F32), wba[:, k, :],
                                               start=i + k == 0, stop=i == 1 and k == KD - 1)
                    mm.then_inc(full(*st), 1)
                elif kind == "norm":
                    pe.wait_ge(s_sq, st[1] // 4 + 1)
                    pe.matmul(vacant(pe, *st)[:, 0:NT], con("ones"), sqb[:, st[1], :], start=True, stop=True).then_inc(full(*st), 1)
                elif kind in ("D", "drow"):
                    c = st[1]
                    n = CH[c][1]
                    pe.wait_ge(s_gm, 2 * c + 1 + (kind == "drow"))
                    bank = heads(vacant(pe, *st))
                    for h in range(DN_H):
                        if kind == "D":
                            mm = pe.matmul(bank[0:n, h, 0:n], mat(dN, cN, c)[:, h, :], con("le")[0:n, 0:n], start=True, stop=True)
                        else:
                            g = dX[:, c, h, :] if c < 2 else cV[0:n, h, :]
                            mm = pe.matmul(bank[:, h, 0:n], g, con("le")[0:n, 0:n], start=True, stop=True)
                    mm.then_inc(full(*st), 1)
                elif kind == "dcol":
                    c = st[1]
                    n = CH[c][1]
                    pe.wait_ge(s_gm, 2 * c + 2)
                    pe.matmul(vacant(pe, *st)[0:n, 0:DN_H], con("le")[0:n, 0:n], gdec[0:n, c, :], start=True, stop=True).then_inc(full(*st), 1)
                elif kind in ("G", "QK"):
                    c = st[1]
                    t0, n = CH[c]
                    pe.wait_ge(s_l2, 8)
                    bank = heads(vacant(pe, *st))
                    for h in range(DN_H):
                        k = dnT[:, 4 + h, t0:t0 + n]
                        mm = pe.matmul(bank[0:n, h, 0:n], k, k if kind == "G" else dnT[:, h, t0:t0 + n], start=True, stop=True)
                    mm.then_inc(full(*st), 1)
                elif kind in ("ktr", "vtr"):
                    c = st[1]
                    t0, n = CH[c]
                    pe.wait_ge(s_dnsilu, 6)
                    bank = heads(vacant(pe, *st))
                    for h in range(DN_H):
                        mm = pe.transpose(bank[0:n, h, :], dnT[:, (4 if kind == "ktr" else 8) + h, t0:t0 + n], con("ident"))
                    mm.then_inc(full(*st), 1)
                elif kind == "sbv":
                    c = st[1]
                    t0, n = CH[c]
                    pe.wait_ge(s_ev, evacs(G_GATE - 1))
                    pe.wait_ge(s_init, 3)
                    bank = heads(vacant(pe, *st))
                    for f in range(4):
                        mm = pe.transpose(bank[0:n, f, :], sbvT[:, f, t0:t0 + n], con("ident"))
                    mm.then_inc(full(*st), 1)
                elif kind in ("L0", "T"):
                    c = st[-1]
                    n = CH[c][1]
                    if kind == "L0":
                        pe.wait_ge(s_U0, c + 1)
                    else:
                        consumed(pe, "Y", st[1], c)
                    bank = heads(vacant(pe, *st), n, n)
                    U = mat(dU, cU, c)
                    for h in range(DN_H):
                        mm = pe.transpose(bank[:, h, :], U[:, h, :], con("ident")[0:n, 0:n])
                    mm.then_inc(full(*st), 1)
                elif kind in ("X", "Y"):
                    s, c = st[1:]
                    n = CH[c][1]
                    if kind == "X":
                        pe.wait_ge(s_N, MASKED[s, c])
                        consumed(pe, *(("T", s - 1, c) if s > 1 else ("L0", c)))
                        l, r = mat(dN, cN, c), mat(dT, cT, c)
                    else:
                        consumed(pe, "X", s, c)
                        if s > 1:
                            consumed(pe, "Y", s - 1, c)
                        l, r = mat(dX, cX, c), mat(dU, cU, c)
                    bank = heads(vacant(pe, *st), n, n)
                    for h in range(DN_H):
                        mm = pe.matmul(bank[:, h, :], l[:, h, :], r[:, h, :], start=True, stop=True)
                    mm.then_inc(full(*st), 1)
                elif kind == "KS":
                    c = st[1]
                    t0, n = CH[c]
                    consumed(pe, "SU", c - 1)
                    bank = heads(vacant(pe, *st))
                    for h in range(DN_H):
                        mm = pe.matmul(bank[0:n, h, :], dnT[:, 4 + h, t0:t0 + n], S[:, h, :], start=True, stop=True)
                    mm.then_inc(full(*st), 1)
                elif kind == "UV":
                    c = st[1]
                    n = CH[c][1]
                    consumed(pe, "Y", LEV[c] - 1, c)
                    consumed(pe, *(("vtr", 0) if c == 0 else ("KS", c)))
                    r = vtok[:, 0, :, :] if c == 0 else dN[:, 1, :, :] if c == 1 else cR[0:n, :, :]
                    bank = heads(vacant(pe, *st))
                    U = mat(dU, cU, c)
                    for h in range(DN_H):
                        mm = pe.matmul(bank[0:n, h, :], U[:, h, :], r[:, h, :], start=True, stop=True)
                    mm.then_inc(full(*st), 1)
                elif kind == "O":
                    c = st[1]
                    t0, n = CH[c]
                    consumed(pe, "UV", c)
                    pe.wait_ge(s_qd, 3)
                    bank = heads(vacant(pe, *st), P, n)
                    v = dX[:, c, :, :] if c < 2 else cV[0:n, :, :]
                    E = mat(dE, cE, c)
                    for h in range(DN_H):
                        if c:
                            pe.matmul(bank[:, h, :], S[:, h, :], dnT[:, h, t0:t0 + n], start=True, stop=False)
                        mm = pe.matmul(bank[:, h, :], v[:, h, :], E[:, h, :], start=c == 0, stop=True)
                    mm.then_inc(full(*st), 1)
                elif kind == "SU":
                    c = st[1]
                    consumed(pe, "UV", c)
                    consumed(pe, "ktr", c)
                    bank = heads(vacant(pe, *st))
                    for h in range(DN_H):
                        mm = pe.matmul(bank[:, h, :], kd[:, c, h, :], dX[:, c, h, :], start=True, stop=True)
                    mm.then_inc(full(*st), 1)
                elif kind == "Z":
                    h = st[1]
                    b = SB_DH * (h % 2)
                    if h == 0:
                        pe.wait_ge(s_ev, evacs(G_GATE - 1))
                        pe.wait_ge(s_init, 3)
                    if h >= 2:
                        pe.wait_ge(s_osblo, h - 1)
                    q, k = sbq[b:b + SB_DH, h // 2, :], sbk[b:b + SB_DH, h // 2, :]
                    Z = PM[:, 2 + h % 2, :]
                    pe.matmul(Z[:, 0:256], k[:, 0:P], q, start=True, stop=False, skip_group_check=True)
                    pe.matmul(Z[:, 256:400], k[:, P:2 * P], q[:, 112:256], start=False, stop=False, skip_group_check=True)
                    pe.matmul(Z[:, 400:416], k[:, 2 * P:3 * P], q[:, 240:256], start=False, stop=True, skip_group_check=True).then_inc(s_z, 1)
                elif kind == "C":
                    h = st[1]
                    pe.wait_ge(s_sp, h + 1)
                    Z, e = PM[:, 2 + h % 2, :], stick[:, h % 2, :]
                    tri, one = con("nge"), con("nones")
                    for o, w, i in ((slice(0, 256), tri, slice(0, 256)), (slice(112, 256), one, slice(256, 400)),
                                    (slice(240, 256), one, slice(400, 416)), (slice(256, 400), tri, slice(256, 400)),
                                    (slice(384, 400), one, slice(400, 416)), (slice(400, 416), tri, slice(400, 416))):
                        mm = pe.matmul(Z[:, o], w, e[:, i], start=False, stop=True, skip_group_check=True)
                    mm.then_inc(s_cs, 1)
                elif kind == "V":
                    h = st[1]
                    b = SB_DH * (h % 2)
                    pe.wait_ge(s_w, h + 1)
                    if h == 0:
                        consumed(pe, "sbv", 2)
                    e = stick[:, h % 2, :]
                    o = PM[b:b + SB_DH, 2 + h % 2, :]
                    x = slice(SB_DH * h, SB_DH * h + SB_DH)
                    pe.matmul(o[:, 0:256], sbv[:, 0, x], e[:, 0:256], start=True, stop=False, skip_group_check=True)
                    pe.matmul(o[:, 112:256], sbv[:, 1, x], e[:, 256:400], start=False, stop=False, skip_group_check=True)
                    pe.matmul(o[:, 240:256], sbv[:, 2, x], e[:, 400:416], start=False, stop=True, skip_group_check=True).then_inc(s_pv, 1)
                elif kind == "orms":
                    i = st[1]
                    pe.wait_ge(s_osq, 1)
                    pe.matmul(vacant(pe, *st), con("ones"), osq[:, 2 * i:2 * i + 2, :].rearrange("p h n -> p (h n)"),
                              start=True, stop=True).then_inc(full(*st), 1)
            for t in range(TT):
                pe.wait_ge(s_h, TT + t + 1)
                for k in range(KD):
                    mm = pe.transpose(PM[:, 2 * t + k // 4, P * (k % 4):P * (k % 4) + P], X[:, t, P * k:P * k + P], con("ident"))
                    if k % 4 == 3:
                        mm.then_inc(s_xT, 1)
            pe.wait_ge(s_h1T, 4)
            pe.wait_ge(s_wr, 112)
            for t in range(TT):
                for k in range(KD):
                    mm = pe.matmul(PG[:, 0, NL * t:NL * t + NL], h1T[:, k, P * t:P * t + P], wr[:, k, :], start=k == 0, stop=k == KD - 1)
            mm.then_inc(s_logit, 1)
            pe.wait_ge(s_M, 1)
            pe.matmul(PG[:, 1, 0:NE], con("lt"), M12[:, 0, :], start=True, stop=True)
            pe.matmul(PG[:, 1, NE:2 * NE], con("ones"), M12[:, 0, :], start=True, stop=False)
            pe.matmul(PG[:, 1, NE:2 * NE], con("lt"), M12[:, 1, :], start=False, stop=True)
            pe.matmul(PG[:, 1, 2 * NE:3 * NE], con("ones"), M12[:, 0, :], start=True, stop=False)
            pe.matmul(PG[:, 1, 2 * NE:3 * NE], con("ones"), M12[:, 1, :], start=False, stop=True).then_inc(s_rank, 1)
            pe.wait_ge(s_xlo3, TT)
            pe.wait_ge(s_P, TT)
            for k in range(KD):
                if k >= 4:
                    pe.wait_ge(s_xgv if k % 2 else s_xga, k // 2 - 1)
                for t in range(TT):
                    for i, x in enumerate((X_hi, X_lo)):
                        mm = pe.matmul(PM[:, k % 4, :], x[:, t, P * k:P * k + P], pick[:, t, :], start=t + i == 0, stop=t + i == 2)
                mm.then_inc(s_xg, 1)
            pe.wait_ge(s_w12, 1)
            for j in range(PAIRS // P):
                for t in range(TT):
                    for pk, w in ((pick1, w1), (pick2, w2)):
                        pe.matmul(PG[:, 1, 128 + j:129 + j], pk[:, t, P * j:P * j + P], w[:, t, :], start=t == 0 and pk is pick1,
                                  stop=t == 1 and pk is pick2)
            for j in range(PAIRS // P):
                for t in range(TT):
                    mm = pe.transpose(PG[:, 2 + j // 2, SEQ * (j % 2) + P * t:SEQ * (j % 2) + P * t + P],
                                      pick[:, t, P * j:P * j + P].bitcast(F32), con("ident"))
            mm.then_inc(s_pT, 1)
            pe.wait_ge(s_pickT, 2)
            pe.wait_ge(s_xga, KD // 2)
            pe.wait_ge(s_xgv, KD // 2)

            def moe(W):
                with pe.Fori(0, NE // 4) as r:
                    for i in range(4):
                        pe.wait_ge(s_win, 4 * r + i + 1)
                        for kind, done in enumerate((s_mg, s_mu)):
                            pe.wait_ge(in_ring[3 * i + kind], 16 * r + 16)
                            w = ring[3 * i + kind][:, :].rearrange("p (k n) -> p k n", k=KD)
                            dst = sums(W, i % 2, kind)
                            for f in range(2):
                                for k in range(KD):
                                    mm = pe.matmul(dst[:, f, :], w[:, k, P * f:P * f + P], xw[:, i % 2, k, 0:W], start=k == 0, stop=k == KD - 1)
                            mm.then_inc(done, 1)
                        pe.wait_ge(in_ring[3 * i + 2], 16 * r + 16)
                        pe.wait_ge(s_hm, 4 * r + i + 1)
                        w = ring[3 * i + 2][:, :].rearrange("p (f n) -> p f n", f=2)
                        dst = sums(W, i % 2, 2)
                        for k in range(KD):
                            for f in range(2):
                                mm = pe.matmul(dst[:, k, :], w[:, f, P * k:P * k + P], hm[:, i % 2, f, 0:W], start=f == 0, stop=f == 1)
                        mm.then_inc(s_md, 1)

            by_count(pe, moe)
            pe.wait_ge(s_yg, NE)
            for j in range(PAIRS // P):
                dst = PM if j < 2 else PG
                for k in range(KD):
                    mm = pe.transpose(dst[:, 2 * (j % 2) + k // 4, P * (k % 4):P * (k % 4) + P], pair[:, k, P * j:P * j + P], con("ident"))
                mm.then_inc(s_ygT, 1)
            for j in range(PAIRS // P):
                pe.wait_ge(s_yglo, max(j + 1, 2))
                for t in range(TT):
                    for b in range(2):
                        for y in (yg_hi, yg_lo):
                            mm = pe.matmul(PM[:, 2 * t + b, :], pickT[:, j, P * t:P * t + P], y[:, j, 512 * b:512 * b + 512],
                                           start=j == 0 and y is yg_hi, stop=j == PAIRS // P - 1 and y is yg_lo)
            mm.then_inc(s_sum, 1)


INPUTS = ["x", "norm_mix", "norm_ffn", "norm_final", "ffn_w_up", "ffn_conv_w", "ffn_conv_b", "ffn_w_down", "moba_w_qkv",
          "moba_w_o", "meta_tokens_2", "ln_emb_g_2", "ln_emb_b_2", "w_in_2", "b_gate_2", "dn_conv_w_2", "dn_a_log_2",
          "dn_dt_bias_2", "dn_norm_g_2", "w_branch_dn_2", "w_branch_sb_2", "w_out_2", "ln1_g_2", "ln1_b_2",
          "router_group_w_2", "router_group_b_2", "router_expert_w_2", "router_expert_b_2", "expert_w_gate_2",
          "expert_w_up_2", "expert_w_down_2", "ln2_g_2", "ln2_b_2"]


def kernel(**inputs):
    import concourse.bacc as bacc
    from concourse.bass_utils import run_bass_kernel_spmd

    nc = bacc.Bacc("TRN2", target_bir_lowering=False, num_devices=1)
    arrays = {f"in_{name}": np.ascontiguousarray(inputs[name]) for name in INPUTS}
    arrays["in_consts"] = constants()
    aps = {}
    for name, value in arrays.items():
        aps[name[3:]] = nc.dram_tensor(name, value.shape, mybir.dt.from_np(value.dtype), kind="ExternalInput").ap()
    out = nc.dram_tensor("out", (SEQ, D), F32, kind="ExternalOutput").ap()
    build(nc, aps, out)
    got = run_bass_kernel_spmd(nc, [arrays], core_ids=[0])
    return got.results[0]["out"].reshape(1, SEQ, D)
```

```python
from contextlib import ExitStack

import numpy as np

import concourse.bass as bass
from concourse import mybir

F32 = mybir.dt.float32
F32R = mybir.dt.float32r
BF16 = mybir.dt.bfloat16
I32 = mybir.dt.int32
U32 = mybir.dt.uint32
ACT = mybir.ActivationFunctionType
ALU = mybir.AluOpType
AX = mybir.AxisListType

P = 128
D = 1024
KD = D // P
SEQ = 256
TT = SEQ // P
META = 16
NT = SEQ + META

A_HEADS, A_DH = 16, 64
FF = 2816
FT = FF // P
FJ = FF // 256

DN_H, DN_D = 4, 128
DN_W = DN_H * DN_D
DN_TAPS = 4
SB_H, SB_DH = 8, 64
SB_W = SB_H * SB_DH
LEVELS = 7
GROUPS, EPG = 4, 8
NE = GROUPS * EPG
EFF = 256
PAIRS = 2 * SEQ
ALPHA = 2.0 ** 0.25
GR = 2048
RMS_EPS, LN_EPS = 1e-6, 1e-5
WIN = 64

CONSTS = [("ident", P), ("eps6", 1), ("eps5", 1), ("ones", P), ("le", P), ("gt", P), ("nge", P), ("nones", P), ("lt", P), ("keep", 416), ("drop", 416),
          ("causal", 3 * P), ("level", LEVELS * P), ("slots", PAIRS), ("falling", 8), ("fold", WIN)]
CAT = {}
_o = 0
for _n, _w in CONSTS:
    CAT[_n] = (_o, _w)
    _o += _w
CONST_COLS = _o
CONST_FIRST = P + 2


def constants():
    p = np.arange(P)[:, None]

    def f(n):
        return np.arange(n)[None, :]

    c = {"ident": p == f(P), "ones": np.ones((P, P)), "le": p <= f(P), "gt": p > f(P), "nge": -1.0 * (p >= f(P)),
         "nones": -np.ones((P, P)), "lt": p < f(P)}
    diag = np.where(f(P) <= p, 0.0, -1e30)
    c["causal"] = np.concatenate([diag, np.zeros((P, P)), diag], 1)
    c["keep"] = np.concatenate([p < f(SEQ) + META, p < f(NT - P), p < f(META)], 1)
    c["drop"] = np.where(c["keep"], 0.0, -1e30)
    j, i = p, f(P)
    c["level"] = np.concatenate([(j // (2 << s) == i // (2 << s)) & ((j >> s) % 2 == 0) & ((i >> s) % 2 == 1)
                                 for s in range(LEVELS)], 1)
    c["slots"] = np.broadcast_to(f(PAIRS), (P, PAIRS))
    c["falling"] = np.broadcast_to(8 - f(8), (P, 8))
    c["fold"] = p % WIN == f(WIN)
    c["eps6"] = np.full((P, 1), 1e-6)
    c["eps5"] = np.full((P, 1), 1e-5)
    return np.concatenate([c[n].astype(np.float32) for n, _ in CONSTS], 1)


def build(nc, a, out):
    with ExitStack() as ctx:
        def sem(name):
            return ctx.enter_context(nc.semaphore(name))

        ARENA = 212800
        SBUF0 = -(-nc.sbuf_base // 32) * 32

        def place(name, shape, at, dt=F32):
            nbytes = 4 * int(np.prod(shape[1:]))
            assert at % 32 == 0 and at + nbytes <= ARENA, (name, at, nbytes)
            return nc.alloc_sbuf_tensor_at(name, shape, dt, offset=SBUF0 + at)

        cst = place("cst", [P, CONST_COLS], 0)

        def con(name, n=None, rows=P):
            o, w = CAT[name]
            return cst[0:rows, o:o + (n or w)]

        small = place("small", [P, 1024], 14400)
        cols = place("cols", [P, 256], 19200)
        vrow = place("vrow", [P, 2, P], 20224)
        X = place("X", [P, TT, D], 21248)
        hT_hi = place("hT_hi", [P, KD, NT], 29440, F32R)
        hT_lo = place("hT_lo", [P, KD, NT], 38144, F32R)
        R, H = 3, 2
        raw = place("raw", [P, R, GR], 46848)
        whi = place("whi", [P, H, GR], 71424, F32R)
        wlo = place("wlo", [P, H, GR], 87808, F32R)
        PH = 104192
        rows = place("rows", [P, 4, D], PH)
        XN = place("XN", [P, TT, D], PH + 16384)
        qT = place("qT", [P, KD, SEQ], PH + 24576)
        kT = place("kT", [P, KD, SEQ], PH + 32768)
        vv = place("vv", [P, TT, D], PH + 40960)
        oT_hi = place("oT_hi", [P, KD, SEQ], PH + 49152, F32R)
        oT_lo = place("oT_lo", [P, KD, SEQ], PH + 57344, F32R)
        scratch = place("scratch", [P, TT, D], PH + 49152)
        scratch2 = place("scratch2", [P, TT, D], PH + 57344)
        prob = place("prob", [P, 3, 3 * P], PH + 98304)
        probT = place("probT", [P, 2, 3 * P], PH + 68608)
        cgate = place("cgate", [P, 2, 2, SEQ], PH + 71680)
        cup = place("cup", [P, 2, 2, SEQ], PH + 75776)
        hid = place("hid", [P, 2, 2, SEQ], PH + 79872)
        hid_hi = place("hid_hi", [P, 2, 2, SEQ], PH + 83968, F32R)
        hid_lo = place("hid_lo", [P, 2, 2, SEQ], PH + 88064, F32R)
        MT = place("MT", [META, D], PH + 92160)
        zero = place("zero", [1, D], PH + 96256, BF16)

        PG = ctx.enter_context(nc.psum_tensor("PG", [P, 4, 512], F32))
        PM = ctx.enter_context(nc.psum_tensor("PM", [P, 4, 512], F32))

        _used = [0]

        def tiny(n):
            o = _used[0]
            _used[0] += n
            assert _used[0] <= 1024
            return small[:, o:o + n]

        ss, rt, rs = tiny(6), tiny(6), tiny(6)
        ssq = tiny(4 * TT).rearrange("p (t n) -> p t n", t=TT)
        zsum, nmu, vs, ve = tiny(TT), tiny(TT), tiny(TT), tiny(TT)
        mx, nmx, psum_, rinv = tiny(6), tiny(6), tiny(6), tiny(6)
        lnst, lnmv, lnrt, lnrs = tiny(48), tiny(8), tiny(4), tiny(4)

        s_x = [sem(f"s_x{t}") for t in range(TT)]
        s_ssq, s_ffn, s_xg2, s_nmu, s_vs, s_ve = (sem(n) for n in ("s_ssq", "s_ffn", "s_xg2", "s_nmu", "s_vs", "s_ve"))
        s_cst2, s_row_mix = sem("s_cst2"), sem("s_row_mix")
        s_cst, s_row, s_vrow, s_meta = sem("s_cst"), [sem(f"s_row{i}") for i in range(4)], sem("s_vrow"), sem("s_meta")
        landed = [sem(f"landed{i}") for i in range(R)]
        s_hi, s_lo, s_gran, s_ev = sem("s_hi"), sem("s_lo"), sem("s_gran"), sem("s_ev")
        s_ss, s_rt, s_rs, s_xn, s_xT, s_xhi, s_xlo = (sem(n) for n in ("s_ss", "s_rt", "s_rs", "s_xn", "s_xT", "s_xhi", "s_xlo"))
        s_S, s_mx, s_nmx, s_exp, s_rinv, s_prob, s_PT, s_probT, s_PV, s_oThi, s_oTlo = (
            sem(n) for n in ("s_S", "s_mx", "s_nmx", "s_exp", "s_rinv", "s_prob", "s_PT", "s_probT", "s_PV", "s_oThi", "s_oTlo"))
        s_colsT, s_cols = sem("s_colsT"), sem("s_cols")
        s_gaff, s_gtap, s_gconv, s_gsilu, s_uaff, s_utap, s_uconv, s_hid, s_hidhi, s_hidlo = (
            sem(n) for n in ("s_gaff", "s_gtap", "s_gconv", "s_gsilu", "s_uaff", "s_utap", "s_uconv", "s_hid", "s_hidhi", "s_hidlo"))
        s_mst, s_mmv, s_mrt, s_metaln = sem("s_mst"), sem("s_mmv"), sem("s_mrt"), sem("s_metaln")
        s_zero, s_x2 = sem("s_zero"), sem("s_x2")
        s_ln, s_lnv, s_lnrt, s_h, s_out = sem("s_ln"), sem("s_lnv"), sem("s_lnrt"), sem("s_h"), sem("s_out")

        def colview(w):
            return w.rearrange("(k p) n -> p k n", p=P)

        wqkv, wo = colview(a["moba_w_qkv"][0]), colview(a["moba_w_o"][0])
        wup, wdn = colview(a["ffn_w_up"][0]), a["ffn_w_down"][0].rearrange("(g p) n -> p g n", p=P)
        G_QKV, G_WO, G_FFN = 0, 12, 16
        G_IN = G_FFN + 3 * FJ
        G_DN, G_Z, G_SB, G_GATE, G_BSB, G_BDN, G_OUT = G_IN, G_IN + 6, G_IN + 8, G_IN + 14, G_IN + 22, G_IN + 24, G_IN + 26
        G_END = G_OUT + 4
        win = colview(a["w_in_2"][0])
        IN_Z, IN_BA, IN_SB, IN_GATE = 3 * DN_W, 4 * DN_W, 4 * DN_W + 2 * DN_H, 4 * DN_W + 2 * DN_H + 3 * SB_W
        CH = [(0, P), (P, P), (2 * P, META)]
        LEV = [LEVELS, LEVELS, 4]

        plan = []

        def plan_add(kind, *args):
            plan.append((kind, *args))

        for n in range(G_DN, G_Z):
            plan_add("gran", n)
            if n > G_DN:
                plan_add("silu", n - 1)
            if n == G_DN + 4:
                plan_add("square")
        plan_add("silu", G_Z - 1)
        plan_add("gran", G_Z)
        plan_add("ba")
        plan_add("gran", G_Z + 1)
        plan_add("gran", G_SB)
        for m in range(4):
            plan_add("norm", m)
        plan_add("gran", G_SB + 1)
        for m in range(4, 8):
            plan_add("norm", m)
        plan_add("decays")
        plan_add("gran", G_SB + 2)
        for c in range(3):
            plan_add("D", c)
        plan_add("gran", G_SB + 3)
        for c in range(3):
            plan_add("drow", c)
        for c in (1, 2):
            plan_add("dcol", c)
        plan_add("gran", G_SB + 4)
        for c in range(3):
            plan_add("G", c)
        for c in range(2):
            plan_add("ktr", c)
        plan_add("gran", G_SB + 5)
        for c in range(3):
            plan_add("QK", c)
        for c in range(3):
            plan_add("L0", c)
        for c in range(3):
            plan_add("vtr", c)
        for c in range(3):
            plan_add("sbv", c)
        for s in range(1, LEVELS):
            h = s - 1
            cs = [c for c in range(3) if s < LEV[c]]
            for c in cs:
                plan_add("X", s, c)
            plan_add("Z", h)
            plan_add("gran", G_GATE + h)
            for c in cs:
                plan_add("Y", s, c)
            plan_add("C", h)
            for c in cs:
                if s < LEV[c] - 1:
                    plan_add("T", s, c)
            if h > 0:
                plan_add("V", h - 1)
        plan_add("UV", 0)
        plan_add("gran", G_GATE + 6)
        plan_add("V", 5)
        plan_add("SU", 0)
        plan_add("Z", 6)
        plan_add("O", 0)
        plan_add("KS", 1)
        plan_add("gran", G_GATE + 7)
        plan_add("C", 6)
        plan_add("UV", 1)
        plan_add("Z", 7)
        plan_add("V", 6)
        plan_add("SU", 1)
        plan_add("C", 7)
        plan_add("O", 1)
        plan_add("KS", 2)
        plan_add("V", 7)
        plan_add("UV", 2)
        plan_add("O", 2)
        plan_add("osq")
        plan_add("gran", G_BSB)
        plan_add("orms", 0)
        plan_add("orms", 1)
        plan_add("gran", G_BSB + 1)
        plan_add("sigmoid")
        plan_add("sbmul", 0)
        plan_add("sbmul", 1)
        for n in range(G_BDN, G_END):
            plan_add("gran", n)

        BANKED = ("ba", "norm", "D", "drow", "dcol", "G", "ktr", "QK", "L0", "vtr", "sbv", "X", "Y", "T", "KS", "UV", "O", "SU", "orms")
        TURN = {}
        for st in plan:
            if st[0] in BANKED:
                TURN[st] = (len(TURN) % 2, len(TURN) // 2)
        pm_full, pm_free = [sem(f"pm_full{b}") for b in range(2)], [sem(f"pm_free{b}") for b in range(2)]

        def vacant(eng, *st):
            b, k = TURN[st]
            if k:
                eng.wait_ge(pm_free[b], k)
            return PM[:, b, :]

        def produced(eng, *st):
            b, k = TURN[st]
            eng.wait_ge(pm_full[b], k + 1)
            return PM[:, b, :]

        def consumed(eng, *st):
            b, k = TURN[st]
            eng.wait_ge(pm_free[b], k + 1)

        def full(*st):
            return pm_full[TURN[st][0]]

        def free(*st):
            return pm_free[TURN[st][0]]

        def heads(bank, n=P, w=P):
            return bank.rearrange("p (h n) -> p h n", h=DN_H)[0:n, :, 0:w]

        gT = place("gT", [P, 16, SEQ], PH)
        sbvT = place("sbvT", [P, 4, NT], PH)
        sqb = place("sqb", [P, 8, NT], PH + 4352)
        stick = place("stick", [P, 2, 416], PH + 16384)
        S = place("S", [P, DN_H, DN_D], PH + 22528)
        dnT = place("dnT", [P, 12, NT], PH + 24576)
        osq = place("osq", [P, DN_H, SEQ], PH + 32768)
        zT = place("zT", [P, DN_H, SEQ], PH + 37632)
        sbq = place("sbq", [P, 4, SEQ], PH + 41728)
        sbk = place("sbk", [P, 4, 3 * P], PH + 45824)
        sbv = place("sbv", [P, 3, SB_W], PH + 51968)
        osb_hi = place("osb_hi", [P, 4, SEQ], PH + 58112, F32R)
        osb_lo = place("osb_lo", [P, 4, SEQ], PH + 62208, F32R)
        dE, dA, dN, dX, dT, dU = (place(n, [P, 2, DN_H, P], PH + 66304 + 4096 * i) for i, n in enumerate(("dE", "dA", "dN", "dX", "dT", "dU")))
        odn = place("odn", [P, DN_H, SEQ], PH + 66304 + 4 * 4096)
        odn_hi = place("odn_hi", [P, DN_H, SEQ], PH + 66304 + 4096, F32R)
        odn_lo = place("odn_lo", [P, DN_H, SEQ], PH + 66304 + 2 * 4096, F32R)
        kd = place("kd", [P, 2, DN_H, DN_D], PH + 90880)
        vtok = place("vtok", [P, 3, DN_H, DN_D], PH + 94976)
        cE, cA, cN, cX, cT, cU = (place(n, [P, DN_H, META], PH + 101120 + 256 * i) for i, n in enumerate(("cE", "cA", "cN", "cX", "cT", "cU")))
        cR = place("cR", [P, DN_H, DN_D], PH + 102656)
        cV = place("cV", [P, DN_H, DN_D], PH + 104704)
        mT = place("mT", [P, KD, SEQ], PH + 24576)
        lnrow = place("lnrow", [P, 2, D], PH + 41728)

        def mat(ab, cc, c):
            return ab[:, c, :, :] if c < 2 else cc[0:META, :, :]

        wba = tiny(KD * 8).rearrange("p (k n) -> p k n", k=KD)
        dtb, alog, ea = tiny(4), tiny(4), tiny(4)
        ba = tiny(24).rearrange("p (c n) -> p c n", c=3)
        gx, gn, gy, gu, gp, beta, gdec, edcol = (tiny(12).rearrange("p (c n) -> p c n", c=3) for _ in range(8))
        cdc = tiny(4)

        s_dnaff, s_dntap, s_dnsilu, s_sq, s_l2, s_wba, s_init = (sem(n) for n in ("s_dnaff", "s_dntap", "s_dnsilu", "s_sq", "s_l2", "s_wba", "s_init"))
        s_bx, s_ey, s_dec, s_gm, s_gb, s_eD, s_E, s_cd = (sem(n) for n in ("s_bx", "s_ey", "s_dec", "s_gm", "s_gb", "s_eD", "s_E", "s_cd"))
        s_A, s_N, s_qd, s_U0, s_R, s_z, s_e, s_sp, s_cs, s_arg, s_w, s_pv, s_osbhi, s_osblo = (
            sem(n) for n in ("s_A", "s_N", "s_qd", "s_U0", "s_R", "s_z", "s_e", "s_sp", "s_cs", "s_arg", "s_w", "s_pv", "s_osbhi", "s_osblo"))
        s_sig, s_osq, s_on, s_odnhi, s_odnlo, s_m, s_mhi, s_mlo, s_lnrow = (
            sem(n) for n in ("s_sig", "s_osq", "s_on", "s_odnhi", "s_odnlo", "s_m", "s_mhi", "s_mlo", "s_lnrow"))

        def evacs(n):
            return 2 * (n + 1) if n < G_FFN else 2 * G_FFN + 2 * (n - G_IN + 1)

        def masks():
            return [(0, st[1]) if st[0] == "L0" else (st[1], st[2]) for st in plan if st[0] in ("L0", "X")]
        E_OF_HEAD = [1 + 8 + 3 + 3 * (h + 1) for h in range(SB_H)]
        MASKED = {m: i + 1 for i, m in enumerate(masks())}

        NL = GROUPS + NE
        KH = KD // 2
        slot_at = [PH, PH + 8192, PH + 16384, 46848, 55040, 63232]
        ring = [place(f"expert_raw{i}", [P, GR], at) for i, at in enumerate(slot_at)]
        ehi = [place(f"expert_hi{i}", [P, GR], PH + 50176 + 8192 * i, F32R) for i in range(3)]
        elo = [place(f"expert_lo{i}", [P, GR], PH + 74752 + 8192 * i, F32R) for i in range(3)]
        X_hi = place("X_hi", [P, TT, D], 29440, F32R)
        X_lo = place("X_lo", [P, TT, D], 37632, F32R)
        xw = {WIN: [place(f"xw{i}", [P, KD, 2 * WIN], 29440 + 4096 * i, F32R) for i in range(2)],
              SEQ: [place("xw_wide", [P, KD, 2 * SEQ], 29440, F32R)]}
        pair = place("pair", [P, KD, PAIRS + 2 * SEQ], 71424)
        xf = {WIN: place("xf", [P, KD, WIN], 37632), SEQ: place("xf_wide", [P, KD, SEQ], PH + 24576)}
        yhalf = place("yhalf", [P, 2, KD, WIN], 39680)
        pick1 = place("pick1", [P, TT, PAIRS], PH + 24576)
        pick2 = place("pick2", [P, TT, PAIRS], PH + 28672)
        pick = place("pick", [P, TT, PAIRS], PH + 32768, F32R)
        pickT = place("pickT", [P, PAIRS // P, SEQ], PH + 36864, F32R)
        h1T = place("h1T", [P, KD, SEQ], PH + 99328)
        gusum = place("gusum", [P, 2 * EFF], PH + 99328)
        sg = {WIN: place("sg", [P, 2, WIN], PH + 103424), SEQ: place("sg_wide", [P, 2, SEQ], PH + 99328)}
        hm = {WIN: place("hm", [P, 2, WIN], PH + 103936), SEQ: place("hm_wide", [P, 2, SEQ], PH + 101376)}
        hw2 = {WIN: [place(f"hw2_{i}", [P, 2, 2 * WIN], PH + 104448 + 1024 * i, F32R) for i in range(2)],
               SEQ: [place("hw2_wide", [P, 2, 2 * SEQ], PH + 103424, F32R)] * 2}
        yg_hi = place("yg_hi", [P, PAIRS // P, D], PH, F32R)
        yg_lo = place("yg_lo", [P, PAIRS // P, D], PH + 50176, F32R)
        offi = place("offi", [P, 40], 18496, I32)
        wide = place("wide", [P, 4, TT, NE], 45824)
        M1, M2, M12, slotpos = (wide[:, i, :, :] for i in range(4))

        def grouped(m):
            return m.rearrange("p t (g e) -> p t g e", g=GROUPS)

        def tiny2(n):
            return tiny(TT * n).rearrange("p (t n) -> p t n", t=TT)

        wr = tiny(KD * NL).rearrange("p (k n) -> p k n", k=KD)
        rb = tiny(NL)
        logit, d5, e5, goh, gkey = tiny2(NL), tiny2(5), tiny2(5), tiny2(GROUPS), tiny2(GROUPS)
        sel, esel, ekey, oh1, oh2 = (tiny2(EPG) for _ in range(5))
        gmax, kmax, top1, top2, gsum, w1, w2, pos1, pos2 = (tiny2(1) for _ in range(9))
        prod = tiny(TT * NE).rearrange("p (t g e) -> p t g e", t=TT, g=GROUPS)
        incl, off, cmax, wslot = tiny(NE), tiny(NE), tiny(1), tiny(PAIRS // P)

        s_wr, s_h1T, s_xhi3, s_xlo3, s_logit, s_d5, s_e5, s_M, s_rank, s_off, s_P, s_w12 = (
            sem(n) for n in ("s_wr", "s_h1T", "s_xhi3", "s_xlo3", "s_logit", "s_d5", "s_e5", "s_M", "s_rank", "s_off", "s_P", "s_w12"))
        s_pad, s_xg, s_xga, s_xgv, s_pT, s_pickT = (sem(n) for n in ("s_pad", "s_xg", "s_xga", "s_xgv", "s_pT", "s_pickT"))
        in_ring = [sem(f"in_ring{i}") for i in range(6)]
        s_ehi, s_elo, s_egran, s_winf, s_winhi, s_win, s_gu, s_fold, s_sg, s_hm, s_hmhi, s_hmlo, s_yhalf, s_yg = (
            sem(n) for n in ("s_ehi", "s_elo", "s_egran", "s_winf", "s_winhi", "s_win", "s_gu", "s_fold", "s_sg", "s_hm", "s_hmhi", "s_hmlo", "s_yhalf", "s_yg"))
        s_ygT, s_yghi, s_yglo, s_sum, s_alpha = (sem(n) for n in ("s_ygT", "s_yghi", "s_yglo", "s_sum", "s_alpha"))

        def by_count(eng, narrow, wide):
            eng.wait_ge(s_off, 1)
            fullest = eng.value_load(offi[0:1, NE:NE + 1], min_val=0, max_val=SEQ)
            with eng.If(fullest > WIN):
                wide()
            with eng.Else():
                narrow()

        def gate_up(W, e2):
            if W == WIN:
                both = PG[:, 1, 0:4 * WIN].rearrange("p (j n) -> p j n", j=4)
                return both[:, 0:2, :], both[:, 2:4, :]
            return tuple(PG[:, 2 * e2 + i, :].rearrange("p (f n) -> p f n", f=2) for i in range(2))

        def down_sums(W, e2):
            if W == WIN:
                return PM[:, 2 * e2:2 * e2 + 2, :].rearrange("p b (k n) -> p (b k) n", k=4)
            return PM[:, :, :].rearrange("p b (k n) -> p (b k) n", k=2)

        def in_step(e):
            return 3 * e
        def scores(h):
            return (PM[:, 0, :], PM[:, 1, :], PG[:, 2, :])[h % 3]

        block = ctx.enter_context(nc.Block())

        @block.sync
        def _(sp):
            def load(n, src, it=0):
                if n >= R:
                    sp.wait_ge(s_lo, n - R + 1 + 6 * it)
                sp.dma_start(raw[:, n % R, :].rearrange("p (k n) -> p k n", k=src.shape[1]), src).then_inc(landed[n % R], 16)

            sp.dma_start(X[:, 0, :], a["x"][0, 0:P, :]).then_inc(s_x[0], 16)
            sp.dma_start(rows[:, 0, :], a["norm_mix"][0].partition_broadcast(P)).then_inc(s_row_mix, 16)
            for i in range(12):
                load(G_QKV + i, wqkv[:, :, 256 * i:256 * i + 256])
            for i in range(4):
                load(G_WO + i, wo[:, :, 256 * i:256 * i + 256])
            load(G_FFN, wup[:, :, 0:256])
            load(G_FFN + 1, wup[:, :, FF:FF + 256])
            with sp.Fori(0, (FJ - 1) // 2) as it:
                for u in range(2):
                    n = G_FFN + 2 + 3 * u
                    j = 2 * it + 1 + u
                    load(n, wup[:, :, bass.ds(256 * j, 256)], it)
                    load(n + 1, wup[:, :, bass.ds(FF + 256 * j, 256)], it)
                    load(n + 2, wdn[:, bass.ds(2 * j - 2, 2), :], it)
            load(G_IN - 1, wdn[:, 2 * FJ - 2:2 * FJ, :])
            for i in range(6):
                load(G_DN + i, win[:, :, 256 * i:256 * i + 256])
            for i in range(2):
                load(G_Z + i, win[:, :, IN_Z + 256 * i:IN_Z + 256 * i + 256])
            for i in range(6):
                load(G_SB + i, win[:, :, IN_SB + 256 * i:IN_SB + 256 * i + 256])
            for i in range(8):
                load(G_GATE + i, win[:, :, IN_GATE + 256 * i:IN_GATE + 256 * i + 256])
            for g, name in ((G_BSB, "w_branch_sb_2"), (G_BDN, "w_branch_dn_2")):
                for i in range(2):
                    load(g + i, colview(a[name][0])[:, :, 512 * i:512 * i + 512])
            for i in range(4):
                load(G_OUT + i, colview(a["w_out_2"][0])[:, :, 256 * i:256 * i + 256])
            wexp = [a[f"expert_w_{n}_2"][0].rearrange("g e r c -> (g e) r c") for n in ("gate", "up", "down")]

            def expert_load(e, kind, par):
                dst, done = ring[3 * par + kind], in_ring[3 * par + kind]
                if kind < 2:
                    for i in range(2):
                        src = wexp[i][bass.ds(e, 1), D // 2 * kind:D // 2 * kind + D // 2, :].rearrange("o (k p) n -> p (o k) n", p=P)
                        sp.dma_start(dst[:, :].rearrange("p (k n) -> p k n", k=KH)[:, :, EFF * i:EFF * i + EFF], src).then_inc(done, 16)
                else:
                    src = wexp[2][bass.ds(e, 1), :, :].rearrange("o (f p) n -> p (o f) n", p=P)
                    sp.dma_start(dst[:, :].rearrange("p (f n) -> p f n", f=2), src).then_inc(done, 16)

            sp.wait_ge(s_m, 2)
            expert_load(0, 0, 0)
            expert_load(0, 1, 0)
            sp.wait_ge(s_lo, G_END)
            expert_load(1, 0, 1)
            expert_load(1, 1, 1)
            expert_load(0, 2, 1)
            with sp.Fori(0, NE // 2 - 1) as r:
                for u in range(2):
                    e = 2 * r + 2 + u
                    for kind in range(3):
                        sp.wait_ge(s_elo, in_step(2 * r + u) + kind + 1)
                        expert_load(e if kind < 2 else 2 * r + 1 + u, kind, u)
            sp.wait_ge(s_elo, in_step(NE - 2) + 3)
            expert_load(NE - 1, 2, 0)
            for t in range(TT):
                sp.wait_ge(s_h, 2 * TT + t + 1)
                sp.dma_start(out[P * t:P * t + P, :], X[:, t, :]).then_inc(s_out, 16)
            sp.wait_ge(s_out, 16 * TT)

        @block.gpsimd
        def _(pool):
            def row(slot, vec):
                pool.dma_start(rows[:, slot, :], vec.partition_broadcast(P)).then_inc(s_row[slot], 16)

            flat = a["ffn_conv_w"][0].rearrange("k (t p) -> (k t) p", p=P)
            n3 = 3 * 2 * FT
            pool.dma_start(vrow[:, 0, :], flat[0:P, :]).then_inc(s_vrow, 16)
            pool.dma_start(vrow[0:4, 1, :], flat[P:n3, :]).then_inc(s_vrow, 16)
            pool.dma_start(vrow[4:48, 1, :], a["ffn_conv_b"][0].rearrange("(t p) -> t p", p=P)).then_inc(s_vrow, 16)
            pool.dma_start(vrow[48:64, 1, :], a["b_gate_2"][0].rearrange("b (t p) -> (b t) p", p=P)).then_inc(s_vrow, 16)
            pool.dma_start(vrow[64:112, 1, :], a["dn_conv_w_2"][0].rearrange("k (t p) -> (k t) p", p=P)).then_inc(s_vrow, 16)
            pool.dma_start(vrow[112:113, 1, :], a["dn_norm_g_2"]).then_inc(s_vrow, 16)
            row(1, a["norm_ffn"][0])
            row(2, a["norm_final"])
            row(3, a["ln_emb_g_2"])
            pool.dma_start(MT[:, :], a["meta_tokens_2"]).then_inc(s_meta, 16)
            pool.wait_ge(s_xn, TT)
            row(0, a["ln_emb_b_2"])
            pool.dma_start(wba, win[:, :, IN_BA:IN_BA + 8]).then_inc(s_wba, 16)
            pool.dma_start(dtb, a["dn_dt_bias_2"][0].partition_broadcast(P)).then_inc(s_wba, 16)
            pool.dma_start(alog, a["dn_a_log_2"][0].partition_broadcast(P)).then_inc(s_wba, 16)
            pool.dma_start(wr[:, :, 0:GROUPS], colview(a["router_group_w_2"][0])).then_inc(s_wr, 16)
            for g in range(GROUPS):
                c = slice(GROUPS + EPG * g, GROUPS + EPG * g + EPG)
                pool.dma_start(wr[:, :, c], colview(a["router_expert_w_2"][0, g])).then_inc(s_wr, 16)
            pool.dma_start(rb[:, 0:GROUPS], a["router_group_b_2"][0].partition_broadcast(P)).then_inc(s_wr, 16)
            pool.dma_start(rb[:, GROUPS:NL], a["router_expert_b_2"][0].rearrange("g e -> (g e)").partition_broadcast(P)).then_inc(s_wr, 16)
            pool.wait_ge(s_xlo, 13)
            pool.memset(sbk[:, :, NT:3 * P], 0.0).then_inc(s_init, 1)
            pool.memset(sbv[:, 2, :], 0.0).then_inc(s_init, 1)
            pool.memset(ba, 0.0).then_inc(s_init, 1)

            def bc(ap, n, w):
                return ap.unsqueeze(1).to_broadcast([n, DN_H, w])

            pool.wait_ge(s_cst2, 16)
            for st in plan:
                if st[0] == "D":
                    c = st[1]
                    n = CH[c][1]
                    pool.wait_ge(s_eD, c + 1)
                    e = mat(dE, cE, c)
                    pool.tensor_tensor(e, e, bc(con("le")[0:n, 0:n], n, n), ALU.mult).then_inc(s_E, 1)
                elif st[0] in ("L0", "X"):
                    s, c = (0, st[1]) if st[0] == "L0" else (st[1], st[2])
                    n = CH[c][1]
                    pool.wait_ge(s_A, c + 1)
                    if s >= 2:
                        produced(pool, "X", s - 1, c)
                    elif s == 1:
                        pool.wait_ge(s_U0, c + 1)
                    m = con("level")[0:n, P * s:P * s + n]
                    pool.tensor_tensor(mat(dN, cN, c), mat(dA, cA, c), bc(m, n, n), ALU.mult).then_inc(s_N, 1)
            pool.wait_ge(s_w, SB_H)
            pool.wait_ge(s_pv, SB_H)
            for i, name in enumerate(("ln1_g_2", "ln1_b_2")):
                pool.dma_start(lnrow[:, i, :], a[name][0].partition_broadcast(P)).then_inc(s_lnrow, 16)
            for i, n in enumerate(("ln2_g_2", "ln2_b_2")):
                if i == 0:
                    pool.wait_ge(s_h, 2 * TT)
                pool.dma_start(lnrow[:, i, :], a[n][0].partition_broadcast(P)).then_inc(s_lnrow, 16)
            pool.wait_ge(s_gran, G_END)
            pool.memset(pair[:, :, PAIRS + SEQ:PAIRS + 2 * SEQ], 0.0).then_inc(s_pad, 1)
            pool.wait_ge(s_xga, KD // 2)
            pool.wait_ge(s_xgv, KD // 2)
            pool.wait_ge(s_pad, 1)

            def moe(W):
                def window(e, buf):
                    at = pool.value_load(offi[0:1, bass.ds(e, 1)], min_val=0, max_val=PAIRS)
                    pool.tensor_copy(xf[W][:, :, :], pair[:, :, bass.ds(at + SEQ, W)]).then_inc(s_winf, 1)
                    pool.wait_ge(s_winhi, e + 1)
                    x = xw[W][buf]
                    pool.tensor_tensor(x[:, :, W:2 * W], xf[W][:, :, :], x[:, :, 0:W].bitcast(F32), ALU.subtract).then_inc(s_win, 1)
                    pool.wait_ge(s_win, e + 1)

                if W == SEQ:
                    pool.wait_ge(s_pickT, 2)
                with pool.Fori(0, NE // 2) as r:
                    for u in range(2):
                        window(2 * r + u, u % len(xw[W]))

            by_count(pool, lambda: moe(WIN), lambda: moe(SEQ))

        @block.scalar
        def _(act):
            act.dma_start(X[:, 1, :], a["x"][0, P:2 * P, :]).then_inc(s_x[1], 16)
            act.dma_start(cst[:, 0:CONST_FIRST], a["consts"][:, 0:CONST_FIRST]).then_inc(s_cst, 16)

            def hi_part(n, it=0):
                act.wait_ge(landed[n % R], 16 * (n // R + 1) + 32 * it)
                if n >= H:
                    act.wait_ge(s_gran, n - H + 1 + 6 * it)
                act.activation(whi[:, n % H, :], raw[:, n % R, :], ACT.Copy).then_inc(s_hi, 1)

            def norm_sq():
                for t in range(TT):
                    act.wait_ge(s_x[t], 16)
                    act.activation(XN[:, t, :], X[:, t, :], ACT.Square, accum_out=ss[:, t:t + 1]).then_inc(s_ss, 1)
                act.wait_ge(s_cst, 16)

            def norm_sqrt(q):
                for t in range(TT):
                    i = 2 * q + t
                    act.wait_ge(s_ss, i + 1)
                    act.activation(rt[:, i:i + 1], ss[:, i:i + 1], ACT.Sqrt, scale=1.0 / D, bias=con("eps6")).then_inc(s_rt, 1)

            def norm_hi(q):
                for t in range(TT):
                    for f in range(2):
                        act.wait_ge(s_xT, 4 * q + 2 * t + f + 1)
                        act.activation(hT_hi[:, 4 * f:4 * f + 4, P * t:P * t + P],
                                       PM[:, 2 * t + f, :].rearrange("p (k n) -> p k n", k=4), ACT.Copy).then_inc(s_xhi, 1)

            norm_sq()
            norm_sqrt(0)
            hi_part(0)
            act.dma_start(cst[:, CONST_FIRST:], a["consts"][:, CONST_FIRST:]).then_inc(s_cst2, 16)
            norm_hi(0)
            for n in range(12):
                hi_part(n + 1)
                act.wait_ge(s_gran, n + 1)
                src = PG[:, 2 * (n % 2), 0:256]
                if n < 4:
                    act.activation(qT[:, 2 * n, :], src, ACT.Copy, scale=A_DH ** -0.5).then_inc(s_ev, 1)
                elif n < 8:
                    act.activation(kT[:, 2 * n - 8, :], src, ACT.Copy).then_inc(s_ev, 1)
                else:
                    act.activation(vv[:, 0, 256 * (n - 8):256 * (n - 8) + 256], src, ACT.Copy).then_inc(s_ev, 1)
            for i in range(A_HEADS + 3):
                if i < A_HEADS:
                    h = i
                    act.wait_ge(s_nmx, h + 1)
                    for t in range(2):
                        c = (0, P) if t == 0 else (P, 3 * P)
                        b = 2 * (h % 3) + t
                        act.activation(prob[:, h % 3, c[0]:c[1]], prob[:, h % 3, c[0]:c[1]], ACT.Exp, bias=nmx[:, b:b + 1],
                                       accum_out=psum_[:, b:b + 1]).then_inc(s_exp, 1)
                if 2 <= i < A_HEADS + 2:
                    h = i - 2
                    act.wait_ge(s_PT, h + 1)
                    if h >= 2:
                        act.wait_ge(s_PV, h - 1)
                    act.activation(probT[:, h % 2, :], PM[:, 2 + h % 2, 0:3 * P], ACT.Copy).then_inc(s_probT, 1)
                if i >= 4 and i % 2 == 0:
                    hp = (i - 4) // 2
                    act.wait_ge(s_PV, 2 * hp + 2)
                    act.activation(oT_hi[:, hp, :], PG[:, hp % 2, 0:SEQ], ACT.Copy).then_inc(s_oThi, 1)
            def ss_block(n):
                act.wait_ge(s_ev, 2 * n + 2)
                for t in range(TT):
                    c = slice(256 * (n - G_WO), 256 * (n - G_WO) + 256)
                    act.activation(XN[:, t, c], X[:, t, c], ACT.Square, accum_out=ssq[:, t, n - G_WO:n - G_WO + 1]).then_inc(s_ssq, 1)

            for n in range(G_WO, G_FFN):
                hi_part(n + 1)
                if n == G_WO:
                    act.wait_ge(s_mmv, 1)
                    act.activation(lnrt[0:META, 2:3], lnmv[0:META, 5:6], ACT.Sqrt, bias=con("eps5", rows=META)).then_inc(s_mrt, 1)
                if n > G_WO:
                    ss_block(n - 1)
            ss_block(G_FFN - 1)
            norm_sqrt(1)
            norm_hi(1)
            act.wait_ge(s_colsT, 1)
            act.activation(cols[:, 0:P + 113], PG[:, 2, 0:P + 113], ACT.Copy).then_inc(s_cols, 1)
            act.wait_ge(s_cols, 1)

            def col(i, n=1):
                return cols[:, bass.ds(i, n)]

            def affine(j, dst, bank, tile0, s_done, par, cnt, gran):
                act.wait_ge(s_gran, gran)
                for f in range(2):
                    act.activation(dst[:, par, f, :], PG[:, bank + f, 0:SEQ], ACT.Identity,
                                   scale=col(2 * 2 * FT + tile0 + f), bias=col(3 * 2 * FT + tile0 + f)).then_inc(s_done, 1)

            def ffn_step(n, j, par, it, first=False, last=False):
                hi_part(n + 1, it)
                affine(j, cgate, 0, 2 * j, s_gaff, par, None, n + 1 + 6 * it)
                hi_part(n + 2, it)
                act.wait_ge(s_gconv, j + 1)
                act.activation(cgate[:, par, :, :], cgate[:, par, :, :], ACT.Silu).then_inc(s_gsilu, 1)
                affine(j, cup, 2, FT + 2 * j, s_uaff, par, None, n + 2 + 6 * it)
                if not first:
                    hi_part(n + 3, it)
                act.wait_ge(s_hid, j + 1)
                act.activation(hid_hi[:, par, :, :], hid[:, par, :, :], ACT.Copy).then_inc(s_hidhi, 1)

            ffn_step(G_FFN, 0, 0, 0, first=True)
            with act.Fori(0, (FJ - 1) // 2) as it:
                for u in range(2):
                    ffn_step(G_FFN + 2 + 3 * u, 2 * it + 1 + u, (1 + u) % 2, it)

            for t in range(TT):
                act.wait_ge(s_x2, t + 1)
                act.activation(scratch[:, t, :], X[:, t, :], ACT.Square, accum_out=ss[:, 4 + t:5 + t]).then_inc(s_ss, 1)
                act.wait_ge(s_nmu, t + 1)
                act.activation(scratch2[:, t, :], XN[:, t, :], ACT.Square, bias=nmu[:, t:t + 1], accum_out=vs[:, t:t + 1]).then_inc(s_vs, 1)
                act.wait_ge(s_vs, t + 1)
                act.wait_ge(s_ve, t + 1)
                act.activation(lnrt[:, t:t + 1], vs[:, t:t + 1], ACT.Sqrt, scale=1.0 / D, bias=ve[:, t:t + 1]).then_inc(s_lnrt, 1)

            def ln_hi(dst, src, i):
                act.wait_ge(s_xT, i + 1)
                act.activation(dst, src, ACT.Copy).then_inc(s_xhi, 1)

            hi_part(G_DN)
            ln_hi(hT_hi[:, :, 0:META], PG[:, 0, 0:P].rearrange("p (k n) -> p k n", k=KD), 8)
            for t in range(TT):
                for f in range(2):
                    c = META + P * t
                    ln_hi(hT_hi[:, 4 * f:4 * f + 4, c:c + P], PM[:, 2 * t + f, :].rearrange("p (k n) -> p k n", k=4), 9 + 2 * t + f)

            achain = [0]

            def astep(ins):
                achain[0] += 1
                ins.then_inc(s_e, 1)
                act.wait_ge(s_e, achain[0])

            def copy_out(dst, src, *st):
                act.activation(dst, src, ACT.Copy).then_inc(free(*st), 1)

            for st in plan:
                kind = st[0]
                if kind == "gran":
                    n = st[1]
                    if n + 1 < G_END:
                        hi_part(n + 1)
                    act.wait_ge(s_gran, n + 1)
                    b = 2 * (n % 2)
                    if n < G_Z:
                        for f in range(2):
                            m = 2 * (n - G_DN) + f
                            act.activation(dnT[:, m, :], PG[:, b + f, 0:NT], ACT.Copy, scale=col(192 + 36 + m)).then_inc(s_dnaff, 1)
                    elif n < G_SB:
                        m = 2 * (n - G_Z)
                        act.activation(zT[:, m:m + 2, :], PG[:, b:b + 2, 0:SEQ], ACT.Silu).then_inc(s_ev, 2)
                    elif n < G_GATE:
                        i, m = divmod(n - G_SB, 2)
                        if i == 0:
                            act.activation(sbq[:, 2 * m, :], PG[:, b, 0:SEQ], ACT.Copy, scale=SB_DH ** -0.5).then_inc(s_ev, 1)
                        elif i == 1:
                            act.activation(sbk[:, 2 * m, 0:NT], PG[:, b, 0:NT], ACT.Copy).then_inc(s_ev, 1)
                        else:
                            act.activation(sbvT[:, 2 * m, :], PG[:, b, 0:NT], ACT.Copy).then_inc(s_ev, 1)
                    elif n < G_BSB:
                        for f in range(2):
                            m = 2 * (n - G_GATE) + f
                            act.activation(gT[:, m, :], PG[:, b + f, 0:SEQ], ACT.Identity, bias=col(176 + m)).then_inc(s_ev, 1)
                    elif G_BDN <= n < G_OUT:
                        i = n - G_BDN
                        act.wait_ge(s_m, i + 1)
                        act.activation(hT_hi[:, 4 * i:4 * i + 4, 0:SEQ], mT[:, 4 * i:4 * i + 4, :], ACT.Copy).then_inc(s_mhi, 1)
                elif kind == "silu":
                    m = 2 * (st[1] - G_DN)
                    act.wait_ge(s_ev, evacs(st[1]))
                    act.activation(dnT[:, m:m + 2, :], dnT[:, m:m + 2, :], ACT.Silu).then_inc(s_dnsilu, 1)
                elif kind == "square":
                    act.wait_ge(s_dnsilu, 4)
                    for i in range(2):
                        act.activation(sqb[:, 4 * i:4 * i + 4, :], dnT[:, 4 * i:4 * i + 4, :], ACT.Square).then_inc(s_sq, 1)
                elif kind == "ba":
                    act.wait_ge(s_init, 3)
                    bank = produced(act, *st)
                    astep(act.activation(ba[:, 0:2, :], bank[:, 0:16].rearrange("p (c n) -> p c n", c=2), ACT.Copy))
                    copy_out(ba[0:META, 2, :], bank[0:META, 16:24], *st)
                elif kind == "norm":
                    if st[1] == 0:
                        act.preload_act_table_set("natural_log_exp_and_others")
                    bank = produced(act, *st)
                    r = sqb[:, st[1], :]
                    astep(act.activation(r, bank[:, 0:NT], ACT.Ln, bias=con("eps6")))
                    act.activation(r, r, ACT.Exp, scale=-0.5).then_inc(free(*st), 1)
                elif kind == "decays":
                    consumed(act, "ba")
                    act.wait_ge(s_wba, 48)
                    act.wait_ge(s_bx, 1)
                    act.activation(gy, gn, ACT.Exp).then_inc(s_ey, 1)
                    act.activation(beta, ba[:, :, 0:4], ACT.Exp, scale=-1.0).then_inc(s_ey, 1)
                    act.activation(ea, alog, ACT.Exp).then_inc(s_ey, 1)
                elif kind == "D":
                    c = st[1]
                    n = CH[c][1]
                    bank = produced(act, *st)
                    astep(act.activation(mat(dE, cE, c), heads(bank, n, n), ACT.Exp))
                    act.sem_inc(s_eD, 1)
                    act.sem_inc(free(*st), 1)
                elif kind == "drow":
                    c = st[1]
                    n = CH[c][1]
                    bank = produced(act, *st)
                    act.activation(dT[:, c, :, :] if c < 2 else cT[:, :, :], heads(bank, P, n), ACT.Exp).then_inc(free(*st), 1)
                elif kind == "dcol":
                    c = st[1]
                    n = CH[c][1]
                    bank = produced(act, *st)
                    act.activation(edcol[0:n, c, :], bank[0:n, 0:DN_H], ACT.Exp).then_inc(free(*st), 1)
                elif kind == "vtr":
                    c = st[1]
                    n = CH[c][1]
                    copy_out(vtok[0:n, c, :, :], heads(produced(act, *st), n), *st)
                elif kind == "sbv":
                    c = st[1]
                    n = CH[c][1]
                    copy_out(sbv[0:n, c, :], produced(act, *st)[0:n, :], *st)
                elif kind == "L0":
                    c = st[1]
                    n = CH[c][1]
                    act.wait_ge(s_qd, 3)
                    copy_out(mat(dT, cT, c), heads(produced(act, *st), n, n), *st)
                elif kind in ("X", "T"):
                    c = st[2]
                    n = CH[c][1]
                    dst = mat(dX, cX, c) if kind == "X" else mat(dT, cT, c)
                    copy_out(dst, heads(produced(act, *st), n, n), *st)
                elif kind == "O":
                    c = st[1]
                    bank = heads(produced(act, *st), P, CH[c][1])
                    if c == 0:
                        copy_out(odn[:, :, 0:P - META], bank[:, :, META:P], *st)
                    elif c == 1:
                        copy_out(odn[:, :, P - META:2 * P - META], bank, *st)
                    else:
                        copy_out(odn[:, :, SEQ - META:SEQ], bank, *st)
                elif kind == "Z":
                    h = st[1]
                    act.wait_ge(s_z, h + 1)
                    e = stick[:, h % 2, :]
                    if h >= 2:
                        act.wait_ge(s_pv, h - 1)
                    astep(act.activation(e, PM[:, 2 + h % 2, 0:416], ACT.Abs))
                    astep(act.activation(e, e, ACT.Exp, scale=-1.0))
                    astep(act.activation(e, e, ACT.Ln, bias=1.0))
                elif kind == "C":
                    h = st[1]
                    act.wait_ge(s_arg, h + 1)
                    e = stick[:, h % 2, :]
                    act.activation(e, e, ACT.Exp).then_inc(s_w, 1)
                elif kind == "V":
                    h = st[1]
                    b = SB_DH * (h % 2)
                    act.wait_ge(s_pv, h + 1)
                    act.activation(osb_hi[b:b + SB_DH, h // 2, :], PM[b:b + SB_DH, 2 + h % 2, 0:SEQ], ACT.Copy).then_inc(s_osbhi, 1)
                elif kind == "sigmoid":
                    act.wait_ge(s_ev, evacs(G_BSB - 1))
                    for i in (1, 0):
                        act.activation(gT[:, 8 * i:8 * i + 8, :], gT[:, 8 * i:8 * i + 8, :], ACT.Sigmoid).then_inc(s_sig, 1)
                elif kind == "osq":
                    consumed(act, "O", 2)
                    act.activation(osq[:, :, :], odn[:, :, :], ACT.Square).then_inc(s_osq, 1)
                elif kind == "orms":
                    i = st[1]
                    bank = produced(act, *st)
                    r = osq[:, 2 * i:2 * i + 2, :]
                    astep(act.activation(r, bank.rearrange("p (h n) -> p h n", h=2), ACT.Ln, scale=1.0 / DN_D, bias=con("eps6")))
                    act.activation(r, r, ACT.Exp, scale=-0.5).then_inc(free(*st), 1)
                    if i == 1:
                        act.wait_ge(s_on, 2)
                        act.activation(odn_hi[:, :, :], odn[:, :, :], ACT.Copy).then_inc(s_odnhi, 1)
            for t in range(TT):
                act.wait_ge(s_lnv, t + 1)
                act.activation(lnrt[:, t:t + 1], lnmv[:, 2 * t + 1:2 * t + 2], ACT.Sqrt, bias=con("eps5")).then_inc(s_lnrt, 1)
            for t in range(TT):
                act.wait_ge(s_h, TT + t + 1)
                act.activation(X_hi[:, t, :], X[:, t, :], ACT.Copy).then_inc(s_xhi3, 1)
                act.wait_ge(s_xT, 13 + 2 * t + 1)
                act.activation(h1T[:, 0:4, P * t:P * t + P], PM[:, 2 * t, :].rearrange("p (k n) -> p k n", k=4), ACT.Copy).then_inc(s_h1T, 1)
            def expert_hi(E, kind, par, count):
                act.wait_ge(in_ring[3 * par + kind], (16 if kind == 2 else 32) * count)
                if not (isinstance(E, int) and E == 0):
                    act.wait_ge(s_egran, in_step(E - 1) + kind + 1)
                else:
                    act.wait_ge(s_gran, G_END)
                act.activation(ehi[kind][:, :], ring[3 * par + kind][:, :], ACT.Copy).then_inc(s_ehi, 2 if isinstance(E, int) and E == 0 and kind == 1 else 1)

            expert_hi(0, 0, 0, 1)
            expert_hi(0, 1, 0, 1)
            act.wait_ge(s_d5, 1)
            act.activation(e5, d5, ACT.Exp).then_inc(s_e5, 1)
            for k in range(0, KD, 2):
                act.wait_ge(s_xg, k + 1)
                act.activation(pair[:, k, SEQ:SEQ + PAIRS], PM[:, k % 4, :], ACT.Copy).then_inc(s_xga, 1)
            def moe(W):
                def window_hi(e, par):
                    act.wait_ge(s_winf, e + 1)
                    act.activation(xw[W][par % len(xw[W])][:, :, 0:W], xf[W][:, :, :], ACT.Copy).then_inc(s_winhi, 1)

                def result_half(e, e2):
                    if W == WIN:
                        act.wait_ge(s_egran, in_step(e + 1) + 3 if not (isinstance(e, int) and e == NE - 1) else in_step(NE) + 1)
                        act.activation(yhalf[:, e2, :, :], down_sums(W, e2)[:, :, 0:W], ACT.Copy).then_inc(s_yhalf, 1)

                def step_of(e, u, r):
                    more = not (isinstance(e, int) and e == NE - 1)
                    if more:
                        expert_hi(e + 1, 0, u, r + 1)
                    act.wait_ge(s_egran, in_step(e) + 2)
                    if W == WIN:
                        act.activation(gusum[:, :], PG[:, 0, :], ACT.Copy).then_inc(s_gu, 1)
                    if more:
                        window_hi(e + 1, u)
                        expert_hi(e + 1, 1, u, r + 1)
                    else:
                        act.wait_ge(in_ring[2], 16 * r)
                        act.activation(ehi[0][:, :], ring[2][:, :], ACT.Copy).then_inc(s_ehi, 1)
                    if W == WIN:
                        if more:
                            expert_hi(e + 1, 2, u, r + (1 if u else 0))
                        act.wait_ge(s_fold, e + 1)
                    act.activation(sg[W][:, :, :], gate_up(W, 1 - u)[0], ACT.Silu).then_inc(s_sg, 1)
                    if W == SEQ:
                        if more:
                            expert_hi(e + 1, 2, u, r + (1 if u else 0))
                        if not (isinstance(e, int) and e == 0):
                            act.wait_ge(s_egran, in_step(e) + 3)
                    act.wait_ge(s_hm, e + 1)
                    act.activation(hw2[W][1 - u][:, :, 0:W], hm[W][:, :, :], ACT.Copy).then_inc(s_hmhi, 1)
                    if not (isinstance(e, int) and e == 0):
                        result_half(e - 1, u)

                if W == WIN:
                    window_hi(0, 0)
                act.wait_ge(s_pT, 1)
                act.activation(pickT[:, :, :].rearrange("p (b j) n -> p b (j n)", b=2), PG[:, 2:4, :], ACT.Copy).then_inc(s_pickT, 1)
                act.activation(wslot, PG[:, 1, 0:PAIRS // P], ACT.Copy).then_inc(s_pickT, 1)
                if W == SEQ:
                    window_hi(0, 0)
                step_of(0, 1, 0)
                with act.Fori(0, NE // 2 - 1) as r:
                    for u in range(2):
                        step_of(2 * r + 1 + u, u, r + 1)
                step_of(NE - 1, 0, NE // 2)
                result_half(NE - 1, 1)

            by_count(act, lambda: moe(WIN), lambda: moe(SEQ))
            act.wait_ge(s_pickT, 2)
            act.activation(X[:, :, :], X[:, :, :], ACT.Copy, scale=ALPHA).then_inc(s_alpha, 1)
            for j in range(PAIRS // P):
                act.wait_ge(s_ygT, j + 1)
                src = (PM if j < 2 else PG)[:, 2 * (j % 2):2 * (j % 2) + 2, :]
                act.activation(yg_hi[:, j, :].rearrange("p (b n) -> p b n", b=2), src, ACT.Copy, scale=wslot[:, j:j + 1]).then_inc(s_yghi, 1)
            for t in range(TT):
                act.wait_ge(s_nmu, TT + t + 1)
                act.activation(pair[:, t, :], X[:, t, :], ACT.Square, bias=nmu[:, t:t + 1], accum_out=vs[:, t:t + 1]).then_inc(s_vs, 1)
                act.wait_ge(s_vs, TT + t + 1)
                act.activation(lnrt[:, t:t + 1], vs[:, t:t + 1], ACT.Sqrt, scale=1.0 / D, bias=con("eps5")).then_inc(s_lnrt, 1)
        @block.vector
        def _(dve):
            seq = [0]
            s_dve = s_rs

            def step(ins):
                seq[0] += 1
                ins.then_inc(s_dve, 1)
                dve.wait_ge(s_dve, seq[0])

            def lo_part(n, it=0):
                dve.wait_ge(s_hi, n + 1 + 6 * it)
                dve.tensor_tensor(wlo[:, n % H, :], raw[:, n % R, :], whi[:, n % H, :].bitcast(F32), ALU.subtract).then_inc(s_lo, 1)

            def norm_apply(q):
                for t in range(TT):
                    i = 2 * q + t
                    dve.wait_ge(s_rt, i + 1)
                    step(dve.reciprocal(rs[:, i:i + 1], rt[:, i:i + 1]))
                    if t == 0:
                        dve.wait_ge(s_row_mix if q == 0 else s_row[q], 16)
                    dve.scalar_tensor_tensor(XN[:, t, :], X[:, t, :], rs[:, i:i + 1], rows[:, q, :], ALU.mult, ALU.mult).then_inc(s_xn, 1)

            def norm_lo(q):
                for t in range(TT):
                    for f in range(2):
                        dve.wait_ge(s_xhi, 4 * q + 2 * t + f + 1)
                        c = slice(P * t, P * t + P)
                        dve.tensor_tensor(hT_lo[:, 4 * f:4 * f + 4, c], PM[:, 2 * t + f, :].rearrange("p (k n) -> p k n", k=4),
                                          hT_hi[:, 4 * f:4 * f + 4, c].bitcast(F32), ALU.subtract).then_inc(s_xlo, 1)

            dve.memset(zero[:, :], 0.0).then_inc(s_zero, 1)
            norm_apply(0)
            lo_part(0)
            norm_lo(0)
            for n in range(12):
                lo_part(n + 1)
                dve.wait_ge(s_gran, n + 1)
                src = PG[:, 2 * (n % 2) + 1, 0:256]
                if n < 4:
                    dve.tensor_scalar(qT[:, 2 * n + 1, :], src, A_DH ** -0.5, None, ALU.mult).then_inc(s_ev, 1)
                elif n < 8:
                    dve.tensor_copy(kT[:, 2 * n - 7, :], src).then_inc(s_ev, 1)
                else:
                    dve.tensor_copy(vv[:, 1, 256 * (n - 8):256 * (n - 8) + 256], src).then_inc(s_ev, 1)
            dve.wait_ge(s_cst2, 16)
            for i in range(A_HEADS + 3):
                if i < A_HEADS:
                    h = i
                    dve.wait_ge(s_S, h + 1)
                    if h >= 3:
                        dve.wait_ge(s_PT, h - 2)
                    for t in range(2):
                        c = (0, P) if t == 0 else (P, 3 * P)
                        b = 2 * (h % 3) + t
                        dve.tensor_tensor_reduce(prob[:, h % 3, c[0]:c[1]], scores(h)[:, c[0]:c[1]], con("causal")[:, c[0]:c[1]],
                                                 1.0, -3e38, ALU.add, ALU.max, mx[:, b:b + 1]).then_inc(s_mx, 1)
                    dve.wait_ge(s_mx, 2 * h + 2)
                    if h >= 3:
                        dve.wait_ge(s_exp, 2 * h - 4)
                    b = slice(2 * (h % 3), 2 * (h % 3) + 2)
                    dve.tensor_scalar(nmx[:, b], mx[:, b], -1.0, None, ALU.mult).then_inc(s_nmx, 1)
                if 1 <= i <= A_HEADS:
                    h = i - 1
                    dve.wait_ge(s_exp, 2 * h + 2)
                    b = slice(2 * (h % 3), 2 * (h % 3) + 2)
                    step(dve.reciprocal(rinv[:, b], psum_[:, b]))
                    for t in range(2):
                        c = (0, P) if t == 0 else (P, 3 * P)
                        dve.tensor_scalar(prob[:, h % 3, c[0]:c[1]], prob[:, h % 3, c[0]:c[1]],
                                          rinv[:, b.start + t:b.start + t + 1], None, ALU.mult).then_inc(s_prob, 1)
                if i >= 4 and i % 2 == 0:
                    hp = (i - 4) // 2
                    dve.wait_ge(s_oThi, hp + 1)
                    dve.tensor_tensor(oT_lo[:, hp, :], PG[:, hp % 2, 0:SEQ], oT_hi[:, hp, :].bitcast(F32), ALU.subtract).then_inc(s_oTlo, 1)
            dve.wait_ge(s_meta, 16)
            for f in range(2):
                dve.bn_stats(lnst[0:META, 24 + 6 * f:30 + 6 * f], MT[:, 512 * f:512 * f + 512]).then_inc(s_mst, 1)
            dve.wait_ge(s_mst, 2)
            dve.bn_aggr(lnmv[0:META, 4:6], lnst[0:META, 24:36]).then_inc(s_mmv, 1)
            for n in range(G_WO, G_FFN):
                lo_part(n + 1)
                if n == G_WO + 1:
                    dve.wait_ge(s_mrt, 1)
                    step(dve.reciprocal(lnrs[0:META, 2:3], lnrt[0:META, 2:3]))
                    step(dve.tensor_scalar(MT[:, :], MT[:, :], lnmv[0:META, 4:5], lnrs[0:META, 2:3], ALU.subtract, ALU.mult))
                    dve.wait_ge(s_row[3], 16)
                    step(dve.tensor_tensor(MT[:, :], MT[:, :], rows[0:META, 3, :], ALU.mult))
                    dve.wait_ge(s_row[0], 16)
                    dve.tensor_tensor(MT[:, :], MT[:, :], rows[0:META, 0, :], ALU.add).then_inc(s_metaln, 1)
                dve.wait_ge(s_gran, n + 1)
                c = slice(256 * (n - G_WO), 256 * (n - G_WO) + 256)
                dve.tensor_tensor(X[:, :, c], X[:, :, c], PG[:, 2 * (n % 2):2 * (n % 2) + 2, 0:256], ALU.add).then_inc(s_ev, 2)
            dve.wait_ge(s_ssq, 4 * TT)
            for t in range(TT):
                dve.tensor_reduce(ss[:, 2 + t:3 + t], ssq[:, t, :], AX.X, ALU.add).then_inc(s_ss, 1)
            norm_apply(1)
            norm_lo(1)
            dve.wait_ge(s_cols, 1)

            def col(i, n=1):
                return cols[:, bass.ds(i, n)]

            def taps(dst, par, bank, tile0, s_aff, s_tap, s_conv, j):
                for back in (1, 2):
                    for f in range(2):
                        if back == 1:
                            dve.wait_ge(s_aff, 2 * j + f + 1)
                        elif f == 0:
                            dve.wait_ge(s_tap, 2 * j + 2)
                        ins = dve.scalar_tensor_tensor(dst[:, par, f, back:SEQ], PG[:, bank + f, 0:SEQ - back],
                                                       col((2 - back) * 2 * FT + tile0 + f), dst[:, par, f, back:SEQ],
                                                       ALU.mult, ALU.add)
                        if back == 1:
                            ins.then_inc(s_tap, 1)
                        elif f == 1:
                            ins.then_inc(s_conv, 1)

            def ffn_step(n, j, par, it, first=False):
                lo_part(n + 1, it)
                taps(cgate, par, 0, 2 * j, s_gaff, s_gtap, s_gconv, j)
                lo_part(n + 2, it)
                taps(cup, par, 2, FT + 2 * j, s_uaff, s_utap, s_uconv, j)
                if not first:
                    lo_part(n + 3, it)
                dve.wait_ge(s_gsilu, j + 1)
                dve.wait_ge(s_uconv, j + 1)
                dve.tensor_tensor(hid[:, par, :, :], cgate[:, par, :, :], cup[:, par, :, :], ALU.mult).then_inc(s_hid, 1)
                dve.wait_ge(s_hidhi, j + 1)
                dve.tensor_tensor(hid_lo[:, par, :, :], hid[:, par, :, :], hid_hi[:, par, :, :].bitcast(F32), ALU.subtract).then_inc(s_hidlo, 1)

            ffn_step(G_FFN, 0, 0, 0, first=True)
            with dve.Fori(0, (FJ - 1) // 2) as it:
                for u in range(2):
                    ffn_step(G_FFN + 2 + 3 * u, 2 * it + 1 + u, (1 + u) % 2, it)

            for t in range(TT):
                if t == 0:
                    dve.wait_ge(s_ffn, 1)
                else:
                    dve.wait_ge(s_gran, G_IN)
                dve.tensor_tensor(X[:, t, :].rearrange("p (h n) -> p h n", h=2), X[:, t, :].rearrange("p (h n) -> p h n", h=2),
                                  PM[:, 2 * t:2 * t + 2, :], ALU.add).then_inc(s_x2, 1)
                dve.wait_ge(s_x2, t + 1)
                dve.wait_ge(s_row[2], 16)
                step(dve.tensor_tensor_reduce(XN[:, t, :], X[:, t, :], rows[:, 2, :], 1.0, 0.0, ALU.mult, ALU.add, zsum[:, t:t + 1]))
                dve.tensor_scalar(nmu[:, t:t + 1], zsum[:, t:t + 1], -1.0 / D, None, ALU.mult).then_inc(s_nmu, 1)
            for t in range(TT):
                dve.wait_ge(s_ss, 4 + t + 1)
                dve.tensor_scalar(ve[:, t:t + 1], ss[:, 4 + t:5 + t], LN_EPS / D, LN_EPS * RMS_EPS, ALU.mult, ALU.add).then_inc(s_ve, 1)
                dve.wait_ge(s_row[3], 16)
                dve.wait_ge(s_vs, t + 1)
                step(dve.scalar_tensor_tensor(XN[:, t, :], XN[:, t, :], nmu[:, t:t + 1], rows[:, 3, :], ALU.add, ALU.mult))
                dve.wait_ge(s_lnrt, t + 1)
                step(dve.reciprocal(lnrs[:, t:t + 1], lnrt[:, t:t + 1]))
                dve.wait_ge(s_row[0], 16)
                dve.scalar_tensor_tensor(X[:, t, :], XN[:, t, :], lnrs[:, t:t + 1], rows[:, 0, :], ALU.mult, ALU.add).then_inc(s_h, 1)

            lo_part(G_DN)

            def ln_lo(dst, src, i):
                dve.wait_ge(s_xhi, i + 1)
                dve.tensor_tensor(dst[0], src, dst[1].bitcast(F32), ALU.subtract).then_inc(s_xlo, 1)

            c = slice(0, META)
            ln_lo((hT_lo[:, :, c], hT_hi[:, :, c]), PG[:, 0, 0:P].rearrange("p (k n) -> p k n", k=KD), 8)
            for t in range(TT):
                for f in range(2):
                    c = slice(META + P * t, META + P * t + P)
                    ln_lo((hT_lo[:, 4 * f:4 * f + 4, c], hT_hi[:, 4 * f:4 * f + 4, c]),
                          PM[:, 2 * t + f, :].rearrange("p (k n) -> p k n", k=4), 9 + 2 * t + f)

            def hbc(ap, n, w):
                return ap.unsqueeze(2).to_broadcast([n, DN_H, w])

            def bc(ap, n, w):
                return ap.unsqueeze(1).to_broadcast([n, DN_H, w])

            for st in plan:
                kind = st[0]
                if kind == "gran":
                    n = st[1]
                    if n + 1 < G_END:
                        lo_part(n + 1)
                    b = 2 * (n % 2)
                    if n < G_Z:
                        i = n - G_DN
                        for back in range(1, DN_TAPS):
                            for f in range(2):
                                m = 2 * i + f
                                if back == 1:
                                    dve.wait_ge(s_dnaff, m + 1)
                                elif f == 0:
                                    dve.wait_ge(s_dntap, 4 * i + 2 * (back - 1))
                                dve.scalar_tensor_tensor(dnT[:, m, back:NT], PG[:, b + f, 0:NT - back],
                                                         col(192 + 12 * (DN_TAPS - 1 - back) + m), dnT[:, m, back:NT],
                                                         ALU.mult, ALU.add).then_inc(s_ev if back == DN_TAPS - 1 else s_dntap, 1)
                    elif G_SB <= n < G_GATE:
                        dve.wait_ge(s_gran, n + 1)
                        i, m = divmod(n - G_SB, 2)
                        m = 2 * m + 1
                        if i == 0:
                            dve.tensor_scalar(sbq[:, m, :], PG[:, b + 1, 0:SEQ], SB_DH ** -0.5, None, ALU.mult).then_inc(s_ev, 1)
                        else:
                            dst = sbk[:, m, 0:NT] if i == 1 else sbvT[:, m, :]
                            dve.tensor_copy(dst, PG[:, b + 1, 0:NT]).then_inc(s_ev, 1)
                    elif G_BDN <= n < G_OUT:
                        i = n - G_BDN
                        dve.wait_ge(s_sig, 2)
                        dve.wait_ge(s_gran, n + 1)
                        g = gT[:, 4 * i:4 * i + 4, :]
                        dve.tensor_tensor(g.rearrange("p (b f) n -> p b (f n)", b=2), PM[:, 2:4, :] if i == 0 else PG[:, b:b + 2, :],
                                          g.rearrange("p (b f) n -> p b (f n)", b=2), ALU.mult).then_inc(s_ev, 2)
                        dve.wait_ge(s_ev, evacs(n))
                        m = mT[:, 4 * i:4 * i + 4, :]
                        dve.tensor_tensor(m, m, g, ALU.add).then_inc(s_m, 1)
                        dve.wait_ge(s_mhi, i + 1)
                        mh = hT_hi[:, 4 * i:4 * i + 4, 0:SEQ].bitcast(F32)
                        dve.tensor_tensor(hT_lo[:, 4 * i:4 * i + 4, 0:SEQ], m, mh, ALU.subtract).then_inc(s_mlo, 1)
                    elif n >= G_OUT:
                        dve.wait_ge(s_gran, n + 1)
                        c = slice(256 * (n - G_OUT), 256 * (n - G_OUT) + 256)
                        dve.scalar_tensor_tensor(X[:, :, c], X[:, :, c], ALPHA, PG[:, b:b + 2, 0:256], ALU.mult, ALU.add).then_inc(s_ev, 2)
                        dve.wait_ge(s_ev, evacs(n))
                        for t in range(TT):
                            i = 24 * t + 6 * (n - G_OUT)
                            dve.bn_stats(lnst[:, i:i + 6], X[:, t, c]).then_inc(s_ln, 1)
                elif kind == "norm":
                    m = st[1]
                    consumed(dve, *st)
                    if m < 4:
                        dve.scalar_tensor_tensor(dnT[:, m, :], dnT[:, m, :], DN_D ** -0.5, sqb[:, m, :], ALU.mult, ALU.mult).then_inc(s_l2, 1)
                    else:
                        dve.tensor_tensor(dnT[:, m, :], dnT[:, m, :], sqb[:, m, :], ALU.mult).then_inc(s_l2, 1)
                elif kind == "decays":
                    consumed(dve, "ba")
                    dve.wait_ge(s_wba, 48)
                    bias3 = dtb.unsqueeze(1).to_broadcast([P, 3, 4])
                    step(dve.tensor_tensor(gx, ba[:, :, 4:8], bias3, ALU.add))
                    step(dve.tensor_scalar(gn, gx, -1.0, None, ALU.mult))
                    dve.tensor_tensor(gn, gn, gx, ALU.min).then_inc(s_bx, 1)
                    dve.wait_ge(s_ey, 3)
                    step(dve.tensor_scalar(gu, gy, 2.0, None, ALU.add))
                    step(dve.reciprocal(gu, gu))
                    step(dve.tensor_tensor(gy, gy, gu, ALU.mult))
                    step(dve.tensor_tensor(gu, gy, gy, ALU.mult))
                    step(dve.tensor_scalar(gp, gu, 1.0 / 17, None, ALU.mult))
                    for k in range(15, 1, -2):
                        step(dve.scalar_tensor_tensor(gp, gp, 1.0 / k, gu, ALU.add, ALU.mult))
                    step(dve.scalar_tensor_tensor(gp, gp, 1.0, gy, ALU.add, ALU.mult))
                    step(dve.tensor_scalar(gp, gp, 2.0, None, ALU.mult))
                    step(dve.scalar_tensor_tensor(gp, gx, 0.0, gp, ALU.max, ALU.add))
                    step(dve.scalar_tensor_tensor(gdec, gp, -1.0, ea.unsqueeze(1).to_broadcast([P, 3, 4]), ALU.mult, ALU.mult))
                    step(dve.tensor_scalar(beta, beta, 1.0, None, ALU.add))
                    step(dve.reciprocal(beta, beta))
                    for c in range(3):
                        n = CH[c][1]
                        gh = gdec[0:n, c, :]
                        dve.tensor_tensor(mat(dN, cN, c), bc(con("gt")[0:n, 0:n], n, n), hbc(gh, n, n), ALU.mult).then_inc(s_gm, 1)
                        dst = dX[:, c, :, :] if c < 2 else cV[0:n, :, :]
                        dve.tensor_tensor(dst, bc(con("ones")[0:n, :], n, P), hbc(gh, n, P), ALU.mult).then_inc(s_gm, 1)
                elif kind == "drow" and st[1] == 1:
                    consumed(dve, *st)
                    dve.tensor_copy(cdc, dT[:, 1, :, P - 1:P].rearrange("p h o -> p (h o)")).then_inc(s_cd, 1)
                elif kind == "G":
                    c = st[1]
                    n = CH[c][1]
                    bank = heads(produced(dve, *st), n, n)
                    A = mat(dA, cA, c)
                    step(dve.tensor_tensor(A, bank, hbc(beta[0:n, c, :], n, n), ALU.mult))
                    dve.wait_ge(s_E, c + 1)
                    dve.tensor_tensor(A, A, mat(dE, cE, c), ALU.mult).then_inc(s_A, 1)
                    dve.wait_ge(s_A, c + 1)
                    dve.sem_inc(free(*st), 1)
                elif kind == "ktr":
                    c = st[1]
                    last = dE[:, c, :, P - 1:P].to_broadcast([P, DN_H, DN_D])
                    dve.tensor_tensor(kd[:, c, :, :], heads(produced(dve, *st)), last, ALU.mult).then_inc(free(*st), 1)
                elif kind == "QK":
                    c = st[1]
                    t0, n = CH[c]
                    E = mat(dE, cE, c)
                    bank = heads(produced(dve, *st), n, n)
                    if c < 2:
                        consumed(dve, "ktr", c)
                    dve.tensor_tensor(E, bank, E, ALU.mult).then_inc(free(*st), 1)
                    consumed(dve, "drow", c)
                    q = dnT[:, 0:4, t0:t0 + n]
                    ed = dT[:, c, :, :] if c < 2 else cT[:, :, :]
                    dve.tensor_tensor(q, q, ed, ALU.mult).then_inc(s_qd, 1)
                elif kind == "L0":
                    c = st[1]
                    n = CH[c][1]
                    dve.wait_ge(s_N, MASKED[0, c])
                    dve.tensor_tensor(mat(dU, cU, c), bc(con("ident")[0:n, 0:n], n, n), mat(dN, cN, c), ALU.subtract).then_inc(s_U0, 1)
                elif kind == "Y":
                    c = st[2]
                    n = CH[c][1]
                    U = mat(dU, cU, c)
                    dve.tensor_tensor(U, U, heads(produced(dve, *st), n, n), ALU.subtract).then_inc(free(*st), 1)
                elif kind == "KS":
                    c = st[1]
                    n = CH[c][1]
                    r = dN[:, c, :, :] if c < 2 else cR[0:n, :, :]
                    step(dve.tensor_tensor(r, heads(produced(dve, *st), n), hbc(edcol[0:n, c, :], n, DN_D), ALU.mult))
                    dve.tensor_tensor(r, vtok[0:n, c, :, :], r, ALU.subtract).then_inc(free(*st), 1)
                elif kind == "UV":
                    c = st[1]
                    n = CH[c][1]
                    dst = dX[:, c, :, :] if c < 2 else cV[0:n, :, :]
                    dve.tensor_tensor(dst, heads(produced(dve, *st), n), hbc(beta[0:n, c, :], n, DN_D), ALU.mult).then_inc(free(*st), 1)
                elif kind == "SU":
                    bank = heads(produced(dve, *st))
                    if st[1] == 0:
                        dve.tensor_copy(S[:, :, :], bank).then_inc(free(*st), 1)
                    else:
                        dve.wait_ge(s_cd, 1)
                        produced(dve, "O", 1)
                        step(dve.tensor_tensor(S[:, :, :], S[:, :, :], hbc(cdc, P, DN_D), ALU.mult))
                        dve.tensor_tensor(S[:, :, :], S[:, :, :], bank, ALU.add).then_inc(free(*st), 1)
                elif kind == "Z":
                    h = st[1]
                    dve.wait_ge(s_e, E_OF_HEAD[h])
                    e = stick[:, h % 2, :]
                    step(dve.scalar_tensor_tensor(e, PM[:, 2 + h % 2, 0:416], 0.0, e, ALU.max, ALU.add))
                    dve.tensor_tensor(e, e, con("keep"), ALU.mult).then_inc(s_sp, 1)
                elif kind == "C":
                    h = st[1]
                    dve.wait_ge(s_cs, h + 1)
                    dve.tensor_tensor(stick[:, h % 2, :], PM[:, 2 + h % 2, 0:416], con("drop"), ALU.add).then_inc(s_arg, 1)
                elif kind == "V":
                    h = st[1]
                    b = SB_DH * (h % 2)
                    dve.wait_ge(s_osbhi, h + 1)
                    dve.tensor_tensor(osb_lo[b:b + SB_DH, h // 2, :], PM[b:b + SB_DH, 2 + h % 2, 0:SEQ],
                                      osb_hi[b:b + SB_DH, h // 2, :].bitcast(F32), ALU.subtract).then_inc(s_osblo, 1)
                elif kind == "sbmul":
                    i = st[1]
                    b = 2 * ((G_BSB + i) % 2)
                    dve.wait_ge(s_sig, 1)
                    dve.wait_ge(s_gran, G_BSB + i + 1)
                    consumed(dve, "O", 2)
                    dve.tensor_tensor(mT[:, 4 * i:4 * i + 4, :].rearrange("p (b f) n -> p b (f n)", b=2), PG[:, b:b + 2, :],
                                      gT[:, 8 + 4 * i:12 + 4 * i, :].rearrange("p (b f) n -> p b (f n)", b=2), ALU.mult).then_inc(s_ev, 2)
                elif kind == "orms":
                    i = st[1]
                    consumed(dve, *st)
                    r = osq[:, 2 * i:2 * i + 2, :]
                    o = odn[:, 2 * i:2 * i + 2, :]
                    step(dve.scalar_tensor_tensor(o, o, col(240), r, ALU.mult, ALU.mult))
                    dve.tensor_tensor(o, o, zT[:, 2 * i:2 * i + 2, :], ALU.mult).then_inc(s_on, 1)
                    if i == 1:
                        dve.wait_ge(s_odnhi, 1)
                        dve.tensor_tensor(odn_lo[:, :, :], odn[:, :, :], odn_hi[:, :, :].bitcast(F32), ALU.subtract).then_inc(s_odnlo, 1)

            def scale_shift(t, k, diff, op):
                step(dve.scalar_tensor_tensor(X[:, t, :], X[:, t, :], diff, lnrow[:, 0, :], op, ALU.mult))
                dve.wait_ge(s_lnrt, TT * k + t + 1)
                step(dve.reciprocal(lnrs[:, t:t + 1], lnrt[:, t:t + 1]))
                dve.scalar_tensor_tensor(X[:, t, :], X[:, t, :], lnrs[:, t:t + 1], lnrow[:, 1, :], ALU.mult, ALU.add).then_inc(s_h, 1)

            dve.wait_ge(s_ln, 4 * TT)
            for t in range(TT):
                dve.bn_aggr(lnmv[:, 2 * t:2 * t + 2], lnst[:, 24 * t:24 * t + 24]).then_inc(s_lnv, 1)
            dve.wait_ge(s_lnv, TT)
            dve.wait_ge(s_lnrow, 32)
            for t in range(TT):
                scale_shift(t, 1, lnmv[:, 2 * t:2 * t + 1], ALU.subtract)
            for t in range(TT):
                dve.wait_ge(s_xT, 13 + 2 * t + 2)
                dve.tensor_copy(h1T[:, 4:8, P * t:P * t + P], PM[:, 2 * t + 1, :].rearrange("p (k n) -> p k n", k=4)).then_inc(s_h1T, 1)
            for t in range(TT):
                dve.wait_ge(s_xhi3, t + 1)
                dve.tensor_tensor(X_lo[:, t, :], X[:, t, :], X_hi[:, t, :].bitcast(F32), ALU.subtract).then_inc(s_xlo3, 1)

            def expert_lo(E, kind, par):
                dve.wait_ge(s_ehi, in_step(E) + kind + 1)
                dve.tensor_tensor(elo[kind][:, :], ring[3 * par + kind][:, :], ehi[kind][:, :].bitcast(F32),
                                  ALU.subtract).then_inc(s_elo, 2 if isinstance(E, int) and E == 0 and kind == 1 else 1)

            for kind in range(2):
                expert_lo(0, kind, 0)

            def wide2(x, n):
                return x.to_broadcast([P, TT, n])

            def first_max(onehot, key, diff, n):
                falling = con("falling")[:, 0:n].unsqueeze(1).to_broadcast([P, TT, n])
                step(dve.scalar_tensor_tensor(key, diff, 0.0, falling, ALU.is_equal, ALU.mult))
                step(dve.tensor_reduce(kmax, key, AX.X, ALU.max))
                step(dve.tensor_tensor(onehot, key, wide2(kmax, n), ALU.is_equal))

            dve.wait_ge(s_logit, 1)
            dve.wait_ge(s_wr, 112)
            step(dve.tensor_tensor(logit, PG[:, 0, 0:2 * NL].rearrange("p (t n) -> p t n", t=TT),
                                   rb.unsqueeze(1).to_broadcast([P, TT, NL]), ALU.add))
            glog, elog = logit[:, :, 0:GROUPS], logit[:, :, GROUPS:NL]
            step(dve.tensor_reduce(gmax, glog, AX.X, ALU.max))
            step(dve.tensor_tensor(d5[:, :, 0:GROUPS], glog, wide2(gmax, GROUPS), ALU.subtract))
            first_max(goh, gkey, d5[:, :, 0:GROUPS], GROUPS)
            gwide = goh.unsqueeze(3).to_broadcast([P, TT, GROUPS, EPG])
            step(dve.tensor_tensor(prod, grouped(elog), gwide, ALU.mult))
            step(dve.tensor_reduce(sel, prod.rearrange("p t g e -> p t e g"), AX.X, ALU.add))
            step(dve.tensor_reduce(top1, sel, AX.X, ALU.max))
            step(dve.tensor_tensor(esel, sel, wide2(top1, EPG), ALU.subtract))
            first_max(oh1, ekey, esel, EPG)
            step(dve.scalar_tensor_tensor(sel, oh1, -1e30, sel, ALU.mult, ALU.add))
            step(dve.tensor_reduce(top2, sel, AX.X, ALU.max))
            dve.tensor_tensor(d5[:, :, GROUPS:5], top2, top1, ALU.subtract).then_inc(s_d5, 1)
            step(dve.tensor_tensor(esel, sel, wide2(top2, EPG), ALU.subtract))
            first_max(oh2, ekey, esel, EPG)
            for m, oh in ((M1, oh1), (M2, oh2)):
                step(dve.tensor_tensor(grouped(m), gwide, oh.unsqueeze(2).to_broadcast([P, TT, GROUPS, EPG]), ALU.mult))
            dve.tensor_tensor(M12, M1, M2, ALU.add).then_inc(s_M, 1)
            dve.wait_ge(s_e5, 1)
            step(dve.tensor_reduce(gsum, e5[:, :, 0:GROUPS], AX.X, ALU.add))
            step(dve.scalar_tensor_tensor(w1, e5[:, :, GROUPS:5], 1.0, gsum, ALU.add, ALU.mult))
            step(dve.reciprocal(w1, w1))
            dve.tensor_tensor(w2, w1, e5[:, :, GROUPS:5], ALU.mult).then_inc(s_w12, 1)
            dve.wait_ge(s_rank, 1)
            cnt = PG[:, 1, 2 * NE:3 * NE]
            step(dve.tensor_tensor_scan(incl, con("ones")[:, 0:NE], cnt, 0.0, ALU.mult, ALU.add))
            step(dve.tensor_tensor(off, incl, cnt, ALU.subtract))
            step(dve.tensor_reduce(cmax, cnt, AX.X, ALU.max))
            step(dve.tensor_copy(offi[0:1, 0:NE], off[0:1, :]))
            dve.tensor_copy(offi[0:1, NE:NE + 1], cmax[0:1, :]).then_inc(s_off, 1)
            step(dve.tensor_tensor(slotpos, PG[:, 1, 0:2 * NE].rearrange("p (t n) -> p t n", t=TT),
                                   off.unsqueeze(1).to_broadcast([P, TT, NE]), ALU.add))
            for m, pos in ((M1, pos1), (M2, pos2)):
                step(dve.tensor_tensor(m, m, slotpos, ALU.mult))
                step(dve.tensor_reduce(pos, m, AX.X, ALU.add))
            for t in range(TT):
                step(dve.tensor_scalar(pick2[:, t, :], con("slots"), pos2[:, t, :], None, ALU.is_equal))
                dve.scalar_tensor_tensor(pick[:, t, :], con("slots"), pos1[:, t, :], pick2[:, t, :], ALU.is_equal, ALU.add).then_inc(s_P, 1)
            for t in range(TT):
                dve.tensor_scalar(pick1[:, t, :], con("slots"), pos1[:, t, :], None, ALU.is_equal).then_inc(s_w12, 1)
            for k in range(1, KD, 2):
                dve.wait_ge(s_xg, k + 1)
                dve.tensor_copy(pair[:, k, SEQ:SEQ + PAIRS], PM[:, k % 4, :]).then_inc(s_xgv, 1)

            def moe(W):
                def results(e, e2):
                    at = dve.value_load(offi[0:1, bass.ds(e, 1)], min_val=0, max_val=PAIRS)
                    y, dst = down_sums(W, e2), pair[:, :, bass.ds(at, W)]
                    if W == WIN:
                        dve.wait_ge(s_yhalf, e + 1)
                        if not (isinstance(e, int) and e == 0):
                            dve.wait_ge(s_yg, e)
                        dve.tensor_tensor(dst, yhalf[:, e2, :, :], y[:, :, W:2 * W], ALU.add).then_inc(s_yg, 1)
                    else:
                        dve.wait_ge(s_egran, in_step(e + 1) + 3 if not (isinstance(e, int) and e == NE - 1) else in_step(NE) + 1)
                        dve.tensor_copy(dst, y).then_inc(s_yg, 1)

                def step_of(e, u, r):
                    last = isinstance(e, int) and e == NE - 1
                    if not last:
                        expert_lo(e + 1, 0, u)
                        expert_lo(e + 1, 1, u)
                    if W == SEQ and not (isinstance(e, int) and e == 0):
                        results(e - 1, u)
                    dve.wait_ge(s_sg, e + 1)
                    if last:
                        dve.wait_ge(s_hmlo, e)
                    dve.tensor_tensor(hm[W][:, :, :], sg[W][:, :, :], gate_up(W, 1 - u)[1], ALU.mult).then_inc(s_hm, 1)
                    if last:
                        dve.wait_ge(s_ehi, in_step(NE) + 1)
                        dve.tensor_tensor(elo[0][:, :], ring[2][:, :], ehi[0][:, :].bitcast(F32), ALU.subtract).then_inc(s_elo, 1)
                    else:
                        expert_lo(e + 1, 2, u)
                    dve.wait_ge(s_hmhi, e + 1)
                    dve.tensor_tensor(hw2[W][1 - u][:, :, W:2 * W], hm[W][:, :, :], hw2[W][1 - u][:, :, 0:W].bitcast(F32), ALU.subtract).then_inc(s_hmlo, 1)
                    if W == WIN and not (isinstance(e, int) and e == 0):
                        results(e - 1, u)

                step_of(0, 1, 0)
                with dve.Fori(0, NE // 2 - 1) as r:
                    for u in range(2):
                        step_of(2 * r + 1 + u, u, r + 1)
                step_of(NE - 1, 0, NE // 2)
                results(NE - 1, 1)

            by_count(dve, lambda: moe(WIN), lambda: moe(SEQ))
            dve.wait_ge(s_pickT, 2)
            for j in range(PAIRS // P):
                dve.wait_ge(s_yghi, j + 1)
                src = (PM if j < 2 else PG)[:, 2 * (j % 2):2 * (j % 2) + 2, :]
                dve.scalar_tensor_tensor(yg_lo[:, j, :].rearrange("p (b n) -> p b n", b=2), src, wslot[:, j:j + 1],
                                         yg_hi[:, j, :].rearrange("p (b n) -> p b n", b=2).bitcast(F32), ALU.mult, ALU.subtract).then_inc(s_yglo, 1)
            dve.wait_ge(s_alpha, 1)
            for t in range(TT):
                dve.wait_ge(s_sum, t + 1)
                x = X[:, t, :].rearrange("p (b n) -> p b n", b=2)
                step(dve.tensor_tensor_reduce(x, x, PM[:, 2 * t:2 * t + 2, :], 1.0, 0.0, ALU.add, ALU.add, zsum[:, t:t + 1]))
                dve.tensor_scalar(nmu[:, t:t + 1], zsum[:, t:t + 1], -1.0 / D, None, ALU.mult).then_inc(s_nmu, 1)
            dve.wait_ge(s_lnrow, 64)
            for t in range(TT):
                dve.wait_ge(s_vs, TT + t + 1)
                scale_shift(t, 2, nmu[:, t:t + 1], ALU.add)
        @block.tensor
        def _(pe):
            def norm_T(q):
                for t in range(TT):
                    pe.wait_ge(s_xn, 2 * q + t + 1)
                    for k in range(KD):
                        mm = pe.transpose(PM[:, 2 * t + k // 4, P * (k % 4):P * (k % 4) + P], XN[:, t, P * k:P * k + P], con("ident"))
                        if k % 4 == 3:
                            mm.then_inc(s_xT, 1)

            def split3(dst, lh, ll, rh, rl, start, stop, **kw):
                pe.matmul(dst, lh, rh, start=start, stop=False, **kw)
                pe.matmul(dst, lh, rl, start=False, stop=False, **kw)
                return pe.matmul(dst, ll, rh, start=False, stop=stop, **kw)

            def w_of(w, n):
                return w[:, n % H, :].rearrange("p (k n) -> p k n", k=KD)

            def features(n, bank, ah, al, c, it=0):
                pe.wait_ge(s_lo, n + 1 + 6 * it)
                hw, lw = w_of(whi, n), w_of(wlo, n)
                for f in range(2):
                    for k in range(KD):
                        mm = split3(PG[:, bank + f, 0:c.stop - c.start], hw[:, k, P * f:P * f + P], lw[:, k, P * f:P * f + P],
                                    ah[:, k, c], al[:, k, c], k == 0, k == KD - 1)
                mm.then_inc(s_gran, 1)

            def tokens(n, bank, ah, al, parts=None):
                pe.wait_ge(s_lo, n + 1)
                hw, lw = w_of(whi, n), w_of(wlo, n)
                for k0, k1, ready, count in parts or [(0, KD, None, 0)]:
                    if ready is not None:
                        pe.wait_ge(ready, count)
                    for t in range(TT):
                        for k in range(k0, k1):
                            c = slice(P * t, P * t + P)
                            mm = split3(PG[:, bank + t, 0:256], ah[:, k, c], al[:, k, c], hw[:, k, :], lw[:, k, :], k == 0, k == KD - 1)
                mm.then_inc(s_gran, 1)

            pe.wait_ge(s_cst, 16)
            norm_T(0)
            pe.wait_ge(s_xlo, 4)
            for n in range(12):
                if n >= 2:
                    pe.wait_ge(s_ev, 2 * (n - 1))
                if n < 8:
                    features(n, 2 * (n % 2), hT_hi, hT_lo, slice(0, SEQ))
                else:
                    tokens(n, 2 * (n % 2), hT_hi, hT_lo)
            pe.wait_ge(s_ev, 24)
            for i in range(A_HEADS + 3):
                if i < A_HEADS:
                    h = i
                    b = A_DH * (h % 2)
                    if h >= 3:
                        pe.wait_ge(s_mx, 2 * h - 4)
                    score = scores(h)
                    pe.matmul(score[:, 0:P], qT[b:b + A_DH, h // 2, 0:P], kT[b:b + A_DH, h // 2, 0:P], start=True, stop=True)
                    pe.matmul(score[:, P:3 * P], qT[b:b + A_DH, h // 2, P:SEQ], kT[b:b + A_DH, h // 2, :], start=True, stop=True).then_inc(s_S, 1)
                if 2 <= i < A_HEADS + 2:
                    h = i - 2
                    pe.wait_ge(s_prob, 2 * h + 2)
                    if h >= 2:
                        pe.wait_ge(s_probT, h - 1)
                    for j in range(3):
                        mm = pe.transpose(PM[:, 2 + h % 2, P * j:P * j + P], prob[:, h % 3, P * j:P * j + P], con("ident"))
                    mm.then_inc(s_PT, 1)
                if i >= 3:
                    h = i - 3
                    hp, b = h // 2, A_DH * (h % 2)
                    pe.wait_ge(s_probT, h + 1)
                    if hp >= 2 and h % 2 == 0:
                        pe.wait_ge(s_oTlo, hp - 1)
                    o = PG[b:b + A_DH, hp % 2, 0:SEQ]
                    pe.matmul(o, vv[:, 0, A_DH * h:A_DH * h + A_DH], probT[:, h % 2, 0:SEQ], start=True, stop=False, skip_group_check=True)
                    pe.matmul(o[:, P:SEQ], vv[:, 1, A_DH * h:A_DH * h + A_DH], probT[:, h % 2, SEQ:3 * P], start=False, stop=True,
                              skip_group_check=True).then_inc(s_PV, 1)
            pe.wait_ge(s_oTlo, KD)
            for n in range(G_WO, G_FFN):
                if n >= G_WO + 2:
                    pe.wait_ge(s_ev, 2 * (n - 1))
                tokens(n, 2 * (n % 2), oT_hi, oT_lo)
            pe.wait_ge(s_vrow, 96)
            pe.wait_ge(s_ev, 32)
            pe.transpose(PG[:, 2, 0:P], vrow[:, 0, :], con("ident"))
            pe.transpose(PG[:, 2, P:P + 113], vrow[0:113, 1, :], con("ident", 113, 113)).then_inc(s_colsT, 1)
            norm_T(1)
            pe.wait_ge(s_xlo, 8)
            pe.wait_ge(s_zero, 1)
            for b in range(4):
                pe.matmul(PM[:, b, :], zero[0:1, 0:P], zero[0:1, 0:512], start=True, stop=True)

            def down(n, par, it, j, last=False):
                pe.wait_ge(s_hidlo, j + 1)
                pe.wait_ge(s_lo, n + 1 + 6 * it)
                hw = whi[:, n % H, :].rearrange("p (c n) -> p c n", c=2)
                lw = wlo[:, n % H, :].rearrange("p (c n) -> p c n", c=2)
                for t in range(TT):
                    for f in range(2):
                        for c in range(2):
                            x = slice(P * t, P * t + P)
                            w = slice(512 * f, 512 * f + 512)
                            mm = split3(PM[:, 2 * t + f, :], hid_hi[:, par, c, x], hid_lo[:, par, c, x], hw[:, c, w], lw[:, c, w],
                                        False, True, skip_group_check=True)
                    if last and t == 0:
                        mm.then_inc(s_ffn, 1)
                mm.then_inc(s_gran, 1)

            def ffn_step(n, j, par, it, first=False):
                if not first:
                    pe.wait_ge(s_gconv, j)
                else:
                    pe.wait_ge(s_cols, 1)
                features(n, 0, hT_hi, hT_lo, slice(0, SEQ), it)
                if not first:
                    pe.wait_ge(s_uconv, j)
                features(n + 1, 2, hT_hi, hT_lo, slice(0, SEQ), it)
                if not first:
                    down(n + 2, 1 - par, it, j - 1)

            ffn_step(G_FFN, 0, 0, 0, first=True)
            with pe.Fori(0, (FJ - 1) // 2) as it:
                for u in range(2):
                    ffn_step(G_FFN + 2 + 3 * u, 2 * it + 1 + u, (1 + u) % 2, it)
            down(G_IN - 1, (FJ - 1) % 2, 0, FJ - 1, last=True)
            pe.wait_ge(s_cst2, 16)
            pe.wait_ge(s_metaln, 1)
            for k in range(KD):
                mm = pe.transpose(PG[:, 0, META * k:META * k + META], MT[:, P * k:P * k + P], con("ident", META, META))
            mm.then_inc(s_xT, 1)
            for t in range(TT):
                pe.wait_ge(s_h, t + 1)
                for k in range(KD):
                    mm = pe.transpose(PM[:, 2 * t + k // 4, P * (k % 4):P * (k % 4) + P], X[:, t, P * k:P * k + P], con("ident"))
                    if k % 4 == 3:
                        mm.then_inc(s_xT, 1)
            pe.wait_ge(s_xlo, 13)

            def branch(n, ah, al):
                pe.wait_ge(s_lo, n + 1)
                hw, lw = (w[:, n % H, :].rearrange("p (k n) -> p k n", k=4) for w in (whi, wlo))
                for f in range(4):
                    bank = (PM if n == G_BDN else PG)[:, (2 if n == G_BDN else 2 * (n % 2)) + f // 2, :]
                    dst = bank[:, SEQ * (f % 2):SEQ * (f % 2) + SEQ]
                    for k in range(4):
                        x = slice(P * f, P * f + P)
                        mm = split3(dst, hw[:, k, x], lw[:, k, x], ah[:, k, :], al[:, k, :], k == 0, k == 3)
                mm.then_inc(s_gran, 1)

            for st in plan:
                kind = st[0]
                if kind == "gran":
                    n = st[1]
                    if n >= G_IN + 2 and n != G_BDN:
                        pe.wait_ge(s_ev, evacs(n - 2))
                    b = 2 * (n % 2)
                    if n < G_BSB:
                        own = G_Z <= n < G_SB + 2 or n >= G_GATE
                        features(n, b, hT_hi, hT_lo, slice(META if own else 0, NT))
                    elif n < G_BDN:
                        pe.wait_ge(s_osblo, SB_H)
                        branch(n, osb_hi, osb_lo)
                    elif n < G_OUT:
                        pe.wait_ge(s_odnlo, 1)
                        branch(n, odn_hi, odn_lo)
                    else:
                        if n == G_OUT:
                            tokens(n, b, hT_hi, hT_lo, [(0, KD // 2, s_mlo, 1), (KD // 2, KD, s_mlo, 2)])
                        else:
                            tokens(n, b, hT_hi, hT_lo)
                elif kind == "ba":
                    pe.wait_ge(s_wba, 48)
                    bank = vacant(pe, *st)
                    for c, (t0, n) in enumerate(CH):
                        for i, hT in enumerate((hT_hi, hT_lo)):
                            for k in range(KD):
                                mm = pe.matmul(bank[0:n, 8 * c:8 * c + 8], hT[:, k, t0:t0 + n].bitcast(F32), wba[:, k, :],
                                               start=i + k == 0, stop=i == 1 and k == KD - 1)
                    mm.then_inc(full(*st), 1)
                elif kind == "norm":
                    pe.wait_ge(s_sq, st[1] // 4 + 1)
                    pe.matmul(vacant(pe, *st)[:, 0:NT], con("ones"), sqb[:, st[1], :], start=True, stop=True).then_inc(full(*st), 1)
                elif kind in ("D", "drow"):
                    c = st[1]
                    n = CH[c][1]
                    pe.wait_ge(s_gm, 2 * c + 1 + (kind == "drow"))
                    bank = heads(vacant(pe, *st))
                    for h in range(DN_H):
                        if kind == "D":
                            mm = pe.matmul(bank[0:n, h, 0:n], mat(dN, cN, c)[:, h, :], con("le")[0:n, 0:n], start=True, stop=True)
                        else:
                            g = dX[:, c, h, :] if c < 2 else cV[0:n, h, :]
                            mm = pe.matmul(bank[:, h, 0:n], g, con("le")[0:n, 0:n], start=True, stop=True)
                    mm.then_inc(full(*st), 1)
                elif kind == "dcol":
                    c = st[1]
                    n = CH[c][1]
                    pe.wait_ge(s_gm, 2 * c + 2)
                    pe.matmul(vacant(pe, *st)[0:n, 0:DN_H], con("le")[0:n, 0:n], gdec[0:n, c, :], start=True, stop=True).then_inc(full(*st), 1)
                elif kind in ("G", "QK"):
                    c = st[1]
                    t0, n = CH[c]
                    pe.wait_ge(s_l2, 8)
                    bank = heads(vacant(pe, *st))
                    for h in range(DN_H):
                        k = dnT[:, 4 + h, t0:t0 + n]
                        mm = pe.matmul(bank[0:n, h, 0:n], k, k if kind == "G" else dnT[:, h, t0:t0 + n], start=True, stop=True)
                    mm.then_inc(full(*st), 1)
                elif kind in ("ktr", "vtr"):
                    c = st[1]
                    t0, n = CH[c]
                    pe.wait_ge(s_dnsilu, 6)
                    bank = heads(vacant(pe, *st))
                    for h in range(DN_H):
                        mm = pe.transpose(bank[0:n, h, :], dnT[:, (4 if kind == "ktr" else 8) + h, t0:t0 + n], con("ident"))
                    mm.then_inc(full(*st), 1)
                elif kind == "sbv":
                    c = st[1]
                    t0, n = CH[c]
                    pe.wait_ge(s_ev, evacs(G_GATE - 1))
                    pe.wait_ge(s_init, 3)
                    bank = heads(vacant(pe, *st))
                    for f in range(4):
                        mm = pe.transpose(bank[0:n, f, :], sbvT[:, f, t0:t0 + n], con("ident"))
                    mm.then_inc(full(*st), 1)
                elif kind in ("L0", "T"):
                    c = st[-1]
                    n = CH[c][1]
                    if kind == "L0":
                        pe.wait_ge(s_U0, c + 1)
                    else:
                        consumed(pe, "Y", st[1], c)
                    bank = heads(vacant(pe, *st), n, n)
                    U = mat(dU, cU, c)
                    for h in range(DN_H):
                        mm = pe.transpose(bank[:, h, :], U[:, h, :], con("ident")[0:n, 0:n])
                    mm.then_inc(full(*st), 1)
                elif kind in ("X", "Y"):
                    s, c = st[1:]
                    n = CH[c][1]
                    if kind == "X":
                        pe.wait_ge(s_N, MASKED[s, c])
                        consumed(pe, *(("T", s - 1, c) if s > 1 else ("L0", c)))
                        l, r = mat(dN, cN, c), mat(dT, cT, c)
                    else:
                        consumed(pe, "X", s, c)
                        if s > 1:
                            consumed(pe, "Y", s - 1, c)
                        l, r = mat(dX, cX, c), mat(dU, cU, c)
                    bank = heads(vacant(pe, *st), n, n)
                    for h in range(DN_H):
                        mm = pe.matmul(bank[:, h, :], l[:, h, :], r[:, h, :], start=True, stop=True)
                    mm.then_inc(full(*st), 1)
                elif kind == "KS":
                    c = st[1]
                    t0, n = CH[c]
                    consumed(pe, "SU", c - 1)
                    bank = heads(vacant(pe, *st))
                    for h in range(DN_H):
                        mm = pe.matmul(bank[0:n, h, :], dnT[:, 4 + h, t0:t0 + n], S[:, h, :], start=True, stop=True)
                    mm.then_inc(full(*st), 1)
                elif kind == "UV":
                    c = st[1]
                    n = CH[c][1]
                    consumed(pe, "Y", LEV[c] - 1, c)
                    consumed(pe, *(("vtr", 0) if c == 0 else ("KS", c)))
                    r = vtok[:, 0, :, :] if c == 0 else dN[:, 1, :, :] if c == 1 else cR[0:n, :, :]
                    bank = heads(vacant(pe, *st))
                    U = mat(dU, cU, c)
                    for h in range(DN_H):
                        mm = pe.matmul(bank[0:n, h, :], U[:, h, :], r[:, h, :], start=True, stop=True)
                    mm.then_inc(full(*st), 1)
                elif kind == "O":
                    c = st[1]
                    t0, n = CH[c]
                    consumed(pe, "UV", c)
                    pe.wait_ge(s_qd, 3)
                    bank = heads(vacant(pe, *st), P, n)
                    v = dX[:, c, :, :] if c < 2 else cV[0:n, :, :]
                    E = mat(dE, cE, c)
                    for h in range(DN_H):
                        if c:
                            pe.matmul(bank[:, h, :], S[:, h, :], dnT[:, h, t0:t0 + n], start=True, stop=False)
                        mm = pe.matmul(bank[:, h, :], v[:, h, :], E[:, h, :], start=c == 0, stop=True)
                    mm.then_inc(full(*st), 1)
                elif kind == "SU":
                    c = st[1]
                    consumed(pe, "UV", c)
                    consumed(pe, "ktr", c)
                    bank = heads(vacant(pe, *st))
                    for h in range(DN_H):
                        mm = pe.matmul(bank[:, h, :], kd[:, c, h, :], dX[:, c, h, :], start=True, stop=True)
                    mm.then_inc(full(*st), 1)
                elif kind == "Z":
                    h = st[1]
                    b = SB_DH * (h % 2)
                    if h == 0:
                        pe.wait_ge(s_ev, evacs(G_GATE - 1))
                        pe.wait_ge(s_init, 3)
                    if h >= 2:
                        pe.wait_ge(s_osblo, h - 1)
                    q, k = sbq[b:b + SB_DH, h // 2, :], sbk[b:b + SB_DH, h // 2, :]
                    Z = PM[:, 2 + h % 2, :]
                    pe.matmul(Z[:, 0:256], k[:, 0:P], q, start=True, stop=False, skip_group_check=True)
                    pe.matmul(Z[:, 256:400], k[:, P:2 * P], q[:, 112:256], start=False, stop=False, skip_group_check=True)
                    pe.matmul(Z[:, 400:416], k[:, 2 * P:3 * P], q[:, 240:256], start=False, stop=True, skip_group_check=True).then_inc(s_z, 1)
                elif kind == "C":
                    h = st[1]
                    pe.wait_ge(s_sp, h + 1)
                    Z, e = PM[:, 2 + h % 2, :], stick[:, h % 2, :]
                    tri, one = con("nge"), con("nones")
                    for o, w, i in ((slice(0, 256), tri, slice(0, 256)), (slice(112, 256), one, slice(256, 400)),
                                    (slice(240, 256), one, slice(400, 416)), (slice(256, 400), tri, slice(256, 400)),
                                    (slice(384, 400), one, slice(400, 416)), (slice(400, 416), tri, slice(400, 416))):
                        mm = pe.matmul(Z[:, o], w, e[:, i], start=False, stop=True, skip_group_check=True)
                    mm.then_inc(s_cs, 1)
                elif kind == "V":
                    h = st[1]
                    b = SB_DH * (h % 2)
                    pe.wait_ge(s_w, h + 1)
                    if h == 0:
                        consumed(pe, "sbv", 2)
                    e = stick[:, h % 2, :]
                    o = PM[b:b + SB_DH, 2 + h % 2, :]
                    x = slice(SB_DH * h, SB_DH * h + SB_DH)
                    pe.matmul(o[:, 0:256], sbv[:, 0, x], e[:, 0:256], start=True, stop=False, skip_group_check=True)
                    pe.matmul(o[:, 112:256], sbv[:, 1, x], e[:, 256:400], start=False, stop=False, skip_group_check=True)
                    pe.matmul(o[:, 240:256], sbv[:, 2, x], e[:, 400:416], start=False, stop=True, skip_group_check=True).then_inc(s_pv, 1)
                elif kind == "orms":
                    i = st[1]
                    pe.wait_ge(s_osq, 1)
                    pe.matmul(vacant(pe, *st), con("ones"), osq[:, 2 * i:2 * i + 2, :].rearrange("p h n -> p (h n)"),
                              start=True, stop=True).then_inc(full(*st), 1)
            for t in range(TT):
                pe.wait_ge(s_h, TT + t + 1)
                for k in range(KD):
                    mm = pe.transpose(PM[:, 2 * t + k // 4, P * (k % 4):P * (k % 4) + P], X[:, t, P * k:P * k + P], con("ident"))
                    if k % 4 == 3:
                        mm.then_inc(s_xT, 1)
            pe.wait_ge(s_h1T, 4)
            pe.wait_ge(s_wr, 112)
            for t in range(TT):
                for k in range(KD):
                    mm = pe.matmul(PG[:, 0, NL * t:NL * t + NL], h1T[:, k, P * t:P * t + P], wr[:, k, :], start=k == 0, stop=k == KD - 1)
            mm.then_inc(s_logit, 1)
            pe.wait_ge(s_M, 1)
            pe.matmul(PG[:, 1, 0:NE], con("lt"), M12[:, 0, :], start=True, stop=True)
            pe.matmul(PG[:, 1, NE:2 * NE], con("ones"), M12[:, 0, :], start=True, stop=False)
            pe.matmul(PG[:, 1, NE:2 * NE], con("lt"), M12[:, 1, :], start=False, stop=True)
            pe.matmul(PG[:, 1, 2 * NE:3 * NE], con("ones"), M12[:, 0, :], start=True, stop=False)
            pe.matmul(PG[:, 1, 2 * NE:3 * NE], con("ones"), M12[:, 1, :], start=False, stop=True).then_inc(s_rank, 1)
            pe.wait_ge(s_xlo3, TT)
            pe.wait_ge(s_P, TT)
            for k in range(KD):
                if k >= 4:
                    pe.wait_ge(s_xgv if k % 2 else s_xga, k // 2 - 1)
                for t in range(TT):
                    for i, x in enumerate((X_hi, X_lo)):
                        mm = pe.matmul(PM[:, k % 4, :], x[:, t, P * k:P * k + P], pick[:, t, :], start=t + i == 0, stop=t + i == 2)
                mm.then_inc(s_xg, 1)
            pe.wait_ge(s_w12, 1 + TT)
            for j in range(PAIRS // P):
                for t in range(TT):
                    for pk, w in ((pick1, w1), (pick2, w2)):
                        pe.matmul(PG[:, 1, j:j + 1], pk[:, t, P * j:P * j + P], w[:, t, :], start=t == 0 and pk is pick1,
                                  stop=t == 1 and pk is pick2)
            for j in range(PAIRS // P):
                for t in range(TT):
                    mm = pe.transpose(PG[:, 2 + j // 2, SEQ * (j % 2) + P * t:SEQ * (j % 2) + P * t + P],
                                      pick[:, t, P * j:P * j + P].bitcast(F32), con("ident"))
            mm.then_inc(s_pT, 1)
            pe.wait_ge(s_xga, KD // 2)
            pe.wait_ge(s_xgv, KD // 2)

            def halves(kind, n):
                return (w[kind][:, :].rearrange("p (k n) -> p k n", k=n) for w in (ehi, elo))

            def gate_up_half(W, e, e2, kind):
                pe.wait_ge(s_elo, in_step(e) + kind + 1)
                if kind == 0:
                    pe.wait_ge(s_win, e + 1)
                x = xw[W][e2 % len(xw[W])]
                hw, lw = halves(kind, KH)
                if W == WIN:
                    for k in range(KH):
                        for w in (hw, lw):
                            mm = pe.matmul(PG[:, 0, :], x[:, KH * kind + k, :], w[:, k, :], start=kind == 0 and k == 0 and w is hw,
                                           stop=kind == 1 and k == KH - 1 and w is lw)
                else:
                    for i, dst in enumerate(gate_up(W, e2)):
                        for f in range(2):
                            for k in range(KH):
                                c, q = slice(EFF * i + P * f, EFF * i + P * f + P), KH * kind + k
                                mm = split3(dst[:, f, :], hw[:, k, c], lw[:, k, c], x[:, q, 0:W], x[:, q, W:2 * W],
                                            kind == 0 and k == 0 and f == 0, kind == 1 and k == KH - 1, skip_group_check=True)
                mm.then_inc(s_egran, 2 if isinstance(e, int) and e == 0 and kind == 1 else 1)

            def down_of(W, e, e2):
                pe.wait_ge(s_elo, in_step(e + 1) + 3 if not (isinstance(e, int) and e == NE - 1) else in_step(NE) + 1)
                pe.wait_ge(s_hmlo, e + 1)
                dst = down_sums(W, e2)
                hw, lw = halves(0 if isinstance(e, int) and e == NE - 1 else 2, 2)
                for d in range(KD):
                    c = slice(P * d, P * d + P)
                    for f in range(2):
                        if W == WIN:
                            pe.matmul(dst[:, d, :], hw[:, f, c], hw2[W][e2][:, f, :], start=f == 0, stop=False)
                            mm = pe.matmul(dst[:, d, :], lw[:, f, c], hw2[W][e2][:, f, :], start=False, stop=f == 1)
                        else:
                            mm = split3(dst[:, d, :], hw[:, f, c], lw[:, f, c], hw2[W][e2][:, f, 0:W], hw2[W][e2][:, f, W:2 * W], f == 0, f == 1)
                mm.then_inc(s_egran, 1)

            def moe(W):
                def step_of(e, e2):
                    last = isinstance(e, int) and e == NE - 1
                    gate_up_half(W, e, e2, 0)
                    gate_up_half(W, e, e2, 1)
                    if not (isinstance(e, int) and e == 0) and not (last and W == WIN):
                        down_of(W, e - 1, 1 - e2)
                    if W == WIN:
                        pe.wait_ge(s_gu, e + 1)
                        if isinstance(e, int) and e == 0:
                            pe.wait_ge(s_pickT, 2)
                        for j in range(4):
                            mm = pe.matmul(PG[:, 1, WIN * j:WIN * j + WIN], gusum[:, P * j:P * j + P], con("fold"), start=True, stop=True)
                        mm.then_inc(s_fold, 1)
                        if last:
                            down_of(W, e - 1, 1 - e2)

                if W == SEQ:
                    pe.wait_ge(s_pickT, 2)
                step_of(0, 0)
                with pe.Fori(0, NE // 2 - 1) as r:
                    for u in range(2):
                        step_of(2 * r + 1 + u, 1 - u)
                step_of(NE - 1, 1)
                down_of(W, NE - 1, 1)

            by_count(pe, lambda: moe(WIN), lambda: moe(SEQ))
            pe.wait_ge(s_yg, NE)
            for j in range(PAIRS // P):
                dst = PM if j < 2 else PG
                for k in range(KD):
                    mm = pe.transpose(dst[:, 2 * (j % 2) + k // 4, P * (k % 4):P * (k % 4) + P], pair[:, k, P * j:P * j + P], con("ident"))
                mm.then_inc(s_ygT, 1)
            for j in range(PAIRS // P):
                pe.wait_ge(s_yglo, max(j + 1, 2))
                for t in range(TT):
                    for b in range(2):
                        for y in (yg_hi, yg_lo):
                            mm = pe.matmul(PM[:, 2 * t + b, :], pickT[:, j, P * t:P * t + P], y[:, j, 512 * b:512 * b + 512],
                                           start=j == 0 and y is yg_hi, stop=j == PAIRS // P - 1 and y is yg_lo)
                    if j == PAIRS // P - 1:
                        mm.then_inc(s_sum, 1)


INPUTS = ["x", "norm_mix", "norm_ffn", "norm_final", "ffn_w_up", "ffn_conv_w", "ffn_conv_b", "ffn_w_down", "moba_w_qkv",
          "moba_w_o", "meta_tokens_2", "ln_emb_g_2", "ln_emb_b_2", "w_in_2", "b_gate_2", "dn_conv_w_2", "dn_a_log_2",
          "dn_dt_bias_2", "dn_norm_g_2", "w_branch_dn_2", "w_branch_sb_2", "w_out_2", "ln1_g_2", "ln1_b_2",
          "router_group_w_2", "router_group_b_2", "router_expert_w_2", "router_expert_b_2", "expert_w_gate_2",
          "expert_w_up_2", "expert_w_down_2", "ln2_g_2", "ln2_b_2"]


def kernel(**inputs):
    import concourse.bacc as bacc
    from concourse.bass_utils import run_bass_kernel_spmd

    nc = bacc.Bacc("TRN2", target_bir_lowering=False, num_devices=1)
    arrays = {f"in_{name}": np.ascontiguousarray(inputs[name]) for name in INPUTS}
    arrays["in_consts"] = constants()
    aps = {}
    for name, value in arrays.items():
        aps[name[3:]] = nc.dram_tensor(name, value.shape, mybir.dt.from_np(value.dtype), kind="ExternalInput").ap()
    out = nc.dram_tensor("out", (SEQ, D), F32, kind="ExternalOutput").ap()
    build(nc, aps, out)
    got = run_bass_kernel_spmd(nc, [arrays], core_ids=[0])
    return got.results[0]["out"].reshape(1, SEQ, D)
```
